# Optimizing a Trainium2 kernel written in Bass

```python
import jax, jax.numpy as jnp
from jax import lax
import numpy as np

D_MODEL = 1024
BATCH = 1
SEQ = 2048
DEPTH = 1
DEC_BATCH = 1
DEC_SEQ = 64
PAST_LEN = 4096

CHUNK = 64
D_MIX = D_MODEL
ATTN_HEADS = 8
ATTN_KV_HEADS = 2
HEAD_DIM = 64
ATTN_GROUP = ATTN_HEADS // ATTN_KV_HEADS
ATTN_DIM = ATTN_HEADS * HEAD_DIM
KV_DIM = ATTN_KV_HEADS * HEAD_DIM
WINDOW = 128
GLA_HEADS = 4
GLA_DK = 32
GLA_DV = 64
GLA_KDIM = GLA_HEADS * GLA_DK
GLA_VDIM = GLA_HEADS * GLA_DV
GLA_LOWRANK = 16
GLA_TAU = 16.0
CONV_DIM = D_MIX - ATTN_DIM - GLA_VDIM
CONV_WIDTH = 31
NORM_EPS = 1e-6
NEG_INF = -1e30
IN_SPLITS = (ATTN_DIM, KV_DIM, KV_DIM, ATTN_DIM,
             GLA_KDIM, GLA_KDIM, GLA_VDIM, GLA_VDIM, GLA_LOWRANK,
             CONV_DIM, CONV_DIM, CONV_DIM)
IN_COLS = 2832

kernel_name = 'hybrid_streaming_encoder_step'

def rmsnorm(x, g):
    xf = x.astype(jnp.float32)
    xf = xf * lax.rsqrt(jnp.mean(xf * xf, axis=-1, keepdims=True) + NORM_EPS)
    return (xf * g.astype(jnp.float32)).astype(x.dtype)

def layernorm(x, g, b):
    xf = x.astype(jnp.float32)
    mu = jnp.mean(xf, axis=-1, keepdims=True)
    var = jnp.mean(jnp.square(xf - mu), axis=-1, keepdims=True)
    y = (xf - mu) * lax.rsqrt(var + NORM_EPS) * g.astype(jnp.float32) + b.astype(jnp.float32)
    return y.astype(x.dtype)

def alibi_slopes():
    h = jnp.arange(1, ATTN_HEADS + 1, dtype=jnp.float32)
    return jnp.exp2(-8.0 * h / ATTN_HEADS)

def band_attention(q, k_all, v_all, sinks, q_pos0):
    B, L = q.shape[0], q.shape[1]
    C = min(CHUNK, L)
    N = L // C
    band = WINDOW + C
    idx = (jnp.arange(N) * C)[:, None] + jnp.arange(band)[None, :]
    kb = k_all[:, idx].astype(jnp.float32)
    vb = v_all[:, idx].astype(jnp.float32)
    qb = q.astype(jnp.float32).reshape(B, N, C, ATTN_KV_HEADS, ATTN_GROUP, HEAD_DIM)
    q_pos = q_pos0 + jnp.arange(L).reshape(N, C)
    k_pos = q_pos0 - WINDOW + idx
    valid = k_pos >= 0
    s = jnp.einsum('bnqhgd,bnkhd->bnhgqk', qb, kb) * (HEAD_DIM ** -0.5)
    dist = jnp.abs(q_pos[:, :, None] - k_pos[:, None, :]).astype(jnp.float32)
    slopes = alibi_slopes().reshape(ATTN_KV_HEADS, ATTN_GROUP)
    s = s - slopes[None, None, :, :, None, None] * dist[None, :, None, None, :, :]
    s = jnp.where(valid[None, :, None, None, None, :], s, NEG_INF)
    sink = sinks.astype(jnp.float32).reshape(ATTN_KV_HEADS, ATTN_GROUP)[None, None, :, :, None, None]
    m = jnp.maximum(jnp.max(s, axis=-1, keepdims=True), sink)
    p = jnp.exp(s - m)
    w = p / (jnp.sum(p, axis=-1, keepdims=True) + jnp.exp(sink - m))
    o = jnp.einsum('bnhgqk,bnkhd->bnqhgd', w, vb)
    return o.reshape(B, L, ATTN_DIM).astype(q.dtype)

def gla_chunked(q, k, v, log_a, s0):
    B, L, H, _ = q.shape
    DV = v.shape[-1]
    C = min(CHUNK, L)
    N = L // C

    def to_blocks(t):
        return t.astype(jnp.float32).reshape(B, N, C, H, t.shape[-1]).swapaxes(0, 1)

    causal = jnp.tril(jnp.ones((C, C), dtype=bool))

    def step(S, inp):
        qc, kc, vc, gc = inp
        b = jnp.cumsum(gc, axis=1)
        b_last = b[:, -1:]
        q_t = qc * jnp.exp(b)
        k_t = kc * jnp.exp(-b)
        A = jnp.where(causal, jnp.einsum('bthd,bshd->bhts', q_t, k_t), 0.0)
        o = jnp.einsum('bhts,bshv->bthv', A, vc) + jnp.einsum('bthd,bhdv->bthv', q_t, S)
        k_end = kc * jnp.exp(b_last - b)
        S = jnp.exp(b_last[:, 0])[..., None] * S + jnp.einsum('bshd,bshv->bhdv', k_end, vc)
        return S, o

    S, o = lax.scan(step, s0.astype(jnp.float32), (to_blocks(q), to_blocks(k), to_blocks(v), to_blocks(log_a)))
    o = o.swapaxes(0, 1).reshape(B, L, H, DV)
    return o.astype(v.dtype), S

def mixer_layer(x, q_pos0, k_hist, v_hist, gla_s0, conv_hist,
                norm_g, w_in, q_g, k_g, sinks, gla_w_up, gla_b, gla_g,
                conv_w, conv_b, ln_g, ln_b, w_pw, b_pw, w_out):
    B, L, _ = x.shape
    h = rmsnorm(x, norm_g)
    proj = h @ w_in
    offsets = [int(o) for o in np.cumsum(IN_SPLITS)[:-1]]
    aq, ak, av, ag, gq, gk, gv, gg, glr, cv, cgl, cg = jnp.split(proj, offsets, axis=-1)

    q = rmsnorm(aq.reshape(B, L, ATTN_HEADS, HEAD_DIM), q_g)
    k = rmsnorm(ak.reshape(B, L, ATTN_KV_HEADS, HEAD_DIM), k_g)
    v = av.reshape(B, L, ATTN_KV_HEADS, HEAD_DIM)
    k_all = jnp.concatenate([k_hist.astype(k.dtype), k], axis=1)
    v_all = jnp.concatenate([v_hist.astype(v.dtype), v], axis=1)
    y_attn = band_attention(q, k_all, v_all, sinks, q_pos0) * jax.nn.silu(ag)
    new_k = k_all[:, -WINDOW:]
    new_v = v_all[:, -WINDOW:]

    log_a = jax.nn.log_sigmoid((glr @ gla_w_up + gla_b).astype(jnp.float32)) / GLA_TAU
    o, s_fin = gla_chunked(gq.reshape(B, L, GLA_HEADS, GLA_DK) * (GLA_DK ** -0.5),
                           gk.reshape(B, L, GLA_HEADS, GLA_DK),
                           gv.reshape(B, L, GLA_HEADS, GLA_DV),
                           log_a.reshape(B, L, GLA_HEADS, GLA_DK), gla_s0)
    y_gla = rmsnorm(o, gla_g).reshape(B, L, GLA_VDIM) * jax.nn.silu(gg)

    u = cv * jax.nn.sigmoid(cgl)
    u_all = jnp.concatenate([conv_hist.astype(u.dtype), u], axis=1)
    c = lax.conv_general_dilated(u_all, conv_w[:, None, :].astype(u_all.dtype), window_strides=(1,),
                                 padding='VALID', dimension_numbers=('NWC', 'WIO', 'NWC'),
                                 feature_group_count=CONV_DIM) + conv_b
    c = jax.nn.silu(layernorm(c, ln_g, ln_b)) @ w_pw + b_pw
    y_conv = c * jax.nn.silu(cg)
    new_conv = u_all[:, -(CONV_WIDTH - 1):]

    y = jnp.concatenate([y_attn, y_gla.astype(y_attn.dtype), y_conv.astype(y_attn.dtype)], axis=-1) @ w_out
    return x + y.astype(x.dtype), new_k, new_v, s_fin, new_conv

def setup_inputs(seed: int = 0) -> dict:
    key = jax.random.key(seed)
    ks = jax.random.split(key, 24)
    f32 = jnp.float32
    nrm = lambda k, shape, scale: jax.random.normal(k, shape, f32) * scale
    win_rows = min(WINDOW, PAST_LEN)
    return {
        'x_prompt': nrm(ks[0], (BATCH, SEQ, D_MODEL), 1.0),
        'x_sample': nrm(ks[1], (DEC_BATCH, DEC_SEQ, D_MODEL), 1.0),
        'cache_k': nrm(ks[2], (DEPTH, DEC_BATCH, win_rows, ATTN_KV_HEADS, HEAD_DIM), 1.0),
        'cache_v': nrm(ks[3], (DEPTH, DEC_BATCH, win_rows, ATTN_KV_HEADS, HEAD_DIM), 0.5),
        'state_gla': nrm(ks[4], (DEPTH, DEC_BATCH, GLA_HEADS, GLA_DK, GLA_DV), 0.5),
        'state_conv': nrm(ks[5], (DEPTH, DEC_BATCH, CONV_WIDTH - 1, CONV_DIM), 0.5),
        'norm_gain': 1.0 + nrm(ks[6], (DEPTH, D_MODEL), 0.05),
        'w_in': nrm(ks[7], (DEPTH, D_MODEL, IN_COLS), D_MODEL ** -0.5),
        'q_norm_gain': 1.0 + nrm(ks[8], (DEPTH, HEAD_DIM), 0.05),
        'k_norm_gain': 1.0 + nrm(ks[9], (DEPTH, HEAD_DIM), 0.05),
        'attn_sinks': nrm(ks[10], (DEPTH, ATTN_HEADS), 0.5),
        'gla_w_gate_up': nrm(ks[11], (DEPTH, GLA_LOWRANK, GLA_KDIM), GLA_LOWRANK ** -0.5),
        'gla_b_gate': nrm(ks[12], (DEPTH, GLA_KDIM), 0.1),
        'gla_norm_gain': 1.0 + nrm(ks[13], (DEPTH, GLA_DV), 0.05),
        'conv_w': nrm(ks[14], (DEPTH, CONV_WIDTH, CONV_DIM), CONV_WIDTH ** -0.5),
        'conv_b': nrm(ks[15], (DEPTH, CONV_DIM), 0.02),
        'conv_ln_gain': 1.0 + nrm(ks[16], (DEPTH, CONV_DIM), 0.05),
        'conv_ln_bias': nrm(ks[17], (DEPTH, CONV_DIM), 0.02),
        'conv_w_pw': nrm(ks[18], (DEPTH, CONV_DIM, CONV_DIM), CONV_DIM ** -0.5),
        'conv_b_pw': nrm(ks[19], (DEPTH, CONV_DIM), 0.02),
        'w_out': nrm(ks[20], (DEPTH, D_MIX, D_MODEL), D_MIX ** -0.5),
    }

def reference(x_prompt, x_sample, cache_k, cache_v, state_gla, state_conv,
              norm_gain, w_in, q_norm_gain, k_norm_gain, attn_sinks,
              gla_w_gate_up, gla_b_gate, gla_norm_gain,
              conv_w, conv_b, conv_ln_gain, conv_ln_bias, conv_w_pw, conv_b_pw, w_out):
    bp = x_prompt.shape[0]
    zk = jnp.zeros((bp, WINDOW, ATTN_KV_HEADS, HEAD_DIM), x_prompt.dtype)
    zs = jnp.zeros((bp, GLA_HEADS, GLA_DK, GLA_DV), jnp.float32)
    zc = jnp.zeros((bp, CONV_WIDTH - 1, CONV_DIM), x_prompt.dtype)
    yp, ys = x_prompt, x_sample
    pk, pv, ps, pc, sk, sv, ss, sc = [], [], [], [], [], [], [], []
    for l in range(DEPTH):
        params = (norm_gain[l], w_in[l], q_norm_gain[l], k_norm_gain[l], attn_sinks[l],
                  gla_w_gate_up[l], gla_b_gate[l], gla_norm_gain[l],
                  conv_w[l], conv_b[l], conv_ln_gain[l], conv_ln_bias[l], conv_w_pw[l], conv_b_pw[l], w_out[l])
        yp, a, b, c, d = mixer_layer(yp, 0, zk, zk, zs, zc, *params)
        pk.append(a); pv.append(b); ps.append(c); pc.append(d)
        ys, a, b, c, d = mixer_layer(ys, PAST_LEN, cache_k[l], cache_v[l], state_gla[l], state_conv[l], *params)
        sk.append(a); sv.append(b); ss.append(c); sc.append(d)
    return (yp, ys, jnp.stack(pk), jnp.stack(pv), jnp.stack(ps), jnp.stack(pc),
            jnp.stack(sk), jnp.stack(sv), jnp.stack(ss), jnp.stack(sc))


_drawn_inputs = setup_inputs


def setup_inputs(seed=0):
    import zlib

    import numpy as np

    out = dict(_drawn_inputs(seed))
    spreads = {}
    factors = {'q_norm_gain': 23.857,
     'attn_sinks': 57.84,
     'gla_norm_gain': 3.987,
     'conv_b': 8.0,
     'conv_ln_gain': 5.26,
     'conv_ln_bias': 28.061,
     'conv_b_pw': 8.0}
    for name, (base, spread) in spreads.items():
        noise = np.random.default_rng([zlib.crc32(name.encode()), seed]).standard_normal(out[name].shape)
        drawn = base * np.exp(spread * noise) if base else spread * noise
        out[name] = __import__('jax').numpy.asarray(drawn.astype(out[name].dtype))
    for name, factor in factors.items():
        out[name] = (out[name] * factor).astype(out[name].dtype)
    return out
```

```python
from contextlib import ExitStack

import numpy as np

import concourse.bass as bass
from concourse import mybir

ALU = mybir.AluOpType
ACT = mybir.ActivationFunctionType
AX = mybir.AxisListType
F32 = mybir.dt.float32
F32R = mybir.dt.float32r
BF16 = mybir.dt.bfloat16
U16 = mybir.dt.uint16
U32 = mybir.dt.uint32

P = 128
D = 1024
KT = D // P
SEQ = 2048
DEC = 64
CHUNK = 64
TILES = SEQ // P + 1
LAST = TILES - 1
HEADS, KVH, HD = 8, 2, 64
GROUP = HEADS // KVH
GH, GK, GV, LR = 4, 32, 64, 16
CW = 31
HIST = CW - 1
CD = 256
CJ = CD // P
EPS = 1e-6
NEG = -1e30
ATT = HEADS * HD

AQ, AKV, AG = (0, 512), (512, 256), (768, 512)
GQK, GVC, GGC, GLR = (1280, 256), (1536, 256), (1792, 256), (2048, 16)
CV, CGL, CG = (2064, 256), (2320, 256), (2576, 256)
CHUNKS_A = [[AQ], [AKV], [AG]]
CHUNKS_B = [[GLR, GQK], [GVC, GGC], [CV, CGL], [CG]]
WIDTH_A = [sum(w for _, w in c) for c in CHUNKS_A]
WIDTH_B = [sum(w for _, w in c) for c in CHUNKS_B]
B_GLR, B_Q, B_K, B_V, B_GG, B_CV, B_CGL, B_CG = 0, 16, 144, 272, 528, 784, 1040, 1296
B_COLS = sum(WIDTH_B)
STAGES = 4

INS = ["x_prompt", "x_sample", "cache_k", "cache_v", "state_gla", "state_conv", "norm_gain", "w_in",
       "q_norm_gain", "k_norm_gain", "attn_sinks", "gla_w_gate_up", "gla_b_gate", "gla_norm_gain",
       "conv_w", "conv_b", "conv_ln_gain", "conv_ln_bias", "conv_w_pw", "conv_b_pw", "w_out"]
OUTS = [(1, SEQ, D), (1, DEC, D), (1, 1, P, KVH, HD), (1, 1, P, KVH, HD), (1, 1, GH, GK, GV), (1, 1, HIST, CD),
        (1, 1, P, KVH, HD), (1, 1, P, KVH, HD), (1, 1, GH, GK, GV), (1, 1, HIST, CD)]


class Tile:

    def __init__(self, i, c):
        self.i, self.c = i, c
        self.par = c % 2
        self.n = 2 * i + c
        self.half = i + c // 2
        self.fixed = isinstance(self.n, int)

    def __add__(self, k):
        return Tile(self.i, self.c + k)

    def real(self):
        return not self.fixed or 0 <= self.n < TILES


def need(eng, sem, count):
    if isinstance(count, int) and count <= 0:
        return
    eng.wait_ge(sem, count)


def pieces_of(chunks):
    out, base = [], 0
    for n, chunk in enumerate(chunks):
        width = sum(w for _, w in chunk)
        for k in range(KT):
            col = (k * width,) if n == 3 else base + k * width
            out.append(("in", k, chunk, col, width))
        base += KT * width
    for k in range(4):
        for h in range(2):
            out.append(("out", k, h, W_OUT + k * D + h * 512, 512))
    return out


W_OUT = KT * sum(WIDTH_B[:3])
W_COLS = W_OUT + 4 * D


def build(nc, ins, consts, outs):
    io = dict(zip(INS, ins))
    bias_d, ident_d, tri_d, mask_d = consts
    yp, ys, pk_o, pv_o, ps_o, pc_o, sk_o, sv_o, ss_o, sc_o = outs
    es = ExitStack()

    def sb(name, shape, dt=F32, ctx=es):
        return ctx.enter_context(nc.sbuf_tensor(name, shape, dt))

    def sem(name):
        return es.enter_context(nc.semaphore(name))

    with es:
        whi = sb("whi", [P, W_COLS], F32R)
        wlo = sb("wlo", [P, W_COLS], F32R)
        wraw = sb("wraw", [P, STAGES, 512])
        ident = sb("ident", [P, P])
        gain = sb("gain", [P, KT])
        mhalf = sb("mhalf", [P, 16])
        eps_d = sb("eps_d", [P, 1])
        eps_h = sb("eps_h", [P, 16])
        eps_1 = sb("eps_1", [P, 1])
        xin = [sb(f"xin{i}", [P, D]) for i in range(2)]
        xn = sb("xn", [P, D])
        xhi = sb("xhi", [P, KT, P], F32R)
        xlo = sb("xlo", [P, KT, P], F32R)
        res = [sb(f"res{i}", [P, D]) for i in range(2)]
        yhi = sb("yhi", [P, 4, P], F32R)
        ylo = sb("ylo", [P, 4, P], F32R)
        ssum = sb("ssum", [P, 1])
        msum = sb("msum", [P, 1])
        rinv = sb("rinv", [P, 1])
        ea = ExitStack()
        bias = sb("bias", [P, HEADS, 384], BF16, ea)
        qkgain = sb("qkgain", [P, 2, HD], F32, ea)
        sinks = sb("sinks", [P, HEADS], F32, ea)
        raw = sb("raw", [P, 768], F32, ea)
        qkn = sb("qkn", [P, 640], F32, ea)
        agraw = sb("agraw", [P, 512], F32, ea)
        gth = sb("gth", [P, 512], F32, ea)
        qss = sb("qss", [P, 10], F32, ea)
        qms = sb("qms", [P, 10], F32, ea)
        qr = sb("qr", [P, 10], F32, ea)
        qcat = sb("qcat", [P, HEADS, P], F32R, ea)
        kcat = sb("kcat", [P, KVH, 2, P], F32R, ea)
        vcat = [sb(f"vcat{i}", [P, KVH, P], F32R, ea) for i in range(2)]
        qT = sb("qT", [P, HEADS, P], F32R, ea)
        kT = sb("kT", [P, KVH, 2, 2 * P], F32R, ea)
        sc = sb("sc", [P, HEADS, 2 * P], F32, ea)
        mx = sb("mx", [P, HEADS], F32, ea)
        nmx = sb("nmx", [P, HEADS], F32, ea)
        esum = sb("esum", [P, HEADS], F32, ea)
        sdif = sb("sdif", [P, HEADS], F32, ea)
        esink = sb("esink", [P, HEADS], F32, ea)
        den = sb("den", [P, HEADS], F32, ea)
        rden = sb("rden", [P, HEADS], F32, ea)
        pthi = sb("pthi", [P, 2, 512], F32R, ea)
        ptlo = sb("ptlo", [P, 2, 512], F32R, ea)
        olo = sb("olo", [HD, 512], F32, ea)
        osum = sb("osum", [P, 4, P], F32, ea)
        ckv = sb("ckv", [P, 2, P], F32, ea)
        ckcat = sb("ckcat", [P, KVH, 2, P], F32R, ea)
        ea.close()
        w2hi = sb("w2hi", [P, KT * WIDTH_B[3]], F32R)
        w2lo = sb("w2lo", [P, KT * WIDTH_B[3]], F32R)
        tri = sb("tri", [P, 4, P])
        mask = sb("mask", [P, 512], U32)
        wup = sb("wup", [LR + 1, P])
        glagain = sb("glagain", [P, GV])
        bpw = sb("bpw", [P, CD])
        wpw = sb("wpw", [P, CJ, CD])
        convw = sb("convw", [P, CJ, CW])
        convp = sb("convp", [P, 3, CJ])
        braw = [sb(f"braw{i}", [P, B_COLS]) for i in range(2)]
        glr1 = sb("glr1", [P, LR + 1])
        glrT = sb("glrT", [LR + 1, P])
        az = sb("az", [P, P])
        zm = sb("zm", [P, P])
        ez = sb("ez", [P, P])
        ex = sb("ex", [P, 4, P])
        enb = sb("enb", [P, P])
        qt = sb("qt", [P, P])
        qf = sb("qf", [P, P])
        kk = sb("kk", [P, P])
        kt0 = sb("kt0", [64, P])
        kend = sb("kend", [P, P])
        qbd = sb("qbd", [P, GH, P])
        gT = sb("gT", [P, 320])
        dec = sb("dec", [P, 1])
        asb = sb("asb", [P, 512])
        stp = sb("stp", [P, 256])
        sts = sb("sts", [P, 256])
        osq = sb("osq", [P, 256])
        oss = sb("oss", [P, GH])
        oms = sb("oms", [P, GH])
        orr = sb("orr", [P, GH])
        thg = sb("thg", [P, 256])
        thc = sb("thc", [P, 512])
        gc = sb("gc", [P, CD])
        u = sb("u", [P, CD])
        ub = [sb(f"ub{i}", [P, CJ, HIST + P]) for i in range(2)]
        acc = sb("acc", [P, CJ, P])
        bst = sb("bst", [P, 6])
        mv = sb("mv", [P, 2])
        mve = sb("mve", [P, 1])
        rs = sb("rs", [P, 1])
        cn = sb("cn", [P, CD])
        cl = sb("cl", [P, CJ, P])
        cth = sb("cth", [P, CJ, P])
        yb = sb("yb", [P, 512])
        uh = sb("uh", [P, CJ, HIST])

        T = [es.enter_context(nc.psum_tensor(f"T{i}", [P, 512], F32)) for i in range(3)]
        J = [es.enter_context(nc.psum_tensor(f"J{i}", [P, 512], F32)) for i in range(3)]
        S = [es.enter_context(nc.psum_tensor(f"S{i}", [P, 512], F32)) for i in range(2)]

        f = lambda t: t.bitcast(F32)

        def weights(col, width):
            if isinstance(col, tuple):
                return w2hi[:, col[0]:col[0] + width], w2lo[:, col[0]:col[0] + width]
            return whi[:, col:col + width], wlo[:, col:col + width]

        class Pass:

            def __init__(self, tag, chunks):
                self.tag, self.pieces = tag, pieces_of(chunks)
                self.widths = [sum(w for _, w in c) for c in chunks]
                self.raw = [sem(f"weights_loaded_{tag}{i}") for i in range(STAGES)]
                self.whi = sem(f"weights_hi_{tag}")
                self.wlo = sem(f"weights_lo_{tag}")
                self.x_loaded = [sem(f"x_loaded_{tag}{i}") for i in range(2)]
                self.x_squared = sem(f"x_squared_{tag}")
                self.x_mean = sem(f"x_mean_{tag}")
                self.x_rinv = sem(f"x_rinv_{tag}")
                self.xn_ready = sem(f"xn_ready_{tag}")
                self.xT_psum = sem(f"xT_psum_{tag}")
                self.xT_hi = sem(f"xT_hi_{tag}")
                self.xT_lo = sem(f"xT_lo_{tag}")
                self.projected = [sem(f"projected_{tag}{i}") for i in range(len(chunks))]
                self.taken = [sem(f"projection_taken_{tag}{i}") for i in range(len(chunks))]
                self.res_loaded = [sem(f"res_loaded_{tag}{i}") for i in range(2)]
                self.y_hi = sem(f"y_hi_{tag}")
                self.y_lo = sem(f"y_lo_{tag}")
                self.out_psum = sem(f"out_psum_{tag}")
                self.out_added = sem(f"out_added_{tag}")
                self.out_stored = [sem(f"out_stored_{tag}{i}") for i in range(2)]

        A, B = Pass("a", CHUNKS_A), Pass("b", CHUNKS_B)
        consts_a, consts_b, zeros_a, zeros_b = sem("consts_a"), sem("consts_b"), sem("zeros_a"), sem("zeros_b")
        zeros_b1, pool_consts = sem("zeros_b1"), sem("pool_consts")
        v_hi, v_lo = sem("v_hi"), sem("v_lo")
        qkT_psum, qkT_taken = sem("qkT_psum"), sem("qkT_taken")
        gate_psum, gate_tanh, gate_ready = sem("gate_psum"), sem("gate_tanh"), sem("gate_ready")
        s_psum, s_max, s_neg, s_exp = sem("scores_psum"), sem("scores_max"), sem("scores_neg"), sem("scores_exp")
        s_diff, s_esink, s_den, s_rden, p_ready = (sem("sink_diff"), sem("sink_exp"), sem("softmax_den"),
                                                  sem("softmax_rden"), sem("p_ready"))
        n_step, n_mean, n_rinv, n_hi, n_lo = (sem("qk_norm_step"), sem("qk_mean"), sem("qk_rinv"), sem("qk_hi"),
                                              sem("qk_lo"))
        pt_psum, pt_hi, pt_lo = sem("pT_psum"), sem("pT_hi"), sem("pT_lo")
        o_psum, o_low, o_sum, y_gated = sem("o_psum"), sem("o_low"), sem("o_sum"), sem("y_gated")
        windows_stored = sem("windows_stored")
        c_hi, c_lo, c_psum, c_taken = sem("cache_hi"), sem("cache_lo"), sem("cache_psum"), sem("cache_taken")
        pass_a_done = sem("pass_a_done")

        states_stored, u_stored, dec_ready = sem("states_stored"), sem("u_stored"), sem("dec_ready")
        lr_taken, lr_psum, lr_T = sem("lowrank_taken"), sem("lowrank_psum"), sem("lowrank_T")
        z_psum, z_parts, z_exp, z_ln, la_ready = (sem("gate_logit_psum"), sem("gate_logit_parts"),
                                                 sem("gate_logit_exp"), sem("gate_logit_ln"), sem("log_decay_ready"))
        cum_psum, cum_exp, qk_scaled = sem("decay_sums_psum"), sem("decay_exp"), sem("gla_qk_scaled")
        g_psum, g_T, g_dec = sem("gla_T_psum"), sem("gla_T_taken"), sem("gla_decay")
        a_psum, a_masked, su_psum, go_psum = (sem("gla_scores_psum"), sem("gla_scores_masked"),
                                              sem("gla_state_psum"), sem("gla_o_psum"))
        g_state = sem("gla_state_ready")
        go_sq, go_ss, go_ms, go_r, go_n, go_g = (sem("gla_o_squared"), sem("gla_o_sums"), sem("gla_o_mean"),
                                                sem("gla_o_rinv"), sem("gla_o_normed"), sem("gla_y_ready"))
        th_ready, gates_ready, sg_ready, u_ready = (sem("tanh_ready"), sem("gates_ready"), sem("glu_gate_ready"),
                                                   sem("u_ready"))
        uT_psum, hist_ready, uT_taken, conv_step = (sem("uT_psum"), sem("hist_ready"), sem("uT_taken"),
                                                   sem("conv_step"))
        cT_psum, bn_step, ln_mean, ln_r, cn_ready = (sem("cT_psum"), sem("ln_step"), sem("ln_mean"), sem("ln_rinv"),
                                                    sem("conv_normed"))
        cnT_psum, cl_ready, cth_ready, cs_ready = (sem("cnT_psum"), sem("ln_affine_ready"), sem("conv_tanh"),
                                                  sem("conv_silu"))
        pw_psum, c2_ready, yc_ready, yT_psum = sem("pw_psum"), sem("pw_taken"), sem("conv_y_ready"), sem("yT_psum")

        N_CONSTS_A, N_CONSTS_B = 16 * 8, 16 * (14 + GH)

        def load_weights(eng, ps, first, last):
            for n, (part, k, what, col, width) in list(enumerate(ps.pieces))[first:last]:
                if n >= STAGES:
                    need(eng, ps.wlo, n - STAGES + 1)
                rows = slice(k * P, (k + 1) * P)
                dst = wraw[:, n % STAGES, :]
                if part == "in":
                    at = 0
                    for first, w in what:
                        eng.dma_start(dst[:, at:at + w], io["w_in"][0, rows, first:first + w]).then_inc(
                            ps.raw[n % STAGES], 16)
                        at += w
                else:
                    r0 = (0 if ps is A else 512) + k * P
                    eng.dma_start(dst, io["w_out"][0, r0:r0 + P, what * 512:(what + 1) * 512]).then_inc(
                        ps.raw[n % STAGES], 16)

        def raw_counts(ps):
            count, out = [0] * STAGES, []
            for n, (part, k, what, col, width) in enumerate(ps.pieces):
                count[n % STAGES] += 16 * (len(what) if part == "in" else 1)
                out.append(count[n % STAGES])
            return out

        def split_hi(ps):
            for n, (part, k, what, col, width) in enumerate(ps.pieces):
                nc.scalar.wait_ge(ps.raw[n % STAGES], raw_counts(ps)[n])
                if ps is B and n == 0:
                    nc.scalar.wait_ge(A.projected[2], TILES)
                if ps is B and part == "out" and k == 0 and what == 0:
                    nc.scalar.wait_ge(A.out_psum, 2 * TILES)
                scale = gain[:, k:k + 1] if part == "in" else 1.0
                nc.scalar.activation(weights(col, width)[0], wraw[:, n % STAGES, 0:width], ACT.Copy,
                                     scale=scale).then_inc(ps.whi, 1)

        def split_lo(ps):
            for n, (part, k, what, col, width) in enumerate(ps.pieces):
                nc.vector.wait_ge(ps.whi, n + 1)
                src = wraw[:, n % STAGES, 0:width]
                hi, lo = weights(col, width)
                if part == "in":
                    nc.vector.scalar_tensor_tensor(lo, src, gain[:, k:k + 1], f(hi), ALU.mult,
                                                   ALU.subtract).then_inc(ps.wlo, 1)
                else:
                    nc.vector.tensor_tensor(lo, src, f(hi), ALU.subtract).then_inc(ps.wlo, 1)

        def x_rows(src_p, src_s, t, cols=slice(0, D)):
            if t.fixed and t.n == LAST:
                return src_s[0, 0:DEC, cols], DEC
            return src_p[0, bass.ds(t.n * P, P), cols], P

        def load_x(ps, t):
            need(nc.sync, ps.xn_ready, t.n - 1)
            src, rows = x_rows(io["x_prompt"], io["x_sample"], t)
            nc.sync.dma_start(xin[t.par][0:rows, :], src).then_inc(ps.x_loaded[t.par], 16)

        def load_res(ps, t):
            need(nc.sync, ps.out_stored[t.par], 32 * t.half)
            if ps is A:
                src, rows = x_rows(io["x_prompt"], io["x_sample"], t)
            else:
                src, rows = x_rows(yp, ys, t)
            nc.sync.dma_start(res[t.par][0:rows, :], src).then_inc(ps.res_loaded[t.par], 16)

        def store_out(ps, t):
            for h in range(2):
                need(nc.sync, ps.out_added, 2 * t.n + h + 1)
                dst, rows = x_rows(yp, ys, t, slice(h * 512, (h + 1) * 512))
                nc.sync.dma_start(dst, res[t.par][0:rows, h * 512:(h + 1) * 512]).then_inc(
                    ps.out_stored[t.par], 16)

        def norm_square(ps, t):
            nc.scalar.wait_ge(ps.x_loaded[t.par], 16 * (t.half + 1))
            need(nc.scalar, ps.xT_psum, 2 * t.n)
            nc.scalar.activation(xn[:, :], xin[t.par][:, :], ACT.Square, accum_out=ssum[:, :]).then_inc(
                ps.x_squared, 1)

        def norm_rinv(ps, t):
            nc.gpsimd.wait_ge(ps.x_squared, t.n + 1)
            nc.gpsimd.tensor_tensor(msum[:, :], ssum[:, :], eps_d[:, :], ALU.add).then_inc(ps.x_mean, 1)
            nc.gpsimd.wait_ge(ps.x_mean, t.n + 1)
            nc.gpsimd.tensor_tensor(rinv[:, :], msum[:, :], mhalf[:, 0:1], ALU.pow).then_inc(ps.x_rinv, 1)

        def norm_scale(ps, t):
            nc.vector.wait_ge(ps.x_rinv, t.n + 1)
            nc.vector.tensor_scalar(xn[:, :], xin[t.par][:, :], rinv[:, :], D ** 0.5, ALU.mult,
                                    ALU.mult).then_inc(ps.xn_ready, 1)

        def transpose_x(ps, t, g):
            if g == 0:
                nc.tensor.wait_ge(ps.xn_ready, t.n + 1)
            for j in range(4):
                last = nc.tensor.transpose(T[g][:, j * P:(j + 1) * P], xn[:, (4 * g + j) * P:(4 * g + j + 1) * P],
                                           ident[:, :])
            last.then_inc(ps.xT_psum, 1)

        def split_x_hi(ps, t, g):
            nc.scalar.wait_ge(ps.xT_psum, 2 * t.n + g + 1)
            nc.scalar.activation(xhi[:, 4 * g:4 * g + 4, :], T[g][:, :].rearrange("p (j n) -> p j n", n=P),
                                 ACT.Copy).then_inc(ps.xT_hi, 1)

        def split_x_lo(ps, t, g):
            nc.vector.wait_ge(ps.xT_hi, 2 * t.n + g + 1)
            nc.vector.tensor_tensor(xlo[:, 4 * g:4 * g + 4, :], T[g][:, :].rearrange("p (j n) -> p j n", n=P),
                                    f(xhi[:, 4 * g:4 * g + 4, :]), ALU.subtract).then_inc(ps.xT_lo, 1)

        def project(ps, t, c, bank):
            width = ps.widths[c]
            base = KT * sum(ps.widths[:c])
            if c == 0:
                nc.tensor.wait_ge(ps.xT_lo, 2 * t.n + 2)
            if t.fixed and t.n == 0:
                nc.tensor.wait_ge(ps.wlo, KT * (c + 1))
            for k in range(KT):
                hi, lo = weights((k * width,) if c == 3 else base + k * width, width)
                for n, (x, w) in enumerate(((xhi, hi), (xhi, lo), (xlo, hi))):
                    last = nc.tensor.matmul(bank[:, 0:width], x[:, k, :], w, start=(k == 0 and n == 0),
                                            stop=(k == KT - 1 and n == 2))
            last.then_inc(ps.projected[c], 1)

        def output(ps, t, h, bank):
            if h == 0:
                nc.tensor.wait_ge(ps.y_lo, (t.n + 1) * (2 if ps is A else 1))
            if t.fixed and t.n == 0:
                nc.tensor.wait_ge(ps.wlo, len(ps.pieces))
            for k in range(4):
                col = W_OUT + k * D + h * 512
                hi, lo = weights(col, 512)
                for n, (y, w) in enumerate(((yhi, hi), (yhi, lo), (ylo, hi))):
                    last = nc.tensor.matmul(bank[:, :], y[:, k, :], w, start=(k == 0 and n == 0),
                                            stop=(k == 3 and n == 2))
            last.then_inc(ps.out_psum, 1)

        def add_out(ps, t, h, bank):
            if h == 0:
                nc.vector.wait_ge(ps.res_loaded[t.par], 16 * (t.half + 1))
            nc.vector.wait_ge(ps.out_psum, 2 * t.n + h + 1)
            dst = res[t.par][:, h * 512:(h + 1) * 512]
            nc.vector.tensor_tensor(dst, bank[:, :], dst, ALU.add).then_inc(ps.out_added, 1)

        def over_tiles(eng, body, first=3, last=14):
            for c in range(-2, first):
                body(Tile(0, c))
            with eng.Fori(0, (last - first + 1) // 2) as i:
                body(Tile(i, first))
                body(Tile(i, first + 1))
            for c in range(last + 1, TILES + 1):
                body(Tile(0, c))

        def when(t, *steps):
            for s in steps if t.real() else ():
                s(t)

        es.enter_context(nc.allow_non_contiguous_dma(reason="small vectors of parameters, once"))
        block = es.enter_context(nc.Block())

        @block.sync
        def _(sp):
            for dst, src in ((gain[:, :], io["norm_gain"][0].rearrange("(k p) -> p k", p=P)),
                             (ident[:, :], ident_d)):
                sp.dma_start(dst, src).then_inc(consts_a, 16)
            load_x(A, Tile(0, 0))
            load_x(A, Tile(0, 1))
            for dst, src in ((bias[:, :, :], bias_d.bitcast(BF16)),
                             (qkgain[:, 0, :], io["q_norm_gain"].partition_broadcast(P)),
                             (qkgain[:, 1, :], io["k_norm_gain"].partition_broadcast(P)),
                             (sinks[:, :], io["attn_sinks"].partition_broadcast(P)),
                             (ckv[:, 0, :], io["cache_k"][0, 0].rearrange("w h d -> w (h d)")),
                             (ckv[:, 1, :], io["cache_v"][0, 0].rearrange("w h d -> w (h d)"))):
                sp.dma_start(dst, src).then_inc(consts_a, 16)
            load_weights(sp, A, 0, len(A.pieces))
            for src, dst in ((io["cache_k"], sk_o), (io["cache_v"], sv_o)):
                sp.dma_start(dst[0, 0, 0:DEC], src[0, 0, DEC:P]).then_inc(windows_stored, 16)

            def body_a(t):
                if t.fixed and t.n == -2:
                    return
                if (t + 3).real():
                    load_x(A, t + 3)
                if t.real():
                    load_res(A, t)
                if t.fixed and t.n == LAST - 2:
                    load_weights(sp, B, 0, STAGES)
                if t.fixed and t.n + 1 in (LAST - 1, LAST):
                    rows = P if t.n + 1 == LAST - 1 else DEC
                    k_dst, v_dst = (pk_o, pv_o) if rows == P else (sk_o, sv_o)
                    sp.wait_ge(n_step, 5 * (t.n + 2))
                    sp.dma_start(k_dst[0, 0, P - rows:P].rearrange("w h d -> w (h d)"),
                                 qkn[0:rows, 512:640]).then_inc(windows_stored, 16)
                    sp.dma_start(v_dst[0, 0, P - rows:P].rearrange("w h d -> w (h d)"),
                                 raw[0:rows, 640:768]).then_inc(windows_stored, 16)
                if (t + -1).real():
                    store_out(A, t + -1)

            over_tiles(sp, body_a, 3, 12)
            load_weights(sp, B, STAGES, len(B.pieces))
            for i in range(2):
                sp.wait_ge(A.out_stored[i], 32 * ((TILES + 1 - i) // 2))
            sp.wait_ge(windows_stored, 16 * 6)
            sp.wait_ge(pass_a_done, 4)
            for i in range(2):
                load_x(B, Tile(0, i))
            for dst, src in ((tri[:, :, :], tri_d), (mask[:, :], mask_d.bitcast(U32)),
                             (wup[0:LR, :], io["gla_w_gate_up"][0]), (wup[LR:LR + 1, :], io["gla_b_gate"]),
                             (glagain[:, :], io["gla_norm_gain"].partition_broadcast(P)),
                             (bpw[:, :], io["conv_b_pw"].partition_broadcast(P)),
                             (wpw[:, :, :], io["conv_w_pw"][0].rearrange("(j p) n -> p j n", p=P)),
                             (convp[:, 0, :], io["conv_b"][0].rearrange("(j p) -> p j", p=P)),
                             (convp[:, 1, :], io["conv_ln_gain"][0].rearrange("(j p) -> p j", p=P)),
                             (convp[:, 2, :], io["conv_ln_bias"][0].rearrange("(j p) -> p j", p=P)),
                             (convw[:, 0, :], io["conv_w"][0, :, 0:P].rearrange("w p -> p w")),
                             (convw[:, 1, :], io["conv_w"][0, :, P:CD].rearrange("w p -> p w")),
                             (uh[:, 0, :], io["state_conv"][0, 0, :, 0:P].rearrange("w p -> p w")),
                             (uh[:, 1, :], io["state_conv"][0, 0, :, P:CD].rearrange("w p -> p w"))):
                sp.dma_start(dst, src).then_inc(consts_b, 16)
            sp.wait_ge(zeros_b1, 1)
            for h in range(GH):
                sp.dma_start(sts[h * GK:(h + 1) * GK, h * GV:(h + 1) * GV], io["state_gla"][0, 0, h]).then_inc(
                    consts_b, 16)

            def body_b(t):
                if t.fixed and t.n == -2:
                    return
                if (t + 3).real():
                    load_x(B, t + 3)
                if t.real():
                    load_res(B, t)
                if t.fixed and t.n in (LAST - 1, LAST):
                    end, dst = (P, pc_o) if t.n == LAST - 1 else (DEC, sc_o)
                    sp.wait_ge(u_ready, t.n + 1)
                    sp.dma_start(dst[0, 0], u[end - HIST:end, :]).then_inc(u_stored, 16)
                    st, dst = (stp, ps_o) if t.n == LAST - 1 else (sts, ss_o)
                    sp.wait_ge(g_state, t.n + 1)
                    for h in range(GH):
                        sp.dma_start(dst[0, 0, h], st[h * GK:(h + 1) * GK, h * GV:(h + 1) * GV]).then_inc(
                            states_stored, 16)
                if (t + -1).real():
                    store_out(B, t + -1)

            over_tiles(sp, body_b, 3, 12)
            for i in range(2):
                sp.wait_ge(B.out_stored[i], 32 * ((TILES + 1 - i) // 2))
            sp.wait_ge(states_stored, 16 * 8)
            sp.wait_ge(u_stored, 16 * 2)

        @block.gpsimd
        def _(pool):
            for buf, value in ((mhalf, -0.5), (eps_d, D * EPS), (eps_h, HD * EPS), (eps_1, EPS)):
                nc.gpsimd.memset(buf[:, :], value).then_inc(pool_consts, 1)
            pool.wait_ge(pool_consts, 4)
            norm_rinv(A, Tile(0, 0))

            def body_a(t):
                n = t + 1
                if n.real():
                    pool.wait_ge(n_step, 5 * n.n + 2)
                    nc.gpsimd.tensor_tensor(qms[:, :], qss[:, :], eps_h[:, 0:10], ALU.add).then_inc(
                        n_mean, 1)
                    pool.wait_ge(n_mean, n.n + 1)
                    nc.gpsimd.tensor_tensor(qr[:, :], qms[:, :], mhalf[:, 0:10], ALU.pow).then_inc(n_rinv, 1)
                if not (t.fixed and t.n == -2):
                    when(t + 2, lambda n: norm_rinv(A, n))

            over_tiles(pool, body_a)
            pool.sem_inc(pass_a_done, 1)
            pool.wait_ge(pass_a_done, 4)
            nc.gpsimd.memset(sts[:, :], 0.0).then_inc(zeros_b1, 1)
            for buf in (stp, asb):
                nc.gpsimd.memset(buf[:, :], 0.0).then_inc(zeros_b, 1)
            nc.gpsimd.memset(qbd[:, :, :], 0.0).then_inc(zeros_b, 1)
            nc.gpsimd.memset(glr1[:, LR:LR + 1], 1.0).then_inc(zeros_b, 1)

            def body_b(t):
                if t.real():
                    pool.wait_ge(go_ss, t.n + 1)
                    nc.gpsimd.tensor_tensor(oms[:, :], oss[:, :], eps_h[:, 0:GH], ALU.add).then_inc(
                        go_ms, 1)
                    pool.wait_ge(go_ms, t.n + 1)
                    nc.gpsimd.tensor_tensor(orr[:, :], oms[:, :], mhalf[:, 0:GH], ALU.pow).then_inc(go_r, 1)
                    pool.wait_ge(bn_step, 2 * t.n + 2)
                    nc.gpsimd.tensor_tensor(mve[:, :], mv[:, 1:2], eps_1[:, :], ALU.add).then_inc(ln_mean, 1)
                    pool.wait_ge(ln_mean, t.n + 1)
                    nc.gpsimd.tensor_tensor(rs[:, :], mve[:, :], mhalf[:, 0:1], ALU.pow).then_inc(ln_r, 1)
                when(t + 2, lambda n: norm_rinv(B, n))

            over_tiles(pool, body_b)

        @block.scalar
        def _(act):
            act.wait_ge(consts_a, N_CONSTS_A)
            norm_square(A, Tile(0, 0))
            split_hi(A)

            def body_a(t):
                t1 = t + 1
                if t.real():
                    need(act, o_psum, 2 * t.n)
                    act.wait_ge(A.taken[1], t.n + 1)
                    nc.scalar.activation(vcat[t.par][:, :, 0:HD], raw[:, 640:768].rearrange("p (h d) -> p h d", d=HD),
                                         ACT.Copy).then_inc(v_hi, 1)
                    if t.fixed and t.n == LAST:
                        cache_hi(act)
                if t1.real():
                    split_x_hi(A, t1, 0)
                    split_x_hi(A, t1, 1)
                if t.real():
                    for n in range(3):
                        act.wait_ge(qkT_psum, 3 * t.n + n + 1)
                        src = (T[2], T[0], T[1])[n][:, :].rearrange("p (a b) -> p a b", b=P)
                        if n < 2:
                            dst = qT[:, 4 * n:4 * n + 4, :]
                        else:
                            dst = kT[:, :, :, t.par * P:(t.par + 1) * P].rearrange("p h o n -> p (h o) n")
                        nc.scalar.activation(dst, src, ACT.Copy).then_inc(qkT_taken, 1)
                    act.wait_ge(gate_psum, t.n + 1)
                    need(act, gate_ready, t.n)
                    nc.scalar.activation(gth[:, :], T[2][:, :], ACT.Tanh, scale=0.5).then_inc(gate_tanh, 1)
                if t1.real():
                    act.wait_ge(A.projected[0], t1.n + 1)
                    need(act, n_step, 5 * t1.n)
                    nc.scalar.activation(raw[:, 0:512], J[0][:, :], ACT.Copy).then_inc(A.taken[0], 1)
                if t.real():
                    for n in range(4):
                        act.wait_ge(s_neg, 4 * t.n + n + 1)
                        for h in (2 * n, 2 * n + 1):
                            last = nc.scalar.activation(sc[:, h, :], sc[:, h, :], ACT.Exp, bias=nmx[:, h:h + 1],
                                                        accum_out=esum[:, h:h + 1])
                        last.then_inc(s_exp, 1)
                    act.wait_ge(s_diff, t.n + 1)
                    nc.scalar.activation(esink[:, :], sdif[:, :], ACT.Exp).then_inc(s_esink, 1)
                if t1.real():
                    act.wait_ge(A.projected[1], t1.n + 1)
                    need(act, v_lo, t1.n)
                    if t1.fixed and t1.n == LAST:
                        act.wait_ge(windows_stored, 16 * 4)
                    nc.scalar.activation(raw[:, 512:768], J[1][:, 0:256], ACT.Copy).then_inc(A.taken[1], 1)
                    act.wait_ge(A.projected[2], t1.n + 1)
                    nc.scalar.activation(agraw[:, :], J[2][:, :], ACT.Copy).then_inc(A.taken[2], 1)
                    act.wait_ge(n_step, 5 * t1.n + 5)
                    nc.scalar.activation(qcat[:, :, 0:HD], qkn[:, 0:512].rearrange("p (h d) -> p h d", d=HD),
                                         ACT.Copy).then_inc(n_hi, 1)
                    kn = qkn[:, 512:640].rearrange("p (h d) -> p h d", d=HD)
                    for o in range(2):
                        nc.scalar.activation(kcat[:, :, o, o * HD:(o + 1) * HD], kn, ACT.Copy).then_inc(n_hi, 1)
                if t.real():
                    def pT_hi(k):
                        act.wait_ge(pt_psum, 4 * t.n + k + 1)
                        nc.scalar.activation(pthi[:, k % 2, :], T[k % 3][:, :], ACT.Copy).then_inc(pt_hi, 1)

                    def o_low_half(g):
                        act.wait_ge(o_psum, 2 * t.n + g + 1)
                        need(act, o_sum, 4 * t.n + 2 * g)
                        nc.scalar.activation(olo[:, :], S[g][HD:P, :], ACT.Copy).then_inc(o_low, 1)

                    def y_hi_half(g):
                        act.wait_ge(y_gated, 2 * t.n + g + 1)
                        need(act, A.out_psum, 2 * t.n)
                        nc.scalar.activation(yhi[:, 2 * g:2 * g + 2, :], osum[:, 2 * g:2 * g + 2, :],
                                             ACT.Copy).then_inc(A.y_hi, 1)

                    pT_hi(0)
                    pT_hi(1)
                    o_low_half(0)
                    pT_hi(2)
                    pT_hi(3)
                    y_hi_half(0)
                    o_low_half(1)
                    y_hi_half(1)
                if not (t.fixed and t.n == -2):
                    when(t + 2, lambda n: norm_square(A, n))

            def cache_hi(act):
                for o in range(2):
                    nc.scalar.activation(ckcat[:, :, o, o * HD:(o + 1) * HD],
                                         ckv[:, 0, :].rearrange("p (h d) -> p h d", d=HD), ACT.Copy).then_inc(c_hi, 1)
                nc.scalar.activation(vcat[1][:, :, 0:HD], ckv[:, 1, :].rearrange("p (h d) -> p h d", d=HD),
                                     ACT.Copy).then_inc(c_hi, 1)
                act.wait_ge(c_psum, 1)
                nc.scalar.activation(kT[:, :, :, P:2 * P].rearrange("p h o n -> p (h o) n"),
                                     T[0][:, :].rearrange("p (a b) -> p a b", b=P), ACT.Copy).then_inc(c_taken, 1)

            over_tiles(act, body_a)
            act.sem_inc(pass_a_done, 1)

            split_hi(B)
            act.wait_ge(pass_a_done, 4)
            norm_square(B, Tile(0, 0))
            act.wait_ge(consts_b, N_CONSTS_B)
            act.wait_ge(zeros_b, 4)

            def body_b(t):
                t1 = t + 1
                r = braw[t.par]
                if t.real():
                    act.wait_ge(lr_psum, t.n + 1)
                    nc.scalar.activation(glrT[:, :], T[2][0:LR + 1, 0:P], ACT.Copy).then_inc(lr_T, 1)
                if t1.real():
                    split_x_hi(B, t1, 0)
                    split_x_hi(B, t1, 1)
                if t.real():
                    act.wait_ge(uT_psum, t.n + 1)
                    nc.scalar.activation(ub[t.par][:, :, HIST:], T[2][:, 0:CD].rearrange("p (j n) -> p j n", n=P),
                                         ACT.Copy).then_inc(uT_taken, 1)
                    act.wait_ge(z_parts, 2 * t.n + 2)
                    nc.scalar.activation(ez[:, :], az[:, :], ACT.Exp).then_inc(z_exp, 1)
                    act.wait_ge(z_exp, t.n + 1)
                    nc.scalar.activation(ez[:, :], ez[:, :], ACT.Ln, bias=1.0).then_inc(z_ln, 1)
                    need(act, go_g, t.n)
                    act.wait_ge(B.taken[3], t.n + 1)
                    act.wait_ge(B.taken[1], t.n + 1)
                    nc.scalar.activation(thg[:, :], r[:, B_GG:B_GG + 256], ACT.Tanh, scale=0.5).then_inc(th_ready, 1)
                    act.wait_ge(cum_psum, t.n + 1)
                    nc.scalar.activation(ex[:, :, :], S[1][:, :].rearrange("p (a n) -> p a n", n=P),
                                         ACT.Exp).then_inc(cum_exp, 1)
                    nc.scalar.activation(enb[:, :], S[1][:, 0:P], ACT.Exp, scale=-1.0).then_inc(cum_exp, 1)
                if t1.real():
                    act.wait_ge(B.projected[0], t1.n + 1)
                    nc.scalar.activation(glr1[:, 0:LR], J[0][:, 0:LR], ACT.Copy).then_inc(lr_taken, 1)
                    nc.scalar.activation(braw[t1.par][:, LR:272], J[0][:, LR:272], ACT.Copy).then_inc(B.taken[0], 1)
                if t.real():
                    act.wait_ge(g_psum, t.n + 1)
                    for h in range(GH):
                        rows = slice(h * GK, (h + 1) * GK)
                        nc.scalar.activation(qbd[rows, h, :], T[0][rows, 0:P], ACT.Copy)
                    nc.scalar.activation(gT[:, :], T[0][:, P:448], ACT.Copy).then_inc(g_T, 1)
                if t1.real():
                    act.wait_ge(B.projected[1], t1.n + 1)
                    nc.scalar.activation(braw[t1.par][:, 272:784], J[1][:, :], ACT.Copy).then_inc(B.taken[1], 1)
                    act.wait_ge(B.projected[2], t1.n + 1)
                    nc.scalar.activation(braw[t1.par][:, 784:1296], J[2][:, :], ACT.Copy).then_inc(B.taken[2], 1)
                    act.wait_ge(B.projected[3], t1.n + 1)
                    nc.scalar.activation(braw[t1.par][:, 1296:1552], J[0][:, 0:256], ACT.Copy).then_inc(B.taken[3], 1)
                if t.real():
                    act.wait_ge(go_psum, t.n + 1)
                    nc.scalar.activation(osq[:, :], T[2][:, 0:256], ACT.Square).then_inc(go_sq, 1)
                    act.wait_ge(cl_ready, 2 * t.n + 2)
                    nc.scalar.activation(cth[:, :, :], cl[:, :, :], ACT.Tanh, scale=0.5).then_inc(cth_ready, 1)
                if t1.real():
                    need(act, gates_ready, 2 * t1.n)
                    act.wait_ge(B.taken[3], t1.n + 1)
                    nc.scalar.activation(thc[:, :], braw[t1.par][:, B_CGL:B_CGL + 512], ACT.Tanh,
                                         scale=0.5).then_inc(th_ready, 1)
                if t.real():
                    act.wait_ge(yT_psum, t.n + 1)
                    nc.scalar.activation(yhi[:, :, :], T[1][:, :].rearrange("p (j n) -> p j n", n=P),
                                         ACT.Copy).then_inc(B.y_hi, 1)
                if not (t.fixed and t.n == -2):
                    when(t + 2, lambda n: norm_square(B, n))

            over_tiles(act, body_b)

        @block.vector
        def _(dve):
            for i in range(1):
                nc.vector.memset(f(vcat[1][:, :, :]), 0.0).then_inc(zeros_a, 1)
                nc.vector.memset(f(kT[:, :, :, P:2 * P]), 0.0).then_inc(zeros_a, 1)
                nc.vector.memset(sc[:, :, P:2 * P], NEG).then_inc(zeros_a, 1)
            dve.wait_ge(consts_a, N_CONSTS_A)
            norm_scale(A, Tile(0, 0))
            split_lo(A)

            def body_a(t):
                t1 = t + 1
                if t.real():
                    dve.wait_ge(v_hi, t.n + 1)
                    nc.vector.tensor_tensor(vcat[t.par][:, :, HD:P], raw[:, 640:768].rearrange("p (h d) -> p h d", d=HD),
                                            f(vcat[t.par][:, :, 0:HD]), ALU.subtract).then_inc(v_lo, 1)
                    if t.fixed and t.n == LAST:
                        dve.wait_ge(c_hi, 3)
                        for o in range(2):
                            nc.vector.tensor_tensor(ckcat[:, :, o, (1 - o) * HD:(2 - o) * HD],
                                                    ckv[:, 0, :].rearrange("p (h d) -> p h d", d=HD),
                                                    f(ckcat[:, :, o, o * HD:(o + 1) * HD]), ALU.subtract).then_inc(c_lo, 1)
                        nc.vector.tensor_tensor(vcat[1][:, :, HD:P], ckv[:, 1, :].rearrange("p (h d) -> p h d", d=HD),
                                                f(vcat[1][:, :, 0:HD]), ALU.subtract).then_inc(c_lo, 1)
                if t1.real():
                    split_x_lo(A, t1, 0)
                    split_x_lo(A, t1, 1)
                if t.real():
                    need(dve, pt_psum, 4 * t.n)
                    dve.wait_ge(s_psum, 4 * t.n + 1)
                    dve.wait_ge(gate_tanh, t.n + 1)
                    nc.vector.scalar_tensor_tensor(gth[:, :], gth[:, :], 1.0, T[2][:, :], ALU.add,
                                                   ALU.mult).then_inc(gate_ready, 1)
                    for n in range(4):
                        for e in range(2):
                            h = 2 * n + e
                            cols = slice(0, P) if t.fixed and t.n == 0 else slice(0, 2 * P)
                            b0 = 0 if t.par else P
                            nc.vector.tensor_tensor_reduce(
                                out=sc[:, h, cols], in0=S[n % 2][:, e * 256:(e + 1) * 256][:, cols],
                                in1=bias[:, h, b0:b0 + 256][:, cols], scale=1.0, scalar=sinks[:, h:h + 1],
                                op0=ALU.add, op1=ALU.max, accum_out=mx[:, h:h + 1]).then_inc(s_max, 1)
                        dve.wait_ge(s_max, 8 * t.n + 2 * n + 2)
                        if n < 3:
                            dve.wait_ge(s_psum, 4 * t.n + n + 2)
                        nc.vector.tensor_scalar(nmx[:, 2 * n:2 * n + 2], mx[:, 2 * n:2 * n + 2], -1.0, None,
                                                ALU.mult).then_inc(s_neg, 1)
                    dve.wait_ge(s_neg, 4 * t.n + 4)
                    nc.vector.tensor_tensor(sdif[:, :], sinks[:, :], nmx[:, :], ALU.add).then_inc(s_diff, 1)
                    dve.wait_ge(s_exp, 4 * t.n + 4)
                    dve.wait_ge(s_esink, t.n + 1)
                    nc.vector.tensor_tensor(den[:, :], esum[:, :], esink[:, :], ALU.add).then_inc(s_den, 1)
                    dve.wait_ge(s_den, t.n + 1)
                    nc.vector.reciprocal(rden[:, :], den[:, :]).then_inc(s_rden, 1)
                    dve.wait_ge(s_rden, t.n + 1)
                    for h in range(HEADS):
                        nc.vector.tensor_scalar(sc[:, h, :], sc[:, h, :], rden[:, h:h + 1], None,
                                                ALU.mult).then_inc(p_ready, 1)
                if t1.real():
                    dve.wait_ge(A.taken[1], t1.n + 1)
                    if t1.fixed and t1.n == LAST:
                        dve.wait_ge(windows_stored, 16 * 4)
                    nc.vector.tensor_tensor(qkn[:, :], raw[:, 0:640], raw[:, 0:640], ALU.mult).then_inc(n_step, 1)
                    dve.wait_ge(n_step, 5 * t1.n + 1)
                    nc.vector.tensor_reduce(qss[:, :], qkn[:, :].rearrange("p (h d) -> p h d", d=HD), AX.X,
                                            ALU.add).then_inc(n_step, 1)
                    dve.wait_ge(n_rinv, t1.n + 1)
                    heads = lambda b: b.rearrange("p (h d) -> p h d", d=HD)
                    nc.vector.tensor_tensor(heads(qkn[:, :]), heads(raw[:, 0:640]),
                                            qr[:, :].unsqueeze(2).to_broadcast([P, 10, HD]),
                                            ALU.mult).then_inc(n_step, 1)
                    dve.wait_ge(n_step, 5 * t1.n + 3)
                    nc.vector.scalar_tensor_tensor(heads(qkn[:, 0:512]), heads(qkn[:, 0:512]), 1.0,
                                                   qkgain[:, 0, :].unsqueeze(1).to_broadcast([P, HEADS, HD]),
                                                   ALU.mult, ALU.mult).then_inc(n_step, 1)
                    nc.vector.scalar_tensor_tensor(heads(qkn[:, 512:640]), heads(qkn[:, 512:640]), HD ** 0.5,
                                                   qkgain[:, 1, :].unsqueeze(1).to_broadcast([P, KVH, HD]),
                                                   ALU.mult, ALU.mult).then_inc(n_step, 1)
                    dve.wait_ge(n_hi, 3 * t1.n + 3)
                    nc.vector.tensor_tensor(qcat[:, :, HD:P], heads(qkn[:, 0:512]), f(qcat[:, :, 0:HD]),
                                            ALU.subtract).then_inc(n_lo, 1)
                    for o in range(2):
                        nc.vector.tensor_tensor(kcat[:, :, o, (1 - o) * HD:(2 - o) * HD], heads(qkn[:, 512:640]),
                                                f(kcat[:, :, o, o * HD:(o + 1) * HD]), ALU.subtract).then_inc(n_lo, 1)
                def pT_lo(k):
                    dve.wait_ge(pt_hi, 4 * t.n + k + 1)
                    nc.vector.tensor_tensor(ptlo[:, k % 2, :], T[k % 3][:, :], f(pthi[:, k % 2, :]),
                                            ALU.subtract).then_inc(pt_lo, 1)

                def y_half(g):
                    dve.wait_ge(o_low, 2 * t.n + g + 1)
                    for e in range(2):
                        pick = lambda b: b.rearrange("p (j e n) -> p j e n", e=2, n=P)[:, :, e, :]
                        nc.vector.tensor_tensor(osum[e * HD:(e + 1) * HD, 2 * g:2 * g + 2, :],
                                                pick(S[g][0:HD, :]), pick(olo[:, :]), ALU.add).then_inc(o_sum, 1)
                    dve.wait_ge(o_sum, 4 * t.n + 2 * g + 2)
                    nc.vector.scalar_tensor_tensor(osum[:, 2 * g:2 * g + 2, :], osum[:, 2 * g:2 * g + 2, :], 0.5,
                                                   gth[:, 256 * g:256 * g + 256].rearrange("p (j n) -> p j n", n=P),
                                                   ALU.mult, ALU.mult).then_inc(y_gated, 1)

                def y_lo_half(g):
                    dve.wait_ge(A.y_hi, 2 * t.n + g + 1)
                    nc.vector.tensor_tensor(ylo[:, 2 * g:2 * g + 2, :], osum[:, 2 * g:2 * g + 2, :],
                                            f(yhi[:, 2 * g:2 * g + 2, :]), ALU.subtract).then_inc(A.y_lo, 1)

                if t.real():
                    pT_lo(0)
                    pT_lo(1)
                if (t + -1).real():
                    add_out(A, t + -1, 0, J[0])
                if t.real():
                    y_half(0)
                    pT_lo(2)
                    pT_lo(3)
                if (t + -1).real():
                    add_out(A, t + -1, 1, J[1])
                if t.real():
                    y_lo_half(0)
                    y_half(1)
                    y_lo_half(1)
                if not (t.fixed and t.n == -2):
                    when(t + 2, lambda n: norm_scale(A, n))

            over_tiles(dve, body_a)
            dve.sem_inc(pass_a_done, 1)

            split_lo(B)
            dve.wait_ge(pass_a_done, 4)
            norm_scale(B, Tile(0, 0))
            dve.wait_ge(consts_b, N_CONSTS_B)
            dve.wait_ge(zeros_b, 4)

            def body_b(t):
                t1 = t + 1
                r = braw[t.par]
                st = sts if t.fixed and t.n == LAST else stp
                if t1.real():
                    split_x_lo(B, t1, 0)
                    split_x_lo(B, t1, 1)
                if t.real():
                    dve.wait_ge(z_psum, t.n + 1)
                    nc.vector.tensor_scalar(zm[:, :], S[0][:, 0:P], 0.0, None, ALU.min).then_inc(z_parts, 1)
                    dve.wait_ge(z_parts, 2 * t.n + 1)
                    nc.vector.scalar_tensor_tensor(az[:, :], zm[:, :], 2.0, S[0][:, 0:P], ALU.mult,
                                                   ALU.subtract).then_inc(z_parts, 1)
                    if t.fixed and t.n == LAST:
                        nc.vector.tensor_copy(ub[t.par][:, :, 0:HIST], uh[:, :, :]).then_inc(hist_ready, 1)
                    elif t.fixed and t.n == 0:
                        nc.vector.memset(ub[t.par][:, :, 0:HIST], 0.0).then_inc(hist_ready, 1)
                    else:
                        nc.vector.tensor_copy(ub[t.par][:, :, 0:HIST], ub[1 - t.par][:, :, P:P + HIST]).then_inc(
                            hist_ready, 1)
                    dve.wait_ge(z_ln, t.n + 1)
                    nc.vector.tensor_tensor(zm[:, :], zm[:, :], ez[:, :], ALU.subtract).then_inc(la_ready, 1)
                    dve.wait_ge(uT_taken, t.n + 1)
                    dve.wait_ge(hist_ready, t.n + 1)
                    conv(t, 0, 8)
                    dve.wait_ge(cum_exp, 2 * t.n + 2)
                    scale = GK ** -0.5
                    q, k = r[:, B_Q:B_Q + P], r[:, B_K:B_K + P]
                    nc.vector.scalar_tensor_tensor(qt[:, :], q, scale, ex[:, 0, :], ALU.mult, ALU.mult).then_inc(
                        qk_scaled, 1)
                    nc.vector.scalar_tensor_tensor(qf[:, :], q, scale, ex[:, 1, :], ALU.mult, ALU.mult).then_inc(
                        qk_scaled, 1)
                    nc.vector.tensor_tensor(kend[:, :], k, ex[:, 2, :], ALU.mult).then_inc(qk_scaled, 1)
                    nc.vector.tensor_tensor(kk[0:64, :], k[0:64], ex[0:64, 3, :], ALU.mult).then_inc(qk_scaled, 1)
                    nc.vector.tensor_tensor(kk[64:P, :], k[64:P], enb[64:P, :], ALU.mult).then_inc(qk_scaled, 1)
                    nc.vector.tensor_tensor(kt0[:, :], k[0:64], enb[0:64, :], ALU.mult).then_inc(qk_scaled, 1)
                    conv(t, 8, 30)
                    dve.wait_ge(g_dec, t.n + 1)
                    col = DEC - 1 if t.fixed and t.n == LAST else P - 1
                    dve.wait_ge(a_psum, t.n + 1)
                    nc.vector.tensor_copy(dec[:, :], T[1][:, col:col + 1]).then_inc(dec_ready, 1)
                    nc.vector.copy_predicated(asb[0:64, 0:256], mask[0:64, 0:256], S[0][0:64, 0:256]).then_inc(
                        a_masked, 1)
                    nc.vector.copy_predicated(asb[:, 256:512], mask[:, 256:512], S[0][:, 256:512]).then_inc(a_masked, 1)
                    conv(t, 30, 2 * CW)
                    dve.wait_ge(th_ready, 2 * t.n + 2)
                    nc.vector.scalar_tensor_tensor(thg[:, :], thg[:, :], 1.0, r[:, B_GG:B_GG + 256], ALU.add,
                                                   ALU.mult).then_inc(gates_ready, 1)
                    nc.vector.scalar_tensor_tensor(gc[:, :], thc[:, 256:512], 1.0, r[:, B_CG:B_CG + 256], ALU.add,
                                                   ALU.mult).then_inc(gates_ready, 1)
                    dve.wait_ge(go_psum, t.n + 1)
                    dve.wait_ge(dec_ready, t.n + 1)
                    for h in range(GH):
                        rows, cols = slice(h * GK, (h + 1) * GK), slice(h * GV, (h + 1) * GV)
                        last = nc.vector.scalar_tensor_tensor(st[rows, cols], st[rows, cols], dec[rows, :],
                                                              S[1][rows, cols], ALU.mult, ALU.add)
                    last.then_inc(g_state, 1)
                    dve.wait_ge(cT_psum, t.n + 1)
                    nc.vector.bn_stats(bst[:, :], T[0][:, 0:CD]).then_inc(bn_step, 1)
                    dve.wait_ge(bn_step, 2 * t.n + 1)
                    dve.wait_ge(go_sq, t.n + 1)
                    nc.vector.tensor_reduce(oss[:, :], osq[:, :].rearrange("p (h d) -> p h d", d=GV), AX.X,
                                            ALU.add).then_inc(go_ss, 1)
                    nc.vector.bn_aggr(mv[:, :], bst[:, :]).then_inc(bn_step, 1)
                if (t + -1).real():
                    add_out(B, t + -1, 0, J[1])
                if t.real():
                    dve.wait_ge(ln_r, t.n + 1)
                    nc.vector.tensor_scalar(cn[:, :], T[0][:, 0:CD], mv[:, 0:1], rs[:, :], ALU.subtract,
                                            ALU.mult).then_inc(cn_ready, 1)
                    dve.wait_ge(go_r, t.n + 1)
                    need(dve, yT_psum, t.n)
                    gv = lambda b: b.rearrange("p (h d) -> p h d", d=GV)
                    nc.vector.tensor_tensor(gv(yb[:, 0:256]), gv(T[2][:, 0:256]),
                                            orr[:, :].unsqueeze(2).to_broadcast([P, GH, GV]),
                                            ALU.mult).then_inc(go_n, 1)
                    dve.wait_ge(go_n, 2 * t.n + 1)
                    nc.vector.scalar_tensor_tensor(gv(yb[:, 0:256]), gv(yb[:, 0:256]), 0.5 * GV ** 0.5,
                                                   glagain[:, :].unsqueeze(1).to_broadcast([P, GH, GV]),
                                                   ALU.mult, ALU.mult).then_inc(go_n, 1)
                    dve.wait_ge(go_n, 2 * t.n + 2)
                    nc.vector.tensor_tensor(yb[:, 0:256], yb[:, 0:256], thg[:, :], ALU.mult).then_inc(go_g, 1)
                    dve.wait_ge(cnT_psum, t.n + 1)
                    for j in range(CJ):
                        nc.vector.tensor_scalar(cl[:, j, :], T[1][:, j * P:(j + 1) * P], convp[:, 1, j:j + 1],
                                                convp[:, 2, j:j + 1], ALU.mult, ALU.add).then_inc(cl_ready, 1)
                if (t + -1).real():
                    add_out(B, t + -1, 1, J[2])
                if t.real():
                    dve.wait_ge(cth_ready, t.n + 1)
                    nc.vector.scalar_tensor_tensor(cth[:, :, :], cth[:, :, :], 1.0, cl[:, :, :], ALU.add,
                                                   ALU.mult).then_inc(cs_ready, 1)
                if t1.real():
                    dve.wait_ge(th_ready, 2 * t1.n + 1)
                    nc.vector.tensor_scalar(thc[:, 0:256], thc[:, 0:256], 0.5, 0.5, ALU.mult, ALU.add).then_inc(sg_ready, 1)
                    dve.wait_ge(sg_ready, t1.n + 1)
                    if t1.fixed and t1.n == LAST:
                        dve.wait_ge(u_stored, 16)
                    nc.vector.tensor_tensor(u[:, :], braw[t1.par][:, B_CV:B_CV + 256], thc[:, 0:256], ALU.mult).then_inc(
                        u_ready, 1)
                if t.real():
                    dve.wait_ge(pw_psum, t.n + 1)
                    nc.vector.scalar_tensor_tensor(yb[:, 256:512], T[0][:, 0:CD], 0.5, bpw[:, :], ALU.mult,
                                                   ALU.add).then_inc(c2_ready, 1)
                    dve.wait_ge(c2_ready, t.n + 1)
                    nc.vector.scalar_tensor_tensor(yb[:, 256:512], yb[:, 256:512], 0.5, gc[:, :], ALU.mult,
                                                   ALU.mult).then_inc(yc_ready, 1)
                    dve.wait_ge(B.y_hi, t.n + 1)
                    nc.vector.tensor_tensor(ylo[:, :, :], T[1][:, :].rearrange("p (j n) -> p j n", n=P),
                                            f(yhi[:, :, :]), ALU.subtract).then_inc(B.y_lo, 1)
                if not (t.fixed and t.n == -2):
                    when(t + 2, lambda n: norm_scale(B, n))

            def conv(t, a, b):
                for n in range(a, b):
                    tap, j = n // CJ, n % CJ
                    src = ub[t.par][:, j, tap:tap + P]
                    w = convw[:, j, tap:tap + 1]
                    if tap == 0:
                        nc.vector.tensor_scalar(acc[:, j, :], src, w, convp[:, 0, j:j + 1], ALU.mult,
                                                ALU.add).then_inc(conv_step, 1)
                    else:
                        dve.wait_ge(conv_step, 2 * CW * t.n + n - 1)
                        nc.vector.scalar_tensor_tensor(acc[:, j, :], src, w, acc[:, j, :], ALU.mult,
                                                       ALU.add).then_inc(conv_step, 1)

            over_tiles(dve, body_b)

        @block.tensor
        def _(pe):
            pe.wait_ge(consts_a, N_CONSTS_A)
            pe.wait_ge(zeros_a, 3)

            def body_a(t):
                t1 = t + 1
                if t1.real():
                    need(pe, pt_lo, 4 * t.n)
                    transpose_x(A, t1, 0)
                    transpose_x(A, t1, 1)
                if t.real():
                    if t.fixed and t.n == LAST:
                        pe.wait_ge(c_lo, 3)
                        pe.wait_ge(pt_lo, 4 * t.n)
                        for j in range(4):
                            last = nc.tensor.transpose(T[0][:, j * P:(j + 1) * P], f(ckcat[:, j // 2, j % 2, :]),
                                                       ident[:, :])
                        last.then_inc(c_psum, 1)
                        pe.wait_ge(c_taken, 1)
                    order = ((T[2], 0), (T[0], 4))
                    pe.wait_ge(n_lo, 3 * t.n + 3)
                    need(pe, pt_lo, 4 * t.n)
                    for n, (bank, h0) in enumerate(order):
                        if n == 1 and t1.real():
                            pe.wait_ge(A.xT_lo, 2 * t1.n + 1)
                        for j in range(4):
                            last = nc.tensor.transpose(bank[:, j * P:(j + 1) * P], f(qcat[:, h0 + j, :]), ident[:, :])
                        last.then_inc(qkT_psum, 1)
                    if t1.real():
                        pe.wait_ge(A.xT_lo, 2 * t1.n + 2)
                    for j in range(4):
                        last = nc.tensor.transpose(T[1][:, j * P:(j + 1) * P], f(kcat[:, j // 2, j % 2, :]),
                                                   ident[:, :])
                    last.then_inc(qkT_psum, 1)
                    pe.wait_ge(qkT_taken, 3 * t.n + 1)
                    for j in range(4):
                        last = nc.tensor.transpose(T[2][:, j * P:(j + 1) * P], agraw[:, j * P:(j + 1) * P],
                                                   ident[:, :])
                    last.then_inc(gate_psum, 1)
                if t1.real():
                    need(pe, A.out_added, 2 * t.n - 2)
                    project(A, t1, 0, J[0])
                if t.real():
                    pe.wait_ge(qkT_taken, 3 * t.n + 3)
                    for n in range(4):
                        if n < 2:
                            need(pe, o_sum, 4 * t.n)
                        else:
                            pe.wait_ge(s_max, 8 * t.n + 2 * (n - 1))
                        for e in range(2):
                            h = 2 * n + e
                            for o in range(2):
                                last = nc.tensor.matmul(S[n % 2][:, e * 256:(e + 1) * 256], qT[:, h, :],
                                                        kT[:, h // GROUP, o, :], start=(o == 0), stop=(o == 1))
                        last.then_inc(s_psum, 1)
                if t1.real():
                    need(pe, A.out_added, 2 * t.n - 2)
                    project(A, t1, 1, J[1])
                    need(pe, A.taken[2], t1.n)
                    project(A, t1, 2, J[2])

                def pT(g, n):
                    bank = T[(2 * g + n) % 3]
                    k = 2 * g + n
                    if k == 2:
                        pe.wait_ge(gate_ready, t.n + 1)
                    if k == 3:
                        pe.wait_ge(pt_lo, 4 * t.n + 1)
                    for j in range(GROUP):
                        pe.wait_ge(p_ready, 8 * t.n + GROUP * g + j + 1)
                        last = nc.tensor.transpose(bank[:, j * P:(j + 1) * P],
                                                   sc[:, GROUP * g + j, n * P:(n + 1) * P], ident[:, :])
                    last.then_inc(pt_psum, 1)

                def pv(g):
                    pe.wait_ge(pt_lo, 4 * t.n + 2 * g + 2)
                    if g == 0:
                        pe.wait_ge(v_lo, t.n + 1)
                    for n in range(2):
                        for m, pt in enumerate((pthi, ptlo)):
                            last = nc.tensor.matmul(S[g][:, :], vcat[n][:, g, :], pt[:, n, :],
                                                    start=(n == 0 and m == 0), stop=(n == 1 and m == 1))
                    last.then_inc(o_psum, 1)

                def out(h):
                    if (t + -1).real():
                        if t1.real():
                            pe.wait_ge(A.taken[h], t1.n + 1)
                        elif h == 0 and not t1.real():
                            need(pe, A.out_added, 2 * t.n - 2)
                        output(A, t + -1, h, J[h])

                if t.real():
                    pT(0, 0)
                    pT(0, 1)
                out(0)
                if t.real():
                    pv(0)
                    pT(1, 0)
                    pT(1, 1)
                out(1)
                if t.real():
                    pv(1)

            over_tiles(pe, body_a)
            pe.sem_inc(pass_a_done, 1)

            pe.wait_ge(pass_a_done, 4)
            pe.wait_ge(consts_b, N_CONSTS_B)
            pe.wait_ge(zeros_b, 4)

            def body_b(t):
                t1 = t + 1
                r = braw[t.par]
                st = sts if t.fixed and t.n == LAST else stp
                if t.real():
                    pe.wait_ge(lr_taken, t.n + 1)
                    need(pe, go_n, 2 * t.n)
                    nc.tensor.transpose(T[2][0:LR + 1, 0:P], glr1[:, :], ident[:, :]).then_inc(lr_psum, 1)
                if t1.real():
                    need(pe, B.y_lo, t.n)
                    transpose_x(B, t1, 0)
                    transpose_x(B, t1, 1)
                if t.real():
                    pe.wait_ge(lr_T, t.n + 1)
                    need(pe, a_masked, 2 * t.n)
                    nc.tensor.matmul(S[0][:, 0:P], glrT[:, :], wup[:, :], start=True, stop=True).then_inc(z_psum, 1)
                    pe.wait_ge(u_ready, t.n + 1)
                    for j in range(CJ):
                        last = nc.tensor.transpose(T[2][:, j * P:(j + 1) * P], u[:, j * P:(j + 1) * P], ident[:, :])
                    last.then_inc(uT_psum, 1)
                if t1.real():
                    need(pe, B.taken[3], t1.n)
                    project(B, t1, 0, J[0])
                if t.real():
                    pe.wait_ge(la_ready, t.n + 1)
                    need(pe, g_state, t.n)
                    for n in range(4):
                        rows = slice(0, DEC) if n == 2 and t.fixed and t.n == LAST else slice(0, P)
                        last = nc.tensor.matmul(S[1][:, n * P:(n + 1) * P], tri[rows, n, :], zm[rows, :], start=True,
                                                stop=True)
                    last.then_inc(cum_psum, 1)
                if t1.real():
                    need(pe, B.out_added, 2 * t.n - 2)
                    project(B, t1, 1, J[1])
                if t.real():
                    pe.wait_ge(qk_scaled, 6 * t.n + 6)
                    pe.wait_ge(uT_taken, t.n + 1)
                    if t1.real():
                        pe.wait_ge(B.xT_lo, 2 * t1.n + 2)
                    nc.tensor.transpose(T[0][:, 0:P], qt[:, :], ident[:, :])
                    nc.tensor.transpose(T[0][:, P:2 * P], qf[:, :], ident[:, :])
                    nc.tensor.transpose(T[0][:, 2 * P:3 * P], kk[:, :], ident[:, :])
                    nc.tensor.transpose(T[0][:, 3 * P:3 * P + 64], kt0[:, :], ident[0:64, 0:64]).then_inc(g_psum, 1)
                    nc.tensor.transpose(T[1][:, 0:P], ex[:, 1, :], ident[:, :]).then_inc(g_dec, 1)
                if t1.real():
                    need(pe, B.out_added, 2 * t.n - 2)
                    project(B, t1, 2, J[2])
                if t.real():
                    qfT, kkT, ktT = gT[:, 0:P], gT[:, P:2 * P], gT[:, 2 * P:2 * P + 64]
                    pe.wait_ge(g_T, t.n + 1)
                    nc.tensor.matmul(S[0][0:64, 0:256].rearrange("p (h n) -> p h n", n=64), ktT, qbd[:, :, 0:64],
                                     start=True, stop=True)
                    nc.tensor.matmul(S[0][:, 256:512].rearrange("p (h n) -> p h n", n=64), kkT, qbd[:, :, 64:P],
                                     start=True, stop=True).then_inc(a_psum, 1)
                    rows = slice(0, DEC) if t.fixed and t.n == LAST else slice(0, P)
                    pe.wait_ge(cum_exp, 2 * t.n + 2)
                    pe.wait_ge(B.taken[1], t.n + 1)
                    nc.tensor.matmul(S[1][:, 0:256], kend[rows, :], r[rows, B_V:B_V + 256], start=True,
                                     stop=True).then_inc(su_psum, 1)
                if t1.real():
                    pe.wait_ge(B.taken[0], t1.n + 1)
                    project(B, t1, 3, J[0])
                if t.real():
                    pe.wait_ge(a_masked, 2 * t.n + 2)
                    nc.tensor.matmul(T[2][:, 0:256], qfT, st[:, :], start=True, stop=False, skip_group_check=True)
                    for c in range(2):
                        for h in range(GH):
                            rows = slice(0, 64) if c == 0 else slice(0, P)
                            last = nc.tensor.matmul(T[2][64 * c:64 * c + 64, h * GV:(h + 1) * GV],
                                                    asb[rows, 256 * c + 64 * h:256 * c + 64 * h + 64],
                                                    r[rows, B_V + h * GV:B_V + (h + 1) * GV], start=False,
                                                    stop=(c == 1 and h == GH - 1), skip_group_check=True)
                    last.then_inc(go_psum, 1)
                    pe.wait_ge(conv_step, 2 * CW * (t.n + 1))
                    for j in range(CJ):
                        last = nc.tensor.transpose(T[0][:, j * P:(j + 1) * P], acc[:, j, :], ident[:, :])
                    last.then_inc(cT_psum, 1)
                if (t + -1).real():
                    if t1.real():
                        pe.wait_ge(B.taken[1], t1.n + 1)
                    else:
                        need(pe, B.out_added, 2 * t.n - 2)
                    output(B, t + -1, 0, J[1])
                if t.real():
                    pe.wait_ge(cn_ready, t.n + 1)
                    pe.wait_ge(dec_ready, t.n + 1)
                    for j in range(CJ):
                        last = nc.tensor.transpose(T[1][:, j * P:(j + 1) * P], cn[:, j * P:(j + 1) * P], ident[:, :])
                    last.then_inc(cnT_psum, 1)
                if (t + -1).real():
                    if t1.real():
                        pe.wait_ge(B.taken[2], t1.n + 1)
                    output(B, t + -1, 1, J[2])
                if t.real():
                    pe.wait_ge(cs_ready, t.n + 1)
                    for j in range(CJ):
                        last = nc.tensor.matmul(T[0][:, 0:CD], cth[:, j, :], wpw[:, j, :], start=(j == 0),
                                                stop=(j == CJ - 1))
                    last.then_inc(pw_psum, 1)
                    pe.wait_ge(go_g, t.n + 1)
                    pe.wait_ge(yc_ready, t.n + 1)
                    for j in range(4):
                        last = nc.tensor.transpose(T[1][:, j * P:(j + 1) * P], yb[:, j * P:(j + 1) * P], ident[:, :])
                    last.then_inc(yT_psum, 1)

            over_tiles(pe, body_b)


def shape_constants():
    q = np.arange(P)[:, None]
    key = np.concatenate([np.arange(-P, P), np.arange(-P, 0)])[None, :]
    seen = np.where(q < CHUNK, (key >= -P) & (key < CHUNK), (key >= -CHUNK) & (key < P))
    slopes = 2.0 ** (-8.0 * np.arange(1, HEADS + 1) / HEADS)
    bias = np.where(seen[:, None, :], -slopes[None, :, None] * np.abs(q - key)[:, None, :], NEG).astype(np.float32)
    bias = (bias.view(np.uint32) >> 16).astype(np.uint16)
    ident = np.eye(P, dtype=np.float32)
    s, t = np.arange(P)[:, None], np.arange(P)[None, :]
    same = (s // CHUNK) == (t // CHUNK)
    tri = np.stack([(s <= t) & same, s <= t, s > t, (s > t) & same], 1).astype(np.float32) / 16.0
    tt = np.arange(64)[None, None, :]
    m0 = (s[:, :, None] < 64) & (s[:, :, None] <= tt)
    m1 = s[:, :, None] <= 64 + tt
    mask = np.concatenate([np.broadcast_to(m, (P, GH, 64)).reshape(P, 256) for m in (m0, m1)], 1).astype(np.float32)
    return bias, ident, tri, mask


def kernel(**inputs):
    import concourse.bacc as bacc
    from concourse.bass_utils import run_bass_kernel_spmd

    nc = bacc.Bacc("TRN2", target_bir_lowering=False, num_devices=1, dynamic_dma_scratch_size=1024)
    arrays, ins, consts = {}, [], []
    for name in INS:
        a = np.ascontiguousarray(inputs[name])
        arrays[f"in_{name}"] = a
        ins.append(nc.dram_tensor(f"in_{name}", a.shape, mybir.dt.from_np(a.dtype), kind="ExternalInput").ap())
    for n, a in enumerate(shape_constants()):
        a = np.ascontiguousarray(a)
        arrays[f"const_{n}"] = a
        consts.append(nc.dram_tensor(f"const_{n}", a.shape, mybir.dt.from_np(a.dtype), kind="ExternalInput").ap())
    outs = [nc.dram_tensor(f"out_{n}", shape, F32, kind="ExternalOutput").ap() for n, shape in enumerate(OUTS)]
    build(nc, ins, consts, outs)
    r = run_bass_kernel_spmd(nc, [arrays], core_ids=[0])
    return tuple(r.results[0][f"out_{n}"] for n in range(len(OUTS)))
```

```python
from contextlib import ExitStack

import numpy as np

import concourse.bass as bass
from concourse import mybir

ALU = mybir.AluOpType
ACT = mybir.ActivationFunctionType
AX = mybir.AxisListType
F32 = mybir.dt.float32
F32R = mybir.dt.float32r
BF16 = mybir.dt.bfloat16
U16 = mybir.dt.uint16
U32 = mybir.dt.uint32

P = 128
D = 1024
KT = D // P
SEQ = 2048
DEC = 64
CHUNK = 64
TILES = SEQ // P + 1
LAST = TILES - 1
HEADS, KVH, HD = 8, 2, 64
GROUP = HEADS // KVH
GH, GK, GV, LR = 4, 32, 64, 16
CW = 31
HIST = CW - 1
CD = 256
CJ = CD // P
EPS = 1e-6
NEG = -1e30
ATT = HEADS * HD

AQ, AKV, AG = (0, 512), (512, 256), (768, 512)
GQK, GVC, GGC, GLR = (1280, 256), (1536, 256), (1792, 256), (2048, 16)
CV, CGL, CG = (2064, 256), (2320, 256), (2576, 256)
CHUNKS_A = [[AQ], [AKV], [AG]]
CHUNKS_B = [[GLR, GQK], [GVC, GGC], [CV, CGL], [CG]]
WIDTH_A = [sum(w for _, w in c) for c in CHUNKS_A]
WIDTH_B = [sum(w for _, w in c) for c in CHUNKS_B]
B_GLR, B_Q, B_K, B_V, B_GG, B_CV, B_CGL, B_CG = 0, 16, 144, 272, 528, 784, 1040, 1296
B_COLS = sum(WIDTH_B)
STAGES = 4

INS = ["x_prompt", "x_sample", "cache_k", "cache_v", "state_gla", "state_conv", "norm_gain", "w_in",
       "q_norm_gain", "k_norm_gain", "attn_sinks", "gla_w_gate_up", "gla_b_gate", "gla_norm_gain",
       "conv_w", "conv_b", "conv_ln_gain", "conv_ln_bias", "conv_w_pw", "conv_b_pw", "w_out"]
OUTS = [(1, SEQ, D), (1, DEC, D), (1, 1, P, KVH, HD), (1, 1, P, KVH, HD), (1, 1, GH, GK, GV), (1, 1, HIST, CD),
        (1, 1, P, KVH, HD), (1, 1, P, KVH, HD), (1, 1, GH, GK, GV), (1, 1, HIST, CD)]


class Tile:

    def __init__(self, i, c):
        self.i, self.c = i, c
        self.par = c % 2
        self.n = 2 * i + c
        self.half = i + c // 2
        self.fixed = isinstance(self.n, int)

    def __add__(self, k):
        return Tile(self.i, self.c + k)

    def real(self):
        return not self.fixed or 0 <= self.n < TILES


def need(eng, sem, count):
    if isinstance(count, int) and count <= 0:
        return
    eng.wait_ge(sem, count)


def pieces_of(chunks):
    out, base = [], 0
    for n, chunk in enumerate(chunks):
        width = sum(w for _, w in chunk)
        for k in range(KT):
            col = (k * width,) if n == 3 else base + k * width
            out.append(("in", k, chunk, col, width))
        base += KT * width
    for k in range(4):
        for h in range(2):
            out.append(("out", k, h, W_OUT + k * D + h * 512, 512))
    return out


W_OUT = KT * sum(WIDTH_B[:3])
W_COLS = W_OUT + 4 * D


def build(nc, ins, consts, outs):
    io = dict(zip(INS, ins))
    bias_d, ident_d, tri_d, mask_d = consts
    yp, ys, pk_o, pv_o, ps_o, pc_o, sk_o, sv_o, ss_o, sc_o = outs
    es = ExitStack()

    def sb(name, shape, dt=F32, ctx=es):
        return ctx.enter_context(nc.sbuf_tensor(name, shape, dt))

    def sem(name):
        return es.enter_context(nc.semaphore(name))

    with es:
        whi = sb("whi", [P, W_COLS], F32R)
        wlo = sb("wlo", [P, W_COLS], F32R)
        wraw = sb("wraw", [P, STAGES, 512])
        ident = sb("ident", [P, P])
        gain = sb("gain", [P, KT])
        mhalf = sb("mhalf", [P, 16])
        eps_d = sb("eps_d", [P, 1])
        eps_h = sb("eps_h", [P, 16])
        eps_1 = sb("eps_1", [P, 1])
        xin = [sb(f"xin{i}", [P, D]) for i in range(2)]
        xn = sb("xn", [P, D])
        xhi = sb("xhi", [P, KT, P], F32R)
        xlo = sb("xlo", [P, KT, P], F32R)
        res = [sb(f"res{i}", [P, D]) for i in range(2)]
        yhi = sb("yhi", [P, 4, P], F32R)
        ylo = sb("ylo", [P, 4, P], F32R)
        ssum = sb("ssum", [P, 1])
        msum = sb("msum", [P, 1])
        rinv = sb("rinv", [P, 1])
        ea = ExitStack()
        bias = sb("bias", [P, HEADS, 384], BF16, ea)
        qkgain = sb("qkgain", [P, 2, HD], F32, ea)
        sinks = sb("sinks", [P, HEADS], F32, ea)
        raw = sb("raw", [P, 768], F32, ea)
        qkn = sb("qkn", [P, 640], F32, ea)
        agraw = sb("agraw", [P, 512], F32, ea)
        gth = sb("gth", [P, 512], F32, ea)
        qss = sb("qss", [P, 10], F32, ea)
        qms = sb("qms", [P, 10], F32, ea)
        qr = sb("qr", [P, 10], F32, ea)
        qcat = sb("qcat", [P, HEADS, P], F32R, ea)
        kcat = sb("kcat", [P, KVH, 2, P], F32R, ea)
        vcat = [sb(f"vcat{i}", [P, KVH, P], F32R, ea) for i in range(2)]
        qT = sb("qT", [P, HEADS, P], F32R, ea)
        kT = sb("kT", [P, KVH, 2, 2 * P], F32R, ea)
        sc = sb("sc", [P, HEADS, 2 * P], F32, ea)
        mx = sb("mx", [P, HEADS], F32, ea)
        nmx = sb("nmx", [P, HEADS], F32, ea)
        esum = sb("esum", [P, HEADS], F32, ea)
        sdif = sb("sdif", [P, HEADS], F32, ea)
        esink = sb("esink", [P, HEADS], F32, ea)
        den = sb("den", [P, HEADS], F32, ea)
        rden = sb("rden", [P, HEADS], F32, ea)
        pthi = sb("pthi", [P, 2, 512], F32R, ea)
        ptlo = sb("ptlo", [P, 2, 512], F32R, ea)
        olo = sb("olo", [HD, 512], F32, ea)
        osum = sb("osum", [P, 4, P], F32, ea)
        ckv = sb("ckv", [P, 2, P], F32, ea)
        ckcat = sb("ckcat", [P, KVH, 2, P], F32R, ea)
        ea.close()
        w2hi = sb("w2hi", [P, KT * WIDTH_B[3]], F32R)
        w2lo = sb("w2lo", [P, KT * WIDTH_B[3]], F32R)
        tri = sb("tri", [P, 4, P])
        mask = sb("mask", [P, 512], U32)
        wup = sb("wup", [LR + 1, P])
        glagain = sb("glagain", [P, GV])
        bpw = sb("bpw", [P, CD])
        wpw = sb("wpw", [P, CJ, CD])
        convw = sb("convw", [P, CJ, CW])
        convp = sb("convp", [P, 3, CJ])
        braw = [sb(f"braw{i}", [P, B_COLS]) for i in range(2)]
        glr1 = sb("glr1", [P, LR + 1])
        glrT = sb("glrT", [LR + 1, P])
        az = sb("az", [P, P])
        zm = sb("zm", [P, P])
        ez = sb("ez", [P, P])
        ex = sb("ex", [P, 4, P])
        enb = sb("enb", [P, P])
        qt = sb("qt", [P, P])
        qf = sb("qf", [P, P])
        kk = sb("kk", [P, P])
        kt0 = sb("kt0", [64, P])
        kend = sb("kend", [P, P])
        qbd = sb("qbd", [P, GH, P])
        gT = sb("gT", [P, 320])
        dec = sb("dec", [P, 1])
        asb = sb("asb", [P, 512])
        stp = sb("stp", [P, 256])
        sts = sb("sts", [P, 256])
        osq = sb("osq", [P, 256])
        oss = sb("oss", [P, GH])
        oms = sb("oms", [P, GH])
        orr = sb("orr", [P, GH])
        thg = sb("thg", [P, 256])
        thc = sb("thc", [P, 512])
        gc = sb("gc", [P, CD])
        u = sb("u", [P, CD])
        ub = [sb(f"ub{i}", [P, CJ, HIST + P]) for i in range(2)]
        acc = sb("acc", [P, CJ, P])
        bst = sb("bst", [P, 6])
        mv = sb("mv", [P, 2])
        mve = sb("mve", [P, 1])
        rs = sb("rs", [P, 1])
        cn = sb("cn", [P, CD])
        cl = sb("cl", [P, CJ, P])
        cth = sb("cth", [P, CJ, P])
        yb = sb("yb", [P, 512])
        uh = sb("uh", [P, CJ, HIST])

        T = [es.enter_context(nc.psum_tensor(f"T{i}", [P, 512], F32)) for i in range(3)]
        J = [es.enter_context(nc.psum_tensor(f"J{i}", [P, 512], F32)) for i in range(3)]
        S = [es.enter_context(nc.psum_tensor(f"S{i}", [P, 512], F32)) for i in range(2)]

        f = lambda t: t.bitcast(F32)

        def weights(col, width):
            if isinstance(col, tuple):
                return w2hi[:, col[0]:col[0] + width], w2lo[:, col[0]:col[0] + width]
            return whi[:, col:col + width], wlo[:, col:col + width]

        class Pass:

            def __init__(self, tag, chunks):
                self.tag, self.pieces = tag, pieces_of(chunks)
                self.widths = [sum(w for _, w in c) for c in chunks]
                self.x_banks = (1, 0) if tag == "a" else (0, 1)
                self.first_chunk = 0 if tag == "a" else 1
                self.raw = [sem(f"weights_loaded_{tag}{i}") for i in range(STAGES)]
                self.whi = sem(f"weights_hi_{tag}")
                self.wlo = sem(f"weights_lo_{tag}")
                self.x_loaded = [sem(f"x_loaded_{tag}{i}") for i in range(2)]
                self.x_squared = sem(f"x_squared_{tag}")
                self.x_mean = sem(f"x_mean_{tag}")
                self.x_rinv = sem(f"x_rinv_{tag}")
                self.xn_ready = sem(f"xn_ready_{tag}")
                self.xT_psum = sem(f"xT_psum_{tag}")
                self.xT_hi = sem(f"xT_hi_{tag}")
                self.xT_lo = sem(f"xT_lo_{tag}")
                self.projected = [sem(f"projected_{tag}{i}") for i in range(len(chunks))]
                self.taken = [sem(f"projection_taken_{tag}{i}") for i in range(len(chunks))]
                self.res_loaded = [sem(f"res_loaded_{tag}{i}") for i in range(2)]
                self.y_hi = sem(f"y_hi_{tag}")
                self.y_lo = sem(f"y_lo_{tag}")
                self.out_psum = sem(f"out_psum_{tag}")
                self.out_added = sem(f"out_added_{tag}")
                self.out_stored = [sem(f"out_stored_{tag}{i}") for i in range(2)]

        A, B = Pass("a", CHUNKS_A), Pass("b", CHUNKS_B)
        first_consts = sem("first_consts")
        consts_a, consts_b, zeros_a, zeros_b = sem("consts_a"), sem("consts_b"), sem("zeros_a"), sem("zeros_b")
        zeros_b1, pool_consts = sem("zeros_b1"), sem("pool_consts")
        v_hi, v_lo = sem("v_hi"), sem("v_lo")
        qkT_psum, qkT_taken = sem("qkT_psum"), sem("qkT_taken")
        gate_psum, gate_tanh, gate_ready = sem("gate_psum"), sem("gate_tanh"), sem("gate_ready")
        s_psum, s_max, s_neg, s_exp = sem("scores_psum"), sem("scores_max"), sem("scores_neg"), sem("scores_exp")
        s_diff, s_esink, s_den, s_rden, p_ready = (sem("sink_diff"), sem("sink_exp"), sem("softmax_den"),
                                                  sem("softmax_rden"), sem("p_ready"))
        n_step, n_mean, n_rinv, n_hi, n_lo = (sem("qk_norm_step"), sem("qk_mean"), sem("qk_rinv"), sem("qk_hi"),
                                              sem("qk_lo"))
        pt_psum, pt_hi, pt_lo = sem("pT_psum"), sem("pT_hi"), sem("pT_lo")
        o_psum, o_low, o_sum, y_gated = sem("o_psum"), sem("o_low"), sem("o_sum"), sem("y_gated")
        windows_stored = sem("windows_stored")
        c_hi, c_lo, c_psum, c_taken = sem("cache_hi"), sem("cache_lo"), sem("cache_psum"), sem("cache_taken")
        pass_a_done = sem("pass_a_done")

        states_stored, u_stored, dec_ready = sem("states_stored"), sem("u_stored"), sem("dec_ready")
        lr_taken, lr_psum, lr_T = sem("lowrank_taken"), sem("lowrank_psum"), sem("lowrank_T")
        z_psum, z_parts, z_exp, z_ln, la_ready = (sem("gate_logit_psum"), sem("gate_logit_parts"),
                                                 sem("gate_logit_exp"), sem("gate_logit_ln"), sem("log_decay_ready"))
        cum_psum, cum_exp, qk_scaled = sem("decay_sums_psum"), sem("decay_exp"), sem("gla_qk_scaled")
        g_psum, g_T, g_dec = sem("gla_T_psum"), sem("gla_T_taken"), sem("gla_decay")
        a_psum, a_masked, su_psum, go_psum = (sem("gla_scores_psum"), sem("gla_scores_masked"),
                                              sem("gla_state_psum"), sem("gla_o_psum"))
        g_state = sem("gla_state_ready")
        go_sq, go_ss, go_ms, go_r, go_n, go_g = (sem("gla_o_squared"), sem("gla_o_sums"), sem("gla_o_mean"),
                                                sem("gla_o_rinv"), sem("gla_o_normed"), sem("gla_y_ready"))
        th_ready, gates_ready, sg_ready, u_ready = (sem("tanh_ready"), sem("gates_ready"), sem("glu_gate_ready"),
                                                   sem("u_ready"))
        uT_psum, hist_ready, uT_taken, conv_step = (sem("uT_psum"), sem("hist_ready"), sem("uT_taken"),
                                                   sem("conv_step"))
        cT_psum, bn_step, ln_mean, ln_r, cn_ready = (sem("cT_psum"), sem("ln_step"), sem("ln_mean"), sem("ln_rinv"),
                                                    sem("conv_normed"))
        cnT_psum, cl_ready, cth_ready, cs_ready = (sem("cnT_psum"), sem("ln_affine_ready"), sem("conv_tanh"),
                                                  sem("conv_silu"))
        pw_psum, c2_ready, yc_ready, yT_psum = sem("pw_psum"), sem("pw_taken"), sem("conv_y_ready"), sem("yT_psum")

        N_CONSTS_A, N_CONSTS_B = 16 * 6, 16 * (14 + GH)

        B_16, B_17 = 2 * KT, 3 * KT

        def load_weights(eng, ps, first, last):
            for n, (part, k, what, col, width) in list(enumerate(ps.pieces))[first:last]:
                if n >= STAGES:
                    need(eng, ps.wlo, n - STAGES + 1)
                rows = slice(k * P, (k + 1) * P)
                dst = wraw[:, n % STAGES, :]
                if part == "in":
                    at = 0
                    for first, w in what:
                        eng.dma_start(dst[:, at:at + w], io["w_in"][0, rows, first:first + w]).then_inc(
                            ps.raw[n % STAGES], 16)
                        at += w
                else:
                    r0 = (0 if ps is A else 512) + k * P
                    eng.dma_start(dst, io["w_out"][0, r0:r0 + P, what * 512:(what + 1) * 512]).then_inc(
                        ps.raw[n % STAGES], 16)

        def raw_counts(ps):
            count, out = [0] * STAGES, []
            for n, (part, k, what, col, width) in enumerate(ps.pieces):
                count[n % STAGES] += 16 * (len(what) if part == "in" else 1)
                out.append(count[n % STAGES])
            return out

        def split_hi(ps, a, b):
            for n, (part, k, what, col, width) in list(enumerate(ps.pieces))[a:b]:
                nc.scalar.wait_ge(ps.raw[n % STAGES], raw_counts(ps)[n])
                if ps is B and n == 0:
                    nc.scalar.wait_ge(A.projected[2], TILES)
                if ps is B and n == 3 * KT:
                    nc.scalar.wait_ge(windows_stored, 16 * 6)
                if ps is B and part == "out" and k == 0 and what == 0:
                    nc.scalar.wait_ge(A.out_psum, 2 * TILES)
                scale = gain[:, k:k + 1] if part == "in" else 1.0
                nc.scalar.activation(weights(col, width)[0], wraw[:, n % STAGES, 0:width], ACT.Copy,
                                     scale=scale).then_inc(ps.whi, 1)

        def split_lo(ps, a, b):
            for n, (part, k, what, col, width) in list(enumerate(ps.pieces))[a:b]:
                nc.vector.wait_ge(ps.whi, n + 1)
                src = wraw[:, n % STAGES, 0:width]
                hi, lo = weights(col, width)
                if part == "in":
                    nc.vector.scalar_tensor_tensor(lo, src, gain[:, k:k + 1], f(hi), ALU.mult,
                                                   ALU.subtract).then_inc(ps.wlo, 1)
                else:
                    nc.vector.tensor_tensor(lo, src, f(hi), ALU.subtract).then_inc(ps.wlo, 1)

        def x_rows(src_p, src_s, t, cols=slice(0, D)):
            if t.fixed and t.n == LAST:
                return src_s[0, 0:DEC, cols], DEC
            return src_p[0, bass.ds(t.n * P, P), cols], P

        def load_x(ps, t):
            need(nc.sync, ps.xn_ready, t.n - 1)
            src, rows = x_rows(io["x_prompt"], io["x_sample"], t)
            nc.sync.dma_start(xin[t.par][0:rows, :], src).then_inc(ps.x_loaded[t.par], 16)

        def load_res(ps, t):
            need(nc.sync, ps.out_stored[t.par], 32 * t.half)
            if ps is A:
                src, rows = x_rows(io["x_prompt"], io["x_sample"], t)
            else:
                src, rows = x_rows(yp, ys, t)
            nc.sync.dma_start(res[t.par][0:rows, :], src).then_inc(ps.res_loaded[t.par], 16)

        def store_out(ps, t):
            for h in range(2):
                need(nc.sync, ps.out_added, 2 * t.n + h + 1)
                dst, rows = x_rows(yp, ys, t, slice(h * 512, (h + 1) * 512))
                nc.sync.dma_start(dst, res[t.par][0:rows, h * 512:(h + 1) * 512]).then_inc(
                    ps.out_stored[t.par], 16)

        def norm_square(ps, t):
            nc.scalar.wait_ge(ps.x_loaded[t.par], 16 * (t.half + 1))
            need(nc.scalar, ps.xT_psum, 2 * t.n)
            nc.scalar.activation(xn[:, :], xin[t.par][:, :], ACT.Square, accum_out=ssum[:, :]).then_inc(
                ps.x_squared, 1)

        def norm_rinv(ps, t):
            nc.gpsimd.wait_ge(ps.x_squared, t.n + 1)
            nc.gpsimd.tensor_tensor(msum[:, :], ssum[:, :], eps_d[:, :], ALU.add).then_inc(ps.x_mean, 1)
            nc.gpsimd.wait_ge(ps.x_mean, t.n + 1)
            nc.gpsimd.tensor_tensor(rinv[:, :], msum[:, :], mhalf[:, 0:1], ALU.pow).then_inc(ps.x_rinv, 1)

        def norm_scale(ps, t):
            nc.vector.wait_ge(ps.x_rinv, t.n + 1)
            nc.vector.tensor_scalar(xn[:, :], xin[t.par][:, :], rinv[:, :], D ** 0.5, ALU.mult,
                                    ALU.mult).then_inc(ps.xn_ready, 1)

        def transpose_x(ps, t, g):
            if g == 0:
                nc.tensor.wait_ge(ps.xn_ready, t.n + 1)
            for j in range(4):
                last = nc.tensor.transpose(T[ps.x_banks[g]][:, j * P:(j + 1) * P], 
                                           xn[:, (4 * g + j) * P:(4 * g + j + 1) * P], ident[:, :])
            last.then_inc(ps.xT_psum, 1)

        def split_x_hi(ps, t, g):
            nc.scalar.wait_ge(ps.xT_psum, 2 * t.n + g + 1)
            nc.scalar.activation(xhi[:, 4 * g:4 * g + 4, :], T[ps.x_banks[g]][:, :].rearrange("p (j n) -> p j n", n=P),
                                 ACT.Copy).then_inc(ps.xT_hi, 1)

        def split_x_lo(ps, t, g):
            nc.vector.wait_ge(ps.xT_hi, 2 * t.n + g + 1)
            nc.vector.tensor_tensor(xlo[:, 4 * g:4 * g + 4, :],
                                    T[ps.x_banks[g]][:, :].rearrange("p (j n) -> p j n", n=P), f(xhi[:, 4 * g:4 * g + 4, :]), ALU.subtract).then_inc(ps.xT_lo, 1)

        def project(ps, t, c, bank):
            width = ps.widths[c]
            base = KT * sum(ps.widths[:c])
            if c == ps.first_chunk:
                nc.tensor.wait_ge(ps.xT_lo, 2 * t.n + 2)
            if t.fixed and t.n == 0:
                nc.tensor.wait_ge(ps.wlo, KT * (c + 1))
            for k in range(KT):
                hi, lo = weights((k * width,) if c == 3 else base + k * width, width)
                for n, (x, w) in enumerate(((xhi, hi), (xhi, lo), (xlo, hi))):
                    last = nc.tensor.matmul(bank[:, 0:width], x[:, k, :], w, start=(k == 0 and n == 0),
                                            stop=(k == KT - 1 and n == 2))
            last.then_inc(ps.projected[c], 1)

        def output(ps, t, h, bank):
            if h == 0:
                nc.tensor.wait_ge(ps.y_lo, (t.n + 1) * (2 if ps is A else 1))
            if t.fixed and t.n == 0:
                nc.tensor.wait_ge(ps.wlo, len(ps.pieces))
            for k in range(4):
                col = W_OUT + k * D + h * 512
                hi, lo = weights(col, 512)
                for n, (y, w) in enumerate(((yhi, hi), (yhi, lo), (ylo, hi))):
                    last = nc.tensor.matmul(bank[:, :], y[:, k, :], w, start=(k == 0 and n == 0),
                                            stop=(k == 3 and n == 2))
            last.then_inc(ps.out_psum, 1)

        def add_out(ps, t, h, bank):
            if h == 0:
                nc.vector.wait_ge(ps.res_loaded[t.par], 16 * (t.half + 1))
            nc.vector.wait_ge(ps.out_psum, 2 * t.n + h + 1)
            dst = res[t.par][:, h * 512:(h + 1) * 512]
            nc.vector.tensor_tensor(dst, bank[:, :], dst, ALU.add).then_inc(ps.out_added, 1)

        def over_tiles(eng, body, first=3, last=14):
            for c in range(-2, first):
                body(Tile(0, c))
            with eng.Fori(0, (last - first + 1) // 2) as i:
                body(Tile(i, first))
                body(Tile(i, first + 1))
            for c in range(last + 1, TILES + 1):
                body(Tile(0, c))

        def when(t, *steps):
            for s in steps if t.real() else ():
                s(t)

        es.enter_context(nc.allow_non_contiguous_dma(reason="small vectors of parameters, once"))
        block = es.enter_context(nc.Block())

        @block.sync
        def _(sp):
            for dst, src in ((gain[:, :], io["norm_gain"][0].rearrange("(k p) -> p k", p=P)),
                             (ident[:, :], ident_d)):
                sp.dma_start(dst, src).then_inc(first_consts, 16)
            load_x(A, Tile(0, 0))
            load_weights(sp, A, 0, STAGES)
            load_x(A, Tile(0, 1))
            load_weights(sp, A, STAGES, KT)
            for dst, src in ((bias[:, :, :], bias_d.bitcast(BF16)),
                             (qkgain[:, 0, :], io["q_norm_gain"].partition_broadcast(P)),
                             (qkgain[:, 1, :], io["k_norm_gain"].partition_broadcast(P)),
                             (sinks[:, :], io["attn_sinks"].partition_broadcast(P)),
                             (ckv[:, 0, :], io["cache_k"][0, 0].rearrange("w h d -> w (h d)")),
                             (ckv[:, 1, :], io["cache_v"][0, 0].rearrange("w h d -> w (h d)"))):
                sp.dma_start(dst, src).then_inc(consts_a, 16)
            load_weights(sp, A, KT, 3 * KT)
            for src, dst in ((io["cache_k"], sk_o), (io["cache_v"], sv_o)):
                sp.dma_start(dst[0, 0, 0:DEC], src[0, 0, DEC:P]).then_inc(windows_stored, 16)

            def body_a(t):
                if t.fixed and t.n == -2:
                    return
                if (t + 3).real():
                    load_x(A, t + 3)
                if t.real():
                    load_res(A, t)
                if t.fixed and t.n == 0:
                    load_weights(sp, A, 3 * KT, len(A.pieces))
                if t.fixed and t.n == TILES:
                    sp.wait_ge(A.xn_ready, TILES)
                    for i in range(2):
                        load_x(B, Tile(0, i))
                for at, first, last in ((LAST - 2, 0, STAGES), (LAST, STAGES, B_16), (TILES, B_16, B_17 + STAGES)):
                    if t.fixed and t.n == at:
                        load_weights(sp, B, first, last)
                if t.fixed and t.n + 1 in (LAST - 1, LAST):
                    rows = P if t.n + 1 == LAST - 1 else DEC
                    k_dst, v_dst = (pk_o, pv_o) if rows == P else (sk_o, sv_o)
                    sp.wait_ge(n_step, 5 * (t.n + 2))
                    sp.dma_start(k_dst[0, 0, P - rows:P].rearrange("w h d -> w (h d)"),
                                 qkn[0:rows, 512:640]).then_inc(windows_stored, 16)
                    sp.dma_start(v_dst[0, 0, P - rows:P].rearrange("w h d -> w (h d)"),
                                 raw[0:rows, 640:768]).then_inc(windows_stored, 16)
                if (t + -1).real():
                    store_out(A, t + -1)

            over_tiles(sp, body_a, 3, 12)
            load_weights(sp, B, B_17 + STAGES, 4 * KT)
            for i in range(2):
                sp.wait_ge(A.out_stored[i], 32 * ((TILES + 1 - i) // 2))
            sp.wait_ge(windows_stored, 16 * 6)
            sp.wait_ge(pass_a_done, 4)
            for dst, src in ((tri[:, :, :], tri_d), (mask[:, :], mask_d.bitcast(U32)),
                             (wup[0:LR, :], io["gla_w_gate_up"][0]), (wup[LR:LR + 1, :], io["gla_b_gate"]),
                             (glagain[:, :], io["gla_norm_gain"].partition_broadcast(P)),
                             (bpw[:, :], io["conv_b_pw"].partition_broadcast(P)),
                             (wpw[:, :, :], io["conv_w_pw"][0].rearrange("(j p) n -> p j n", p=P)),
                             (convp[:, 0, :], io["conv_b"][0].rearrange("(j p) -> p j", p=P)),
                             (convp[:, 1, :], io["conv_ln_gain"][0].rearrange("(j p) -> p j", p=P)),
                             (convp[:, 2, :], io["conv_ln_bias"][0].rearrange("(j p) -> p j", p=P)),
                             (convw[:, 0, :], io["conv_w"][0, :, 0:P].rearrange("w p -> p w")),
                             (convw[:, 1, :], io["conv_w"][0, :, P:CD].rearrange("w p -> p w")),
                             (uh[:, 0, :], io["state_conv"][0, 0, :, 0:P].rearrange("w p -> p w")),
                             (uh[:, 1, :], io["state_conv"][0, 0, :, P:CD].rearrange("w p -> p w"))):
                sp.dma_start(dst, src).then_inc(consts_b, 16)
            sp.wait_ge(zeros_b1, 1)
            for h in range(GH):
                sp.dma_start(sts[h * GK:(h + 1) * GK, h * GV:(h + 1) * GV], io["state_gla"][0, 0, h]).then_inc(
                    consts_b, 16)

            def body_b(t):
                if t.fixed and t.n == -2:
                    return
                if (t + 3).real():
                    load_x(B, t + 3)
                if t.real():
                    load_res(B, t)
                if t.fixed and t.n == 0:
                    load_weights(sp, B, 4 * KT, len(B.pieces))
                if t.fixed and t.n in (LAST - 1, LAST):
                    end, dst = (P, pc_o) if t.n == LAST - 1 else (DEC, sc_o)
                    sp.wait_ge(u_ready, t.n + 1)
                    sp.dma_start(dst[0, 0], u[end - HIST:end, :]).then_inc(u_stored, 16)
                    st, dst = (stp, ps_o) if t.n == LAST - 1 else (sts, ss_o)
                    sp.wait_ge(g_state, t.n + 1)
                    for h in range(GH):
                        sp.dma_start(dst[0, 0, h], st[h * GK:(h + 1) * GK, h * GV:(h + 1) * GV]).then_inc(
                            states_stored, 16)
                if (t + -1).real():
                    store_out(B, t + -1)

            over_tiles(sp, body_b, 3, 12)
            for i in range(2):
                sp.wait_ge(B.out_stored[i], 32 * ((TILES + 1 - i) // 2))
            sp.wait_ge(states_stored, 16 * 8)
            sp.wait_ge(u_stored, 16 * 2)

        @block.gpsimd
        def _(pool):
            for buf, value in ((mhalf, -0.5), (eps_d, D * EPS), (eps_h, HD * EPS), (eps_1, EPS)):
                nc.gpsimd.memset(buf[:, :], value).then_inc(pool_consts, 1)
            pool.wait_ge(pool_consts, 4)
            norm_rinv(A, Tile(0, 0))

            def body_a(t):
                if not (t.fixed and t.n == -2):
                    when(t + 2, lambda n: norm_rinv(A, n))
                n = t + 1
                if n.real():
                    pool.wait_ge(n_step, 5 * n.n + 2)
                    nc.gpsimd.tensor_tensor(qms[:, :], qss[:, :], eps_h[:, 0:10], ALU.add).then_inc(
                        n_mean, 1)
                    pool.wait_ge(n_mean, n.n + 1)
                    nc.gpsimd.tensor_tensor(qr[:, :], qms[:, :], mhalf[:, 0:10], ALU.pow).then_inc(n_rinv, 1)

            over_tiles(pool, body_a)
            pool.sem_inc(pass_a_done, 1)
            norm_rinv(B, Tile(0, 0))
            pool.wait_ge(pass_a_done, 4)
            nc.gpsimd.memset(sts[:, :], 0.0).then_inc(zeros_b1, 1)
            for buf in (stp, asb):
                nc.gpsimd.memset(buf[:, :], 0.0).then_inc(zeros_b, 1)
            nc.gpsimd.memset(qbd[:, :, :], 0.0).then_inc(zeros_b, 1)
            nc.gpsimd.memset(glr1[:, LR:LR + 1], 1.0).then_inc(zeros_b, 1)

            def body_b(t):
                p = t + -1
                if p.real():
                    pool.wait_ge(bn_step, 2 * p.n + 2)
                    nc.gpsimd.tensor_tensor(mve[:, :], mv[:, 1:2], eps_1[:, :], ALU.add).then_inc(ln_mean, 1)
                    pool.wait_ge(ln_mean, p.n + 1)
                    nc.gpsimd.tensor_tensor(rs[:, :], mve[:, :], mhalf[:, 0:1], ALU.pow).then_inc(ln_r, 1)
                if not (t.fixed and t.n == -2):
                    when(t + 2, lambda n: norm_rinv(B, n))
                if t.real():
                    pool.wait_ge(go_ss, t.n + 1)
                    nc.gpsimd.tensor_tensor(oms[:, :], oss[:, :], eps_h[:, 0:GH], ALU.add).then_inc(
                        go_ms, 1)
                    pool.wait_ge(go_ms, t.n + 1)
                    nc.gpsimd.tensor_tensor(orr[:, :], oms[:, :], mhalf[:, 0:GH], ALU.pow).then_inc(go_r, 1)

            over_tiles(pool, body_b)

        @block.scalar
        def _(act):
            act.wait_ge(first_consts, 32)
            norm_square(A, Tile(0, 0))
            split_hi(A, 0, KT)

            def body_a(t):
                t1 = t + 1
                if t.real():
                    need(act, o_psum, 2 * t.n)
                    act.wait_ge(A.taken[1], t.n + 1)
                    nc.scalar.activation(vcat[t.par][:, :, 0:HD], raw[:, 640:768].rearrange("p (h d) -> p h d", d=HD),
                                         ACT.Copy).then_inc(v_hi, 1)
                    if t.fixed and t.n == LAST:
                        cache_hi(act)
                if t1.real():
                    split_x_hi(A, t1, 1)
                if t.fixed and t.n == -1:
                    split_hi(A, KT, 3 * KT)
                if t.real():
                    def qk_taken(n):
                        act.wait_ge(qkT_psum, 3 * t.n + n + 1)
                        src = (T[2], T[1], T[0])[n][:, :].rearrange("p (a b) -> p a b", b=P)
                        if n < 2:
                            dst = qT[:, 4 * n:4 * n + 4, :]
                        else:
                            dst = kT[:, :, :, t.par * P:(t.par + 1) * P].rearrange("p h o n -> p (h o) n")
                        nc.scalar.activation(dst, src, ACT.Copy).then_inc(qkT_taken, 1)

                    qk_taken(0)
                    qk_taken(1)
                    act.wait_ge(gate_psum, t.n + 1)
                    need(act, gate_ready, t.n)
                    nc.scalar.activation(gth[:, :], T[2][:, :], ACT.Tanh, scale=0.5).then_inc(gate_tanh, 1)
                    qk_taken(2)
                if not (t.fixed and t.n == -2):
                    when(t + 2, lambda n: norm_square(A, n))
                if t.fixed and t.n == 0:
                    split_hi(A, 3 * KT, len(A.pieces))
                if t1.real():
                    act.wait_ge(A.projected[0], t1.n + 1)
                    need(act, n_step, 5 * t1.n)
                    nc.scalar.activation(raw[:, 0:512], J[0][:, :], ACT.Copy).then_inc(A.taken[0], 1)
                def exp_scores(n):
                    act.wait_ge(s_neg, 4 * t.n + n + 1)
                    for h in (2 * n, 2 * n + 1):
                        last = nc.scalar.activation(sc[:, h, :], sc[:, h, :], ACT.Exp, bias=nmx[:, h:h + 1],
                                                    accum_out=esum[:, h:h + 1])
                    last.then_inc(s_exp, 1)

                def pT_hi(k):
                    act.wait_ge(pt_psum, 4 * t.n + k + 1)
                    nc.scalar.activation(pthi[:, k % 2, :], T[k % 3][:, :], ACT.Copy).then_inc(pt_hi, 1)

                def o_low_half(g):
                    act.wait_ge(o_psum, 2 * t.n + g + 1)
                    need(act, o_sum, 4 * t.n + 2 * g)
                    nc.scalar.activation(olo[:, :], S[g][HD:P, :], ACT.Copy).then_inc(o_low, 1)

                def y_hi_half(g):
                    act.wait_ge(y_gated, 2 * t.n + g + 1)
                    need(act, A.out_psum, 2 * t.n)
                    nc.scalar.activation(yhi[:, 2 * g:2 * g + 2, :], osum[:, 2 * g:2 * g + 2, :],
                                         ACT.Copy).then_inc(A.y_hi, 1)

                if t.real():
                    exp_scores(0)
                    exp_scores(1)
                if t1.real():
                    act.wait_ge(A.projected[1], t1.n + 1)
                    need(act, v_lo, t1.n)
                    if t1.fixed and t1.n == LAST:
                        act.wait_ge(windows_stored, 16 * 4)
                    nc.scalar.activation(raw[:, 512:768], J[1][:, 0:256], ACT.Copy).then_inc(A.taken[1], 1)
                if t.real():
                    exp_scores(2)
                    exp_scores(3)
                    act.wait_ge(s_diff, t.n + 1)
                    nc.scalar.activation(esink[:, :], sdif[:, :], ACT.Exp).then_inc(s_esink, 1)
                    pT_hi(0)
                    pT_hi(1)
                if t1.real():
                    act.wait_ge(n_step, 5 * t1.n + 5)
                    nc.scalar.activation(qcat[:, :, 0:HD], qkn[:, 0:512].rearrange("p (h d) -> p h d", d=HD),
                                         ACT.Copy).then_inc(n_hi, 1)
                    kn = qkn[:, 512:640].rearrange("p (h d) -> p h d", d=HD)
                    for o in range(2):
                        nc.scalar.activation(kcat[:, :, o, o * HD:(o + 1) * HD], kn, ACT.Copy).then_inc(n_hi, 1)
                if t.fixed and t.n == LAST:
                    split_hi(B, 0, KT)
                if t1.real():
                    act.wait_ge(A.projected[2], t1.n + 1)
                    nc.scalar.activation(agraw[:, :], J[2][:, :], ACT.Copy).then_inc(A.taken[2], 1)
                if t.real():
                    o_low_half(0)
                    pT_hi(2)
                    pT_hi(3)
                when(t + 2, lambda n: split_x_hi(A, n, 0))
                if t.real():
                    y_hi_half(0)
                    o_low_half(1)
                    y_hi_half(1)
                if t.fixed and t.n == LAST:
                    split_hi(B, KT, B_16)
                if t.fixed and t.n == TILES:
                    nc.scalar.wait_ge(A.xT_psum, 2 * TILES)
                    norm_square(B, Tile(0, 0))
                    split_hi(B, B_16, B_17)

            def cache_hi(act):
                for o in range(2):
                    nc.scalar.activation(ckcat[:, :, o, o * HD:(o + 1) * HD],
                                         ckv[:, 0, :].rearrange("p (h d) -> p h d", d=HD), ACT.Copy).then_inc(c_hi, 1)
                nc.scalar.activation(vcat[1][:, :, 0:HD], ckv[:, 1, :].rearrange("p (h d) -> p h d", d=HD),
                                     ACT.Copy).then_inc(c_hi, 1)
                act.wait_ge(c_psum, 1)
                nc.scalar.activation(kT[:, :, :, P:2 * P].rearrange("p h o n -> p (h o) n"),
                                     T[0][:, :].rearrange("p (a b) -> p a b", b=P), ACT.Copy).then_inc(c_taken, 1)

            over_tiles(act, body_a)
            act.sem_inc(pass_a_done, 1)

            act.wait_ge(pass_a_done, 4)

            def body_b(t):
                t1, p = t + 1, t + -1
                r = braw[t.par]
                if t.fixed and t.n == 0:
                    act.wait_ge(consts_b, N_CONSTS_B)
                    act.wait_ge(zeros_b, 4)
                if t.real():
                    act.wait_ge(lr_psum, t.n + 1)
                    nc.scalar.activation(glrT[:, :], T[2][0:LR + 1, 0:P], ACT.Copy).then_inc(lr_T, 1)
                if t.fixed and t.n == -1:
                    split_hi(B, 3 * KT, 4 * KT)
                if t.real():
                    act.wait_ge(uT_psum, t.n + 1)
                    nc.scalar.activation(ub[t.par][:, :, HIST:], T[2][:, 0:CD].rearrange("p (j n) -> p j n", n=P),
                                         ACT.Copy).then_inc(uT_taken, 1)
                    act.wait_ge(z_parts, 2 * t.n + 2)
                    nc.scalar.activation(ez[:, :], az[:, :], ACT.Exp).then_inc(z_exp, 1)
                    act.wait_ge(z_exp, t.n + 1)
                    nc.scalar.activation(ez[:, :], ez[:, :], ACT.Ln, bias=1.0).then_inc(z_ln, 1)
                if not (t.fixed and t.n == -2):
                    when(t + 2, lambda n: norm_square(B, n))
                if t.real():
                    need(act, go_g, t.n)
                    act.wait_ge(B.taken[3], t.n + 1)
                    act.wait_ge(B.taken[1], t.n + 1)
                    nc.scalar.activation(thg[:, :], r[:, B_GG:B_GG + 256], ACT.Tanh, scale=0.5).then_inc(th_ready, 1)
                if t1.real():
                    act.wait_ge(B.projected[1], t1.n + 1)
                    nc.scalar.activation(braw[t1.par][:, 272:784], J[0][:, :], ACT.Copy).then_inc(B.taken[1], 1)
                if t.real():
                    act.wait_ge(cum_psum, t.n + 1)
                    nc.scalar.activation(ex[:, :, :], S[1][:, :].rearrange("p (a n) -> p a n", n=P),
                                         ACT.Exp).then_inc(cum_exp, 1)
                    nc.scalar.activation(enb[:, :], S[1][:, 0:P], ACT.Exp, scale=-1.0).then_inc(cum_exp, 1)
                if p.real():
                    act.wait_ge(cnT_psum, p.n + 1)
                    for j in range(CJ):
                        nc.scalar.activation(cl[:, j, :], T[1][:, (2 + j) * P:(3 + j) * P], ACT.Identity,
                                             scale=convp[:, 1, j:j + 1], bias=convp[:, 2, j:j + 1]).then_inc(
                                                 cl_ready, 1)
                    act.wait_ge(cl_ready, 2 * p.n + 2)
                    nc.scalar.activation(cth[:, :, :], cl[:, :, :], ACT.Tanh, scale=0.5).then_inc(cth_ready, 1)
                if t.real():
                    act.wait_ge(g_psum, t.n + 1)
                    for h in range(GH):
                        rows = slice(h * GK, (h + 1) * GK)
                        nc.scalar.activation(qbd[rows, h, :], T[0][rows, 0:P], ACT.Copy)
                    nc.scalar.activation(gT[:, :], T[0][:, P:448], ACT.Copy).then_inc(g_T, 1)
                if t1.real():
                    act.wait_ge(B.projected[2], t1.n + 1)
                    nc.scalar.activation(braw[t1.par][:, 784:1296], J[1][:, :], ACT.Copy).then_inc(B.taken[2], 1)
                    act.wait_ge(B.projected[0], t1.n + 1)
                    nc.scalar.activation(glr1[:, 0:LR], J[2][:, 0:LR], ACT.Copy).then_inc(lr_taken, 1)
                    nc.scalar.activation(braw[t1.par][:, LR:272], J[2][:, LR:272], ACT.Copy).then_inc(B.taken[0], 1)
                if p.real():
                    act.wait_ge(yT_psum, p.n + 1)
                    nc.scalar.activation(yhi[:, :, :], T[1][:, :].rearrange("p (j n) -> p j n", n=P),
                                         ACT.Copy).then_inc(B.y_hi, 1)
                if t1.real():
                    act.wait_ge(B.projected[3], t1.n + 1)
                    nc.scalar.activation(braw[t1.par][:, 1296:1552], J[0][:, 0:256], ACT.Copy).then_inc(B.taken[3], 1)
                if t.real():
                    act.wait_ge(go_psum, t.n + 1)
                    nc.scalar.activation(osq[:, :], T[2][:, 0:256], ACT.Square).then_inc(go_sq, 1)
                if t1.real():
                    need(act, gates_ready, 2 * t1.n)
                    act.wait_ge(B.taken[3], t1.n + 1)
                    nc.scalar.activation(thc[:, :], braw[t1.par][:, B_CGL:B_CGL + 512], ACT.Tanh,
                                         scale=0.5).then_inc(th_ready, 1)
                when(t + 2, lambda n: split_x_hi(B, n, 0), lambda n: split_x_hi(B, n, 1))
                if t.fixed and t.n == 0:
                    split_hi(B, 4 * KT, len(B.pieces))

            over_tiles(act, body_b)

        @block.vector
        def _(dve):
            for i in range(1):
                nc.vector.memset(f(vcat[1][:, :, :]), 0.0).then_inc(zeros_a, 1)
                nc.vector.memset(f(kT[:, :, :, P:2 * P]), 0.0).then_inc(zeros_a, 1)
                nc.vector.memset(sc[:, :, P:2 * P], NEG).then_inc(zeros_a, 1)
            dve.wait_ge(first_consts, 32)
            norm_scale(A, Tile(0, 0))
            split_lo(A, 0, KT)
            heads = lambda b: b.rearrange("p (h d) -> p h d", d=HD)

            def body_a(t):
                t1, t2 = t + 1, t + 2

                def scores_max(n):
                    for e in range(2):
                        h = 2 * n + e
                        cols = slice(0, P) if t.fixed and t.n == 0 else slice(0, 2 * P)
                        b0 = 0 if t.par else P
                        nc.vector.tensor_tensor_reduce(
                            out=sc[:, h, cols], in0=S[n % 2][:, e * 256:(e + 1) * 256][:, cols],
                            in1=bias[:, h, b0:b0 + 256][:, cols], scale=1.0, scalar=sinks[:, h:h + 1],
                            op0=ALU.add, op1=ALU.max, accum_out=mx[:, h:h + 1]).then_inc(s_max, 1)

                def scores_neg(n):
                    nc.vector.tensor_scalar(nmx[:, 2 * n:2 * n + 2], mx[:, 2 * n:2 * n + 2], -1.0, None,
                                            ALU.mult).then_inc(s_neg, 1)

                if t.real():
                    dve.wait_ge(v_hi, t.n + 1)
                    nc.vector.tensor_tensor(vcat[t.par][:, :, HD:P], raw[:, 640:768].rearrange("p (h d) -> p h d", d=HD),
                                            f(vcat[t.par][:, :, 0:HD]), ALU.subtract).then_inc(v_lo, 1)
                    if t.fixed and t.n == LAST:
                        dve.wait_ge(c_hi, 3)
                        for o in range(2):
                            nc.vector.tensor_tensor(ckcat[:, :, o, (1 - o) * HD:(2 - o) * HD],
                                                    ckv[:, 0, :].rearrange("p (h d) -> p h d", d=HD),
                                                    f(ckcat[:, :, o, o * HD:(o + 1) * HD]), ALU.subtract).then_inc(c_lo, 1)
                        nc.vector.tensor_tensor(vcat[1][:, :, HD:P], ckv[:, 1, :].rearrange("p (h d) -> p h d", d=HD),
                                                f(vcat[1][:, :, 0:HD]), ALU.subtract).then_inc(c_lo, 1)
                if t1.real():
                    split_x_lo(A, t1, 1)
                if t.fixed and t.n == -1:
                    split_lo(A, KT, 3 * KT)
                    dve.wait_ge(consts_a, N_CONSTS_A)
                if t.real():
                    need(dve, pt_psum, 4 * t.n)
                    dve.wait_ge(s_psum, 4 * t.n + 1)
                    dve.wait_ge(gate_tanh, t.n + 1)
                    nc.vector.scalar_tensor_tensor(gth[:, :], gth[:, :], 1.0, T[2][:, :], ALU.add,
                                                   ALU.mult).then_inc(gate_ready, 1)
                    scores_max(0)
                    dve.wait_ge(s_max, 8 * t.n + 2)
                    dve.wait_ge(s_psum, 4 * t.n + 2)
                    scores_neg(0)
                    scores_max(1)
                    dve.wait_ge(s_max, 8 * t.n + 4)
                    scores_neg(1)
                if not (t.fixed and t.n == -2) and t2.real():
                    dve.wait_ge(A.x_rinv, t2.n + 1)
                    need(dve, s_psum, 4 * t.n + 3)
                    norm_scale(A, t2)
                if t.real():
                    if not t2.real():
                        dve.wait_ge(s_psum, 4 * t.n + 3)
                    scores_max(2)
                    dve.wait_ge(s_max, 8 * t.n + 6)
                    dve.wait_ge(s_psum, 4 * t.n + 4)
                    scores_neg(2)
                    scores_max(3)
                    dve.wait_ge(s_max, 8 * t.n + 8)
                    scores_neg(3)
                    dve.wait_ge(s_neg, 4 * t.n + 4)
                    nc.vector.tensor_tensor(sdif[:, :], sinks[:, :], nmx[:, :], ALU.add).then_inc(s_diff, 1)
                if t.fixed and t.n == 0:
                    split_lo(A, 3 * KT, len(A.pieces))
                if t1.real():
                    dve.wait_ge(A.taken[1], t1.n + 1)
                    if t1.fixed and t1.n == LAST:
                        dve.wait_ge(windows_stored, 16 * 4)
                    nc.vector.tensor_tensor(qkn[:, :], raw[:, 0:640], raw[:, 0:640], ALU.mult).then_inc(n_step, 1)
                    dve.wait_ge(n_step, 5 * t1.n + 1)
                    nc.vector.tensor_reduce(qss[:, :], qkn[:, :].rearrange("p (h d) -> p h d", d=HD), AX.X,
                                            ALU.add).then_inc(n_step, 1)
                if t.real():
                    dve.wait_ge(s_exp, 4 * t.n + 4)
                    dve.wait_ge(s_esink, t.n + 1)
                    nc.vector.tensor_tensor(den[:, :], esum[:, :], esink[:, :], ALU.add).then_inc(s_den, 1)
                    dve.wait_ge(s_den, t.n + 1)
                    nc.vector.reciprocal(rden[:, :], den[:, :]).then_inc(s_rden, 1)
                    dve.wait_ge(s_rden, t.n + 1)
                    for h in range(HEADS):
                        nc.vector.tensor_scalar(sc[:, h, :], sc[:, h, :], rden[:, h:h + 1], None,
                                                ALU.mult).then_inc(p_ready, 1)
                if t1.real():
                    dve.wait_ge(n_rinv, t1.n + 1)
                    nc.vector.tensor_tensor(heads(qkn[:, :]), heads(raw[:, 0:640]),
                                            qr[:, :].unsqueeze(2).to_broadcast([P, 10, HD]),
                                            ALU.mult).then_inc(n_step, 1)
                    dve.wait_ge(n_step, 5 * t1.n + 3)
                    nc.vector.scalar_tensor_tensor(heads(qkn[:, 0:512]), heads(qkn[:, 0:512]), 1.0,
                                                   qkgain[:, 0, :].unsqueeze(1).to_broadcast([P, HEADS, HD]),
                                                   ALU.mult, ALU.mult).then_inc(n_step, 1)
                    nc.vector.scalar_tensor_tensor(heads(qkn[:, 512:640]), heads(qkn[:, 512:640]), HD ** 0.5,
                                                   qkgain[:, 1, :].unsqueeze(1).to_broadcast([P, KVH, HD]),
                                                   ALU.mult, ALU.mult).then_inc(n_step, 1)
                if t.fixed and t.n == LAST:
                    split_lo(B, 0, KT)

                def pT_lo(k):
                    dve.wait_ge(pt_hi, 4 * t.n + k + 1)
                    nc.vector.tensor_tensor(ptlo[:, k % 2, :], T[k % 3][:, :], f(pthi[:, k % 2, :]),
                                            ALU.subtract).then_inc(pt_lo, 1)

                def y_half(g):
                    dve.wait_ge(o_low, 2 * t.n + g + 1)
                    for e in range(2):
                        pick = lambda b: b.rearrange("p (j e n) -> p j e n", e=2, n=P)[:, :, e, :]
                        nc.vector.tensor_tensor(osum[e * HD:(e + 1) * HD, 2 * g:2 * g + 2, :],
                                                pick(S[g][0:HD, :]), pick(olo[:, :]), ALU.add).then_inc(o_sum, 1)
                    dve.wait_ge(o_sum, 4 * t.n + 2 * g + 2)
                    nc.vector.scalar_tensor_tensor(osum[:, 2 * g:2 * g + 2, :], osum[:, 2 * g:2 * g + 2, :], 0.5,
                                                   gth[:, 256 * g:256 * g + 256].rearrange("p (j n) -> p j n", n=P),
                                                   ALU.mult, ALU.mult).then_inc(y_gated, 1)

                def y_lo_half(g):
                    dve.wait_ge(A.y_hi, 2 * t.n + g + 1)
                    nc.vector.tensor_tensor(ylo[:, 2 * g:2 * g + 2, :], osum[:, 2 * g:2 * g + 2, :],
                                            f(yhi[:, 2 * g:2 * g + 2, :]), ALU.subtract).then_inc(A.y_lo, 1)

                if t.real():
                    pT_lo(0)
                    pT_lo(1)
                if t1.real():
                    dve.wait_ge(n_hi, 3 * t1.n + 3)
                    nc.vector.tensor_tensor(qcat[:, :, HD:P], heads(qkn[:, 0:512]), f(qcat[:, :, 0:HD]),
                                            ALU.subtract).then_inc(n_lo, 1)
                    for o in range(2):
                        nc.vector.tensor_tensor(kcat[:, :, o, (1 - o) * HD:(2 - o) * HD], heads(qkn[:, 512:640]),
                                                f(kcat[:, :, o, o * HD:(o + 1) * HD]), ALU.subtract).then_inc(n_lo, 1)
                if (t + -1).real():
                    add_out(A, t + -1, 0, J[0])
                if t.real():
                    y_half(0)
                    pT_lo(2)
                    pT_lo(3)
                when(t + 2, lambda n: split_x_lo(A, n, 0))
                if (t + -1).real():
                    add_out(A, t + -1, 1, J[1])
                if t.real():
                    y_lo_half(0)
                    y_half(1)
                    y_lo_half(1)
                if t.fixed and t.n == LAST:
                    split_lo(B, KT, B_16)
                if t.fixed and t.n == TILES:
                    norm_scale(B, Tile(0, 0))
                    split_lo(B, B_16, B_17)

            over_tiles(dve, body_a)
            dve.sem_inc(pass_a_done, 1)

            dve.wait_ge(pass_a_done, 4)

            def body_b(t):
                t1, p = t + 1, t + -1
                r = braw[t.par]
                st = sts if t.fixed and t.n == LAST else stp
                if t.fixed and t.n == -1:
                    split_lo(B, 3 * KT, 4 * KT)
                if t.fixed and t.n == 0:
                    dve.wait_ge(consts_b, N_CONSTS_B)
                    dve.wait_ge(zeros_b, 4)
                if t.real():
                    dve.wait_ge(z_psum, t.n + 1)
                    nc.vector.tensor_scalar(zm[:, :], S[0][:, 0:P], 0.0, None, ALU.min).then_inc(z_parts, 1)
                    dve.wait_ge(z_parts, 2 * t.n + 1)
                    nc.vector.scalar_tensor_tensor(az[:, :], zm[:, :], 2.0, S[0][:, 0:P], ALU.mult,
                                                   ALU.subtract).then_inc(z_parts, 1)
                if p.real():
                    dve.wait_ge(cT_psum, p.n + 1)
                    nc.vector.bn_stats(bst[:, :], S[0][:, 256:512]).then_inc(bn_step, 1)
                    dve.wait_ge(bn_step, 2 * p.n + 1)
                if t.real():
                    if t.fixed and t.n == LAST:
                        nc.vector.tensor_copy(ub[t.par][:, :, 0:HIST], uh[:, :, :]).then_inc(hist_ready, 1)
                    elif t.fixed and t.n == 0:
                        nc.vector.memset(ub[t.par][:, :, 0:HIST], 0.0).then_inc(hist_ready, 1)
                    else:
                        nc.vector.tensor_copy(ub[t.par][:, :, 0:HIST], ub[1 - t.par][:, :, P:P + HIST]).then_inc(
                            hist_ready, 1)
                if p.real():
                    nc.vector.bn_aggr(mv[:, :], bst[:, :]).then_inc(bn_step, 1)
                if t.real():
                    dve.wait_ge(uT_taken, t.n + 1)
                    dve.wait_ge(hist_ready, t.n + 1)
                    conv(t, 0, 6)
                    dve.wait_ge(z_ln, t.n + 1)
                    nc.vector.tensor_tensor(zm[:, :], zm[:, :], ez[:, :], ALU.subtract).then_inc(la_ready, 1)
                if p.real():
                    dve.wait_ge(ln_r, p.n + 1)
                    nc.vector.tensor_scalar(cn[:, :], S[0][:, 256:512], mv[:, 0:1], rs[:, :], ALU.subtract,
                                            ALU.mult).then_inc(cn_ready, 1)
                if t.real():
                    conv(t, 6, 20)
                    dve.wait_ge(cum_exp, 2 * t.n + 2)
                    scale = GK ** -0.5
                    q, k = r[:, B_Q:B_Q + P], r[:, B_K:B_K + P]
                    nc.vector.scalar_tensor_tensor(qt[:, :], q, scale, ex[:, 0, :], ALU.mult, ALU.mult).then_inc(
                        qk_scaled, 1)
                    nc.vector.scalar_tensor_tensor(qf[:, :], q, scale, ex[:, 1, :], ALU.mult, ALU.mult).then_inc(
                        qk_scaled, 1)
                    nc.vector.tensor_tensor(kend[:, :], k, ex[:, 2, :], ALU.mult).then_inc(qk_scaled, 1)
                    nc.vector.tensor_tensor(kk[0:64, :], k[0:64], ex[0:64, 3, :], ALU.mult).then_inc(qk_scaled, 1)
                    nc.vector.tensor_tensor(kk[64:P, :], k[64:P], enb[64:P, :], ALU.mult).then_inc(qk_scaled, 1)
                    nc.vector.tensor_tensor(kt0[:, :], k[0:64], enb[0:64, :], ALU.mult).then_inc(qk_scaled, 1)
                if not (t.fixed and t.n == -2):
                    when(t + 2, lambda n: norm_scale(B, n))
                if p.real():
                    dve.wait_ge(cth_ready, p.n + 1)
                    nc.vector.scalar_tensor_tensor(cth[:, :, :], cth[:, :, :], 1.0, cl[:, :, :], ALU.add,
                                                   ALU.mult).then_inc(cs_ready, 1)
                if t.real():
                    conv(t, 20, 46)
                if p.real():
                    dve.wait_ge(pw_psum, p.n + 1)
                    nc.vector.scalar_tensor_tensor(yb[:, 256:512], T[0][:, 0:CD], 0.5, bpw[:, :], ALU.mult,
                                                   ALU.add).then_inc(c2_ready, 1)
                    dve.wait_ge(c2_ready, p.n + 1)
                    nc.vector.scalar_tensor_tensor(yb[:, 256:512], yb[:, 256:512], 0.5, gc[:, :], ALU.mult,
                                                   ALU.mult).then_inc(yc_ready, 1)
                if t.real():
                    dve.wait_ge(g_dec, t.n + 1)
                    col = DEC - 1 if t.fixed and t.n == LAST else P - 1
                    dve.wait_ge(a_psum, t.n + 1)
                    nc.vector.tensor_copy(dec[:, :], T[1][:, col:col + 1]).then_inc(dec_ready, 1)
                    nc.vector.copy_predicated(asb[0:64, 0:256], mask[0:64, 0:256], S[0][0:64, 0:256]).then_inc(
                        a_masked, 1)
                    nc.vector.copy_predicated(asb[:, 256:512], mask[:, 256:512], S[0][:, 256:512]).then_inc(a_masked, 1)
                    dve.wait_ge(th_ready, 2 * t.n + 2)
                    nc.vector.scalar_tensor_tensor(thg[:, :], thg[:, :], 1.0, r[:, B_GG:B_GG + 256], ALU.add,
                                                   ALU.mult).then_inc(gates_ready, 1)
                    need(dve, yc_ready, t.n)
                    nc.vector.scalar_tensor_tensor(gc[:, :], thc[:, 256:512], 1.0, r[:, B_CG:B_CG + 256], ALU.add,
                                                   ALU.mult).then_inc(gates_ready, 1)
                if p.real():
                    dve.wait_ge(B.y_hi, p.n + 1)
                    nc.vector.tensor_tensor(ylo[:, :, :], T[1][:, :].rearrange("p (j n) -> p j n", n=P),
                                            f(yhi[:, :, :]), ALU.subtract).then_inc(B.y_lo, 1)
                if t.real():
                    conv(t, 46, 2 * CW)
                    dve.wait_ge(go_psum, t.n + 1)
                    dve.wait_ge(dec_ready, t.n + 1)
                    for h in range(GH):
                        rows, cols = slice(h * GK, (h + 1) * GK), slice(h * GV, (h + 1) * GV)
                        last = nc.vector.scalar_tensor_tensor(st[rows, cols], st[rows, cols], dec[rows, :],
                                                              S[1][rows, cols], ALU.mult, ALU.add)
                    last.then_inc(g_state, 1)
                    dve.wait_ge(go_sq, t.n + 1)
                    nc.vector.tensor_reduce(oss[:, :], osq[:, :].rearrange("p (h d) -> p h d", d=GV), AX.X,
                                            ALU.add).then_inc(go_ss, 1)
                if t1.real():
                    dve.wait_ge(th_ready, 2 * t1.n + 1)
                    nc.vector.tensor_scalar(thc[:, 0:256], thc[:, 0:256], 0.5, 0.5, ALU.mult, ALU.add).then_inc(sg_ready, 1)
                    dve.wait_ge(sg_ready, t1.n + 1)
                    if t1.fixed and t1.n == LAST:
                        dve.wait_ge(u_stored, 16)
                    nc.vector.tensor_tensor(u[:, :], braw[t1.par][:, B_CV:B_CV + 256], thc[:, 0:256], ALU.mult).then_inc(
                        u_ready, 1)
                if p.real():
                    add_out(B, p, 0, J[1])
                if t.real():
                    dve.wait_ge(go_r, t.n + 1)
                    need(dve, yT_psum, t.n)
                    gv = lambda b: b.rearrange("p (h d) -> p h d", d=GV)
                    nc.vector.tensor_tensor(gv(yb[:, 0:256]), gv(T[2][:, 0:256]),
                                            orr[:, :].unsqueeze(2).to_broadcast([P, GH, GV]),
                                            ALU.mult).then_inc(go_n, 1)
                    dve.wait_ge(go_n, 2 * t.n + 1)
                    nc.vector.scalar_tensor_tensor(gv(yb[:, 0:256]), gv(yb[:, 0:256]), 0.5 * GV ** 0.5,
                                                   glagain[:, :].unsqueeze(1).to_broadcast([P, GH, GV]),
                                                   ALU.mult, ALU.mult).then_inc(go_n, 1)
                    dve.wait_ge(go_n, 2 * t.n + 2)
                    nc.vector.tensor_tensor(yb[:, 0:256], yb[:, 0:256], thg[:, :], ALU.mult).then_inc(go_g, 1)
                when(t + 2, lambda n: split_x_lo(B, n, 0), lambda n: split_x_lo(B, n, 1))
                if p.real():
                    add_out(B, p, 1, J[2])
                if t.fixed and t.n == 0:
                    split_lo(B, 4 * KT, len(B.pieces))

            def conv(t, a, b):
                for n in range(a, b):
                    tap, j = n // CJ, n % CJ
                    src = ub[t.par][:, j, tap:tap + P]
                    w = convw[:, j, tap:tap + 1]
                    if tap == 0:
                        nc.vector.tensor_scalar(acc[:, j, :], src, w, convp[:, 0, j:j + 1], ALU.mult,
                                                ALU.add).then_inc(conv_step, 1)
                    else:
                        dve.wait_ge(conv_step, 2 * CW * t.n + n - 1)
                        nc.vector.scalar_tensor_tensor(acc[:, j, :], src, w, acc[:, j, :], ALU.mult,
                                                       ALU.add).then_inc(conv_step, 1)

            over_tiles(dve, body_b)

        @block.tensor
        def _(pe):
            pe.wait_ge(first_consts, 32)

            def body_a(t):
                t1 = t + 1
                if t.fixed and t.n == 0:
                    pe.wait_ge(zeros_a, 3)
                if t1.real():
                    need(pe, pt_lo, 4 * t.n)
                    transpose_x(A, t1, 1)
                if t.real():
                    if t.fixed and t.n == LAST:
                        pe.wait_ge(c_lo, 3)
                        pe.wait_ge(pt_lo, 4 * t.n)
                        for j in range(4):
                            last = nc.tensor.transpose(T[0][:, j * P:(j + 1) * P], f(ckcat[:, j // 2, j % 2, :]),
                                                       ident[:, :])
                        last.then_inc(c_psum, 1)
                        pe.wait_ge(c_taken, 1)
                    pe.wait_ge(n_lo, 3 * t.n + 3)
                    need(pe, pt_lo, 4 * t.n)
                    for n, (bank, h0) in enumerate(((T[2], 0), (T[1], 4))):
                        if n == 1 and t1.real():
                            pe.wait_ge(A.xT_lo, 2 * t1.n + 1)
                        for j in range(4):
                            last = nc.tensor.transpose(bank[:, j * P:(j + 1) * P], f(qcat[:, h0 + j, :]), ident[:, :])
                        last.then_inc(qkT_psum, 1)
                    pe.wait_ge(qkT_taken, 3 * t.n + 1)
                    for j in range(4):
                        last = nc.tensor.transpose(T[2][:, j * P:(j + 1) * P], agraw[:, j * P:(j + 1) * P],
                                                   ident[:, :])
                    last.then_inc(gate_psum, 1)
                    if t1.real():
                        pe.wait_ge(A.xT_lo, 2 * t1.n + 2)
                    for j in range(4):
                        last = nc.tensor.transpose(T[0][:, j * P:(j + 1) * P], f(kcat[:, j // 2, j % 2, :]),
                                                   ident[:, :])
                    last.then_inc(qkT_psum, 1)
                if t1.real():
                    need(pe, A.out_added, 2 * t.n - 2)
                    project(A, t1, 0, J[0])

                def scores(n):
                    if n < 2:
                        need(pe, o_sum, 4 * t.n)
                    else:
                        pe.wait_ge(s_max, 8 * t.n + 2 * (n - 1))
                    for e in range(2):
                        h = 2 * n + e
                        for o in range(2):
                            last = nc.tensor.matmul(S[n % 2][:, e * 256:(e + 1) * 256], qT[:, h, :],
                                                    kT[:, h // GROUP, o, :], start=(o == 0), stop=(o == 1))
                    last.then_inc(s_psum, 1)

                if t.real():
                    pe.wait_ge(qkT_taken, 3 * t.n + 3)
                    scores(0)
                    scores(1)
                if t1.real():
                    need(pe, A.out_added, 2 * t.n - 2)
                    project(A, t1, 1, J[1])
                if t.real():
                    scores(2)
                    scores(3)
                if t1.real():
                    need(pe, A.taken[2], t1.n)
                    project(A, t1, 2, J[2])

                def pT(g, n):
                    bank = T[(2 * g + n) % 3]
                    k = 2 * g + n
                    if k == 2:
                        pe.wait_ge(gate_ready, t.n + 1)
                    if k == 3:
                        pe.wait_ge(pt_lo, 4 * t.n + 1)
                    for j in range(GROUP):
                        pe.wait_ge(p_ready, 8 * t.n + GROUP * g + j + 1)
                        last = nc.tensor.transpose(bank[:, j * P:(j + 1) * P],
                                                   sc[:, GROUP * g + j, n * P:(n + 1) * P], ident[:, :])
                    last.then_inc(pt_psum, 1)

                def pv(g):
                    pe.wait_ge(pt_lo, 4 * t.n + 2 * g + 2)
                    if g == 0:
                        pe.wait_ge(v_lo, t.n + 1)
                    for n in range(2):
                        for m, pt in enumerate((pthi, ptlo)):
                            last = nc.tensor.matmul(S[g][:, :], vcat[n][:, g, :], pt[:, n, :],
                                                    start=(n == 0 and m == 0), stop=(n == 1 and m == 1))
                    last.then_inc(o_psum, 1)

                def out(h):
                    if (t + -1).real():
                        if t1.real():
                            pe.wait_ge(A.taken[h], t1.n + 1)
                        elif h == 0 and not t1.real():
                            need(pe, A.out_added, 2 * t.n - 2)
                        output(A, t + -1, h, J[h])

                if t.real():
                    pT(0, 0)
                    pT(0, 1)
                out(0)
                if t.real():
                    pv(0)
                    pT(1, 0)
                    pT(1, 1)
                when(t + 2, lambda n: transpose_x(A, n, 0))
                out(1)
                if t.real():
                    pv(1)

            over_tiles(pe, body_a)
            pe.sem_inc(pass_a_done, 1)

            pe.wait_ge(pass_a_done, 4)

            def body_b(t):
                t1, p = t + 1, t + -1
                r = braw[t.par]
                st = sts if t.fixed and t.n == LAST else stp
                if t.fixed and t.n == 0:
                    pe.wait_ge(consts_b, N_CONSTS_B)
                    pe.wait_ge(zeros_b, 4)
                if p.real():
                    pe.wait_ge(conv_step, 2 * CW * t.n)
                    pe.wait_ge(a_masked, 2 * t.n)
                    for j in range(CJ):
                        last = nc.tensor.transpose(S[0][:, (2 + j) * P:(3 + j) * P], acc[:, j, :], ident[:, :])
                    last.then_inc(cT_psum, 1)
                if t.real():
                    pe.wait_ge(lr_taken, t.n + 1)
                    need(pe, go_n, 2 * t.n)
                    nc.tensor.transpose(T[2][0:LR + 1, 0:P], glr1[:, :], ident[:, :]).then_inc(lr_psum, 1)
                if t.real():
                    pe.wait_ge(lr_T, t.n + 1)
                    nc.tensor.matmul(S[0][:, 0:P], glrT[:, :], wup[:, :], start=True, stop=True).then_inc(z_psum, 1)
                    pe.wait_ge(u_ready, t.n + 1)
                    for j in range(CJ):
                        last = nc.tensor.transpose(T[2][:, j * P:(j + 1) * P], u[:, j * P:(j + 1) * P], ident[:, :])
                    last.then_inc(uT_psum, 1)
                if t1.real():
                    need(pe, B.taken[3], t1.n)
                    project(B, t1, 1, J[0])
                if t.real():
                    pe.wait_ge(la_ready, t.n + 1)
                    need(pe, g_state, t.n)
                    for n in range(4):
                        rows = slice(0, DEC) if n == 2 and t.fixed and t.n == LAST else slice(0, P)
                        last = nc.tensor.matmul(S[1][:, n * P:(n + 1) * P], tri[rows, n, :], zm[rows, :], start=True,
                                                stop=True)
                    last.then_inc(cum_psum, 1)
                if p.real():
                    pe.wait_ge(cn_ready, p.n + 1)
                    for j in range(CJ):
                        last = nc.tensor.transpose(T[1][:, (2 + j) * P:(3 + j) * P], cn[:, j * P:(j + 1) * P],
                                                   ident[:, :])
                    last.then_inc(cnT_psum, 1)
                if t1.real():
                    need(pe, B.out_added, 2 * p.n - 1)
                    project(B, t1, 2, J[1])
                if t.real():
                    pe.wait_ge(qk_scaled, 6 * t.n + 6)
                    pe.wait_ge(uT_taken, t.n + 1)
                    if t1.real():
                        pe.wait_ge(B.xT_lo, 2 * t1.n + 2)
                    nc.tensor.transpose(T[0][:, 0:P], qt[:, :], ident[:, :])
                    nc.tensor.transpose(T[0][:, P:2 * P], qf[:, :], ident[:, :])
                    nc.tensor.transpose(T[0][:, 2 * P:3 * P], kk[:, :], ident[:, :])
                    nc.tensor.transpose(T[0][:, 3 * P:3 * P + 64], kt0[:, :], ident[0:64, 0:64]).then_inc(g_psum, 1)
                    if p.real():
                        pe.wait_ge(cl_ready, 2 * p.n + 2)
                    nc.tensor.transpose(T[1][:, 0:P], ex[:, 1, :], ident[:, :]).then_inc(g_dec, 1)
                if t1.real():
                    need(pe, B.out_added, 2 * p.n)
                    project(B, t1, 0, J[2])
                if p.real():
                    if t.real():
                        pe.wait_ge(g_T, t.n + 1)
                    pe.wait_ge(cs_ready, p.n + 1)
                    for j in range(CJ):
                        last = nc.tensor.matmul(T[0][:, 0:CD], cth[:, j, :], wpw[:, j, :], start=(j == 0),
                                                stop=(j == CJ - 1))
                    last.then_inc(pw_psum, 1)
                if t.real():
                    qfT, kkT, ktT = gT[:, 0:P], gT[:, P:2 * P], gT[:, 2 * P:2 * P + 64]
                    pe.wait_ge(g_T, t.n + 1)
                    nc.tensor.matmul(S[0][0:64, 0:256].rearrange("p (h n) -> p h n", n=64), ktT, qbd[:, :, 0:64],
                                     start=True, stop=True)
                    nc.tensor.matmul(S[0][:, 256:512].rearrange("p (h n) -> p h n", n=64), kkT, qbd[:, :, 64:P],
                                     start=True, stop=True).then_inc(a_psum, 1)
                    rows = slice(0, DEC) if t.fixed and t.n == LAST else slice(0, P)
                    pe.wait_ge(cum_exp, 2 * t.n + 2)
                    pe.wait_ge(B.taken[1], t.n + 1)
                    nc.tensor.matmul(S[1][:, 0:256], kend[rows, :], r[rows, B_V:B_V + 256], start=True,
                                     stop=True).then_inc(su_psum, 1)
                if p.real():
                    if t.real():
                        pe.wait_ge(dec_ready, t.n + 1)
                    pe.wait_ge(go_g, p.n + 1)
                    pe.wait_ge(yc_ready, p.n + 1)
                    for j in range(4):
                        last = nc.tensor.transpose(T[1][:, j * P:(j + 1) * P], yb[:, j * P:(j + 1) * P], ident[:, :])
                    last.then_inc(yT_psum, 1)
                if t1.real():
                    pe.wait_ge(B.taken[1], t1.n + 1)
                    project(B, t1, 3, J[0])
                if t.real():
                    pe.wait_ge(a_masked, 2 * t.n + 2)
                    nc.tensor.matmul(T[2][:, 0:256], qfT, st[:, :], start=True, stop=False, skip_group_check=True)
                    for c in range(2):
                        for h in range(GH):
                            rows = slice(0, 64) if c == 0 else slice(0, P)
                            last = nc.tensor.matmul(T[2][64 * c:64 * c + 64, h * GV:(h + 1) * GV],
                                                    asb[rows, 256 * c + 64 * h:256 * c + 64 * h + 64],
                                                    r[rows, B_V + h * GV:B_V + (h + 1) * GV], start=False,
                                                    stop=(c == 1 and h == GH - 1), skip_group_check=True)
                    last.then_inc(go_psum, 1)
                def out(h):
                    if p.real():
                        if t1.real():
                            pe.wait_ge(B.taken[2 - 2 * h], t1.n + 1)
                        else:
                            need(pe, B.out_added, 2 * p.n - 1 + h)
                        output(B, p, h, J[1 + h])

                out(0)
                if (t + 2).real():
                    if t.real():
                        need(pe, B.y_lo, t.n)
                        pe.wait_ge(dec_ready, t.n + 1)
                    transpose_x(B, t + 2, 0)
                    transpose_x(B, t + 2, 1)
                out(1)

            over_tiles(pe, body_b)


def shape_constants():
    q = np.arange(P)[:, None]
    key = np.concatenate([np.arange(-P, P), np.arange(-P, 0)])[None, :]
    seen = np.where(q < CHUNK, (key >= -P) & (key < CHUNK), (key >= -CHUNK) & (key < P))
    slopes = 2.0 ** (-8.0 * np.arange(1, HEADS + 1) / HEADS)
    bias = np.where(seen[:, None, :], -slopes[None, :, None] * np.abs(q - key)[:, None, :], NEG).astype(np.float32)
    bias = (bias.view(np.uint32) >> 16).astype(np.uint16)
    ident = np.eye(P, dtype=np.float32)
    s, t = np.arange(P)[:, None], np.arange(P)[None, :]
    same = (s // CHUNK) == (t // CHUNK)
    tri = np.stack([(s <= t) & same, s <= t, s > t, (s > t) & same], 1).astype(np.float32) / 16.0
    tt = np.arange(64)[None, None, :]
    m0 = (s[:, :, None] < 64) & (s[:, :, None] <= tt)
    m1 = s[:, :, None] <= 64 + tt
    mask = np.concatenate([np.broadcast_to(m, (P, GH, 64)).reshape(P, 256) for m in (m0, m1)], 1).astype(np.float32)
    return bias, ident, tri, mask


def kernel(**inputs):
    import concourse.bacc as bacc
    from concourse.bass_utils import run_bass_kernel_spmd

    nc = bacc.Bacc("TRN2", target_bir_lowering=False, num_devices=1, dynamic_dma_scratch_size=1024)
    arrays, ins, consts = {}, [], []
    for name in INS:
        a = np.ascontiguousarray(inputs[name])
        arrays[f"in_{name}"] = a
        ins.append(nc.dram_tensor(f"in_{name}", a.shape, mybir.dt.from_np(a.dtype), kind="ExternalInput").ap())
    for n, a in enumerate(shape_constants()):
        a = np.ascontiguousarray(a)
        arrays[f"const_{n}"] = a
        consts.append(nc.dram_tensor(f"const_{n}", a.shape, mybir.dt.from_np(a.dtype), kind="ExternalInput").ap())
    outs = [nc.dram_tensor(f"out_{n}", shape, F32, kind="ExternalOutput").ap() for n, shape in enumerate(OUTS)]
    build(nc, ins, consts, outs)
    r = run_bass_kernel_spmd(nc, [arrays], core_ids=[0])
    return tuple(r.results[0][f"out_{n}"] for n in range(len(OUTS)))
```

```python
from contextlib import ExitStack

import numpy as np

import concourse.bass as bass
from concourse import mybir

ALU = mybir.AluOpType
ACT = mybir.ActivationFunctionType
AX = mybir.AxisListType
F32 = mybir.dt.float32
F32R = mybir.dt.float32r
BF16 = mybir.dt.bfloat16
U16 = mybir.dt.uint16
U32 = mybir.dt.uint32

P = 128
D = 1024
KT = D // P
SEQ = 2048
DEC = 64
CHUNK = 64
TILES = SEQ // P + 1
LAST = TILES - 1
HEADS, KVH, HD = 8, 2, 64
GROUP = HEADS // KVH
GH, GK, GV, LR = 4, 32, 64, 16
CW = 31
HIST = CW - 1
CD = 256
CJ = CD // P
EPS = 1e-6
NEG = -1e30
ATT = HEADS * HD

AQ, AKV, AG = (0, 512), (512, 256), (768, 512)
GQK, GVC, GGC, GLR = (1280, 256), (1536, 256), (1792, 256), (2048, 16)
CV, CGL, CG = (2064, 256), (2320, 256), (2576, 256)
CHUNKS_A = [[AQ], [AKV], [AG]]
CHUNKS_B = [[GLR, GQK], [GVC, GGC], [CV, CGL], [CG]]
WIDTH_A = [sum(w for _, w in c) for c in CHUNKS_A]
WIDTH_B = [sum(w for _, w in c) for c in CHUNKS_B]
B_GLR, B_Q, B_K, B_V, B_GG, B_CV, B_CGL, B_CG = 0, 16, 144, 272, 528, 784, 1040, 1296
B_COLS = sum(WIDTH_B)
STAGES = 4
P_DVE, P_ACT = (0, 1, 2, 4, 6), (3, 5, 7)

INS = ["x_prompt", "x_sample", "cache_k", "cache_v", "state_gla", "state_conv", "norm_gain", "w_in",
       "q_norm_gain", "k_norm_gain", "attn_sinks", "gla_w_gate_up", "gla_b_gate", "gla_norm_gain",
       "conv_w", "conv_b", "conv_ln_gain", "conv_ln_bias", "conv_w_pw", "conv_b_pw", "w_out"]
OUTS = [(1, SEQ, D), (1, DEC, D), (1, 1, P, KVH, HD), (1, 1, P, KVH, HD), (1, 1, GH, GK, GV), (1, 1, HIST, CD),
        (1, 1, P, KVH, HD), (1, 1, P, KVH, HD), (1, 1, GH, GK, GV), (1, 1, HIST, CD)]


class Tile:

    def __init__(self, i, c):
        self.i, self.c = i, c
        self.par = c % 2
        self.n = 2 * i + c
        self.half = i + c // 2
        self.fixed = isinstance(self.n, int)

    def __add__(self, k):
        return Tile(self.i, self.c + k)

    def real(self):
        return not self.fixed or 0 <= self.n < TILES


def need(eng, sem, count):
    if isinstance(count, int) and count <= 0:
        return
    eng.wait_ge(sem, count)


def pieces_of(chunks, order):
    out = []
    widths = [sum(w for _, w in c) for c in chunks]
    for n in order:
        for k in range(KT):
            col = (k * widths[n],) if n == 3 else KT * sum(widths[:n]) + k * widths[n]
            out.append(("in", k, chunks[n], col, widths[n]))
    for k in range(4):
        for h in range(2):
            out.append(("out", k, h, W_OUT + k * D + h * 512, 512))
    return out


W_OUT = KT * sum(WIDTH_B[:3])
W_COLS = W_OUT + 4 * D


def build(nc, ins, consts, outs):
    io = dict(zip(INS, ins))
    bias_d, ident_d, tri_d, mask_d = consts
    yp, ys, pk_o, pv_o, ps_o, pc_o, sk_o, sv_o, ss_o, sc_o = outs
    es = ExitStack()

    def sb(name, shape, dt=F32, ctx=es):
        return ctx.enter_context(nc.sbuf_tensor(name, shape, dt))

    def sem(name):
        return es.enter_context(nc.semaphore(name))

    with es:
        whi = sb("whi", [P, W_COLS], F32R)
        wlo = sb("wlo", [P, W_COLS], F32R)
        wraw = sb("wraw", [P, STAGES, 512])
        ident = sb("ident", [P, P])
        gain = sb("gain", [P, KT])
        mhalf = sb("mhalf", [P, 16])
        eps_d = sb("eps_d", [P, 1])
        eps_h = sb("eps_h", [P, 16])
        eps_1 = sb("eps_1", [P, 1])
        root_d = sb("root_d", [P, 1])
        rscale = sb("rscale", [P, 1])
        xin = [sb(f"xin{i}", [P, D]) for i in range(2)]
        xn = sb("xn", [P, D])
        xhi = sb("xhi", [P, KT, P], F32R)
        xlo = sb("xlo", [P, KT, P], F32R)
        res = [sb(f"res{i}", [P, D]) for i in range(2)]
        yhi = sb("yhi", [P, 4, P], F32R)
        ylo = sb("ylo", [P, 4, P], F32R)
        ssum = sb("ssum", [P, 1])
        msum = sb("msum", [P, 1])
        rinv = sb("rinv", [P, 1])
        ea = ExitStack()
        bias = sb("bias", [P, HEADS, 384], BF16, ea)
        qkgain = sb("qkgain", [P, 2, HD], F32, ea)
        sinks = sb("sinks", [P, HEADS], F32, ea)
        raw = sb("raw", [P, 768], F32, ea)
        qkn = sb("qkn", [P, 640], F32, ea)
        agraw = sb("agraw", [P, 512], F32, ea)
        gth = sb("gth", [P, 512], F32, ea)
        qss = sb("qss", [P, 10], F32, ea)
        qms = sb("qms", [P, 10], F32, ea)
        qr = sb("qr", [P, 10], F32, ea)
        qcat = sb("qcat", [P, HEADS, P], F32R, ea)
        kcat = sb("kcat", [P, KVH, 2, P], F32R, ea)
        vcat = [sb(f"vcat{i}", [P, KVH, P], F32R, ea) for i in range(2)]
        qT = sb("qT", [P, HEADS, P], F32R, ea)
        kT = sb("kT", [P, KVH, 2, 2 * P], F32R, ea)
        sc = sb("sc", [P, HEADS, 2 * P], F32, ea)
        mx = sb("mx", [P, HEADS], F32, ea)
        nmx = sb("nmx", [P, HEADS], F32, ea)
        esum = sb("esum", [P, HEADS], F32, ea)
        sdif = sb("sdif", [P, HEADS], F32, ea)
        esink = sb("esink", [P, HEADS], F32, ea)
        den = sb("den", [P, HEADS], F32, ea)
        rden = sb("rden", [P, HEADS], F32, ea)
        pthi = sb("pthi", [P, 2, 512], F32R, ea)
        ptlo = sb("ptlo", [P, 2, 512], F32R, ea)
        olo = sb("olo", [HD, 512], F32, ea)
        osum = sb("osum", [P, 4, P], F32, ea)
        ckv = sb("ckv", [P, 2, P], F32, ea)
        ckcat = sb("ckcat", [P, KVH, 2, P], F32R, ea)
        ea.close()
        w2hi = sb("w2hi", [P, KT * WIDTH_B[3]], F32R)
        w2lo = sb("w2lo", [P, KT * WIDTH_B[3]], F32R)
        braw = [sb(f"braw{i}", [P, B_COLS]) for i in range(2)]
        glr1 = sb("glr1", [P, LR + 1])
        glrT = sb("glrT", [LR + 1, P])
        az = sb("az", [P, P])
        zm = sb("zm", [P, P])
        ez = sb("ez", [P, P])
        ex = sb("ex", [P, 4, P])
        enb = sb("enb", [P, P])
        qt = sb("qt", [P, P])
        qf = sb("qf", [P, P])
        kk = sb("kk", [P, P])
        kt0 = sb("kt0", [64, P])
        kend = sb("kend", [P, P])
        qbd = sb("qbd", [P, GH, P])
        gT = sb("gT", [P, 320])
        dec = sb("dec", [P, 1])
        asb = sb("asb", [P, 512])
        stp = sb("stp", [P, 256])
        osq = sb("osq", [P, 256])
        oss = sb("oss", [P, GH])
        oms = sb("oms", [P, GH])
        orr = sb("orr", [P, GH])
        thg = sb("thg", [P, 256])
        thc = sb("thc", [P, 512])
        gc = sb("gc", [P, CD])
        u = sb("u", [P, CD])
        ub = [sb(f"ub{i}", [P, CJ, HIST + P]) for i in range(2)]
        acc = sb("acc", [P, CJ, P])
        bst = sb("bst", [P, 6])
        mv = sb("mv", [P, 2])
        mve = sb("mve", [P, 1])
        rs = sb("rs", [P, 1])
        cn = sb("cn", [P, CD])
        cl = sb("cl", [P, CJ, P])
        cth = sb("cth", [P, CJ, P])
        yb = sb("yb", [P, 512])
        tri = sb("tri", [P, 4, P])
        mask = sb("mask", [P, 512], U32)
        wup = sb("wup", [LR + 1, P])
        glagain = sb("glagain", [P, GV])
        bpw = sb("bpw", [P, CD])
        wpw = sb("wpw", [P, CJ, CD])
        convw = sb("convw", [P, CJ, CW])
        convp = sb("convp", [P, 3, CJ])
        sts = sb("sts", [P, 256])
        uh = sb("uh", [P, CJ, HIST])

        T = [es.enter_context(nc.psum_tensor(f"T{i}", [P, 512], F32)) for i in range(3)]
        J = [es.enter_context(nc.psum_tensor(f"J{i}", [P, 512], F32)) for i in range(3)]
        S = [es.enter_context(nc.psum_tensor(f"S{i}", [P, 512], F32)) for i in range(2)]

        f = lambda t: t.bitcast(F32)

        def weights(col, width):
            if isinstance(col, tuple):
                return w2hi[:, col[0]:col[0] + width], w2lo[:, col[0]:col[0] + width]
            return whi[:, col:col + width], wlo[:, col:col + width]

        class Pass:

            def __init__(self, tag, chunks, order):
                self.order = order
                self.pieces = pieces_of(chunks, order)
                self.widths = [sum(w for _, w in c) for c in chunks]
                self.raw = [sem(f"weights_loaded_{tag}{i}") for i in range(2 * STAGES if tag == "a" else STAGES)]
                self.whi = sem(f"weights_hi_{tag}")
                self.wlo = sem(f"weights_lo_{tag}")
                self.x_loaded = [sem(f"x_loaded_{tag}{i}") for i in range(2)]
                self.x_squared = sem(f"x_squared_{tag}")
                self.x_mean = sem(f"x_mean_{tag}")
                self.x_rinv = sem(f"x_rinv_{tag}")
                if tag == "b":
                    self.x_scale = sem("x_scale_b")
                self.xn_ready = sem(f"xn_ready_{tag}")
                self.xT_psum = sem(f"xT_psum_{tag}")
                self.xT_hi = sem(f"xT_hi_{tag}")
                self.xT_lo = sem(f"xT_lo_{tag}")
                self.projected = [sem(f"projected_{tag}{i}") for i in range(len(chunks))]
                self.taken = [sem(f"projection_taken_{tag}{i}") for i in range(len(chunks))]
                self.res_loaded = [sem(f"res_loaded_{tag}{i}") for i in range(2)]
                self.y_hi = sem(f"y_hi_{tag}")
                self.y_lo = sem(f"y_lo_{tag}")
                self.out_psum = sem(f"out_psum_{tag}")
                self.out_added = sem(f"out_added_{tag}")
                self.out_stored = [sem(f"out_stored_{tag}{i}") for i in range(2)]

        A, B = Pass("a", CHUNKS_A, (0, 1, 2)), Pass("b", CHUNKS_B, (1, 2, 0, 3))
        first_consts = sem("first_consts")
        consts_a, consts_b, zeros_a, zeros_b = sem("consts_a"), sem("consts_b"), sem("zeros_a"), sem("zeros_b")
        zeros_b1, pool_consts = sem("zeros_b1"), sem("pool_consts")
        v_hi, v_lo = sem("v_hi"), sem("v_lo")
        qkT_psum, qkT_taken = sem("qkT_psum"), sem("qkT_taken")
        gate_psum, gate_tanh, gate_ready = sem("gate_psum"), sem("gate_tanh"), sem("gate_ready")
        s_psum, s_max, s_neg, s_exp = sem("scores_psum"), sem("scores_max"), sem("scores_neg"), sem("scores_exp")
        s_diff, s_esink, s_den, s_rden, p_ready = (sem("sink_diff"), sem("sink_exp"), sem("softmax_den"),
                                                  sem("softmax_rden"), [sem(f"p_ready{i}") for i in range(2)])
        n_step, n_mean, n_rinv, n_hi, n_lo = (sem("qk_norm_step"), sem("qk_mean"), sem("qk_rinv"), sem("qk_hi"),
                                              sem("qk_lo"))
        pt_psum, pt_hi, pt_lo = sem("pT_psum"), sem("pT_hi"), sem("pT_lo")
        o_psum, o_low, o_sum, y_gated = sem("o_psum"), sem("o_low"), sem("o_sum"), sem("y_gated")
        windows_stored = sem("windows_stored")
        c_hi, c_lo, c_psum, c_taken = sem("cache_hi"), sem("cache_lo"), sem("cache_psum"), sem("cache_taken")
        pass_a_done = sem("pass_a_done")

        states_stored, u_stored, dec_ready = sem("states_stored"), sem("u_stored"), sem("dec_ready")
        lr_taken, lr_psum, lr_T = sem("lowrank_taken"), sem("lowrank_psum"), sem("lowrank_T")
        z_psum, z_parts, z_exp, z_ln, la_ready = (sem("gate_logit_psum"), sem("gate_logit_parts"),
                                                 sem("gate_logit_exp"), sem("gate_logit_ln"), sem("log_decay_ready"))
        cum_psum, cum_exp, qk_scaled = sem("decay_sums_psum"), sem("decay_exp"), sem("gla_qk_scaled")
        g_psum, g_T, g_dec = sem("gla_T_psum"), sem("gla_T_taken"), sem("gla_decay")
        a_psum, a_masked, su_psum, go_psum = (sem("gla_scores_psum"), sem("gla_scores_masked"),
                                              sem("gla_state_psum"), sem("gla_o_psum"))
        g_state = sem("gla_state_ready")
        gate_step = sem("gate_step")
        go_sq, go_ss, go_ms, go_r, go_n, go_g = (sem("gla_o_squared"), sem("gla_o_sums"), sem("gla_o_mean"),
                                                sem("gla_o_rinv"), sem("gla_o_normed"), sem("gla_y_ready"))
        th_ready, gates_ready, sg_ready, u_ready = (sem("tanh_ready"), sem("gates_ready"), sem("glu_gate_ready"),
                                                   sem("u_ready"))
        uT_psum, hist_ready, uT_taken, conv_step = (sem("uT_psum"), sem("hist_ready"), sem("uT_taken"),
                                                   sem("conv_step"))
        cT_psum, bn_step, ln_mean, ln_r, cn_ready = (sem("cT_psum"), sem("ln_step"), sem("ln_mean"), sem("ln_rinv"),
                                                    sem("conv_normed"))
        cnT_psum, cl_ready, cth_ready, cs_ready = (sem("cnT_psum"), sem("ln_affine_ready"), sem("conv_tanh"),
                                                  sem("conv_silu"))
        pw_psum, c2_ready, yc_ready, yT_psum = sem("pw_psum"), sem("pw_taken"), sem("conv_y_ready"), sem("yT_psum")

        N_CONSTS_A, N_CONSTS_B = 16 * 6, 16 * (14 + GH)

        B_16, B_17 = 2 * STAGES, 5 * STAGES

        def stage_of(ps, n):
            return n % (2 * STAGES) if ps is A and n < 3 * KT else n % STAGES

        def stage(i):
            return wraw[:, i, :] if i < STAGES else res[(i - STAGES) // 2][:, i % 2 * 512:(i % 2 + 1) * 512]

        def load_weights(eng, ps, first, last):
            for n, (part, k, what, col, width) in list(enumerate(ps.pieces))[first:last]:
                before = [m for m in range(n) if stage_of(ps, m) == stage_of(ps, n)]
                if before:
                    need(eng, ps.wlo, before[-1] + 1)
                rows = slice(k * P, (k + 1) * P)
                dst = stage(stage_of(ps, n))
                if part == "in":
                    at = 0
                    for first, w in what:
                        eng.dma_start(dst[:, at:at + w], io["w_in"][0, rows, first:first + w]).then_inc(
                            ps.raw[stage_of(ps, n)], 16)
                        at += w
                else:
                    r0 = (0 if ps is A else 512) + k * P
                    eng.dma_start(dst, io["w_out"][0, r0:r0 + P, what * 512:(what + 1) * 512]).then_inc(
                        ps.raw[stage_of(ps, n)], 16)

        def raw_counts(ps):
            count, out = [0] * (2 * STAGES), []
            for n, (part, k, what, col, width) in enumerate(ps.pieces):
                count[stage_of(ps, n)] += 16 * (len(what) if part == "in" else 1)
                out.append(count[stage_of(ps, n)])
            return out

        def split_hi(ps, a, b):
            for n, (part, k, what, col, width) in list(enumerate(ps.pieces))[a:b]:
                nc.scalar.wait_ge(ps.raw[stage_of(ps, n)], raw_counts(ps)[n])
                if ps is B and n == 0:
                    nc.scalar.wait_ge(A.projected[2], TILES)
                if ps is B and n == 3 * KT:
                    nc.scalar.wait_ge(windows_stored, 16 * 6)
                if ps is B and part == "out" and k == 0 and what == 0:
                    nc.scalar.wait_ge(A.out_psum, 2 * TILES)
                scale = gain[:, k:k + 1] if part == "in" else 1.0
                nc.scalar.activation(weights(col, width)[0], stage(stage_of(ps, n))[:, 0:width], ACT.Copy,
                                     scale=scale).then_inc(ps.whi, 1)

        def split_lo(ps, a, b):
            for n, (part, k, what, col, width) in list(enumerate(ps.pieces))[a:b]:
                nc.vector.wait_ge(ps.whi, n + 1)
                src = stage(stage_of(ps, n))[:, 0:width]
                hi, lo = weights(col, width)
                if part == "in":
                    nc.vector.scalar_tensor_tensor(lo, src, gain[:, k:k + 1], f(hi), ALU.mult,
                                                   ALU.subtract).then_inc(ps.wlo, 1)
                else:
                    nc.vector.tensor_tensor(lo, src, f(hi), ALU.subtract).then_inc(ps.wlo, 1)

        def x_rows(src_p, src_s, t, cols=slice(0, D)):
            if t.fixed and t.n == LAST:
                return src_s[0, 0:DEC, cols], DEC
            return src_p[0, bass.ds(t.n * P, P), cols], P

        def load_x(ps, t):
            need(nc.sync, ps.xn_ready, t.n - 1)
            src, rows = x_rows(io["x_prompt"], io["x_sample"], t)
            nc.sync.dma_start(xin[t.par][0:rows, :], src).then_inc(ps.x_loaded[t.par], 16)

        def load_res(ps, t):
            need(nc.sync, ps.out_stored[t.par], 32 * t.half)
            if ps is A and t.fixed and t.n == 0:
                nc.sync.wait_ge(ps.wlo, 3 * KT)
            if ps is A:
                src, rows = x_rows(io["x_prompt"], io["x_sample"], t)
            else:
                src, rows = x_rows(yp, ys, t)
            nc.sync.dma_start(res[t.par][0:rows, :], src).then_inc(ps.res_loaded[t.par], 16)

        def store_out(ps, t):
            for h in range(2):
                need(nc.sync, ps.out_added, 2 * t.n + h + 1)
                dst, rows = x_rows(yp, ys, t, slice(h * 512, (h + 1) * 512))
                nc.sync.dma_start(dst, res[t.par][0:rows, h * 512:(h + 1) * 512]).then_inc(
                    ps.out_stored[t.par], 16)

        def norm_square(ps, t):
            nc.scalar.wait_ge(ps.x_loaded[t.par], 16 * (t.half + 1))
            need(nc.scalar, ps.xT_psum, 2 * t.n)
            nc.scalar.activation(xn[:, :], xin[t.par][:, :], ACT.Square, accum_out=ssum[:, :]).then_inc(
                ps.x_squared, 1)

        def norm_rinv(ps, t):
            nc.gpsimd.wait_ge(ps.x_squared, t.n + 1)
            nc.gpsimd.tensor_tensor(msum[:, :], ssum[:, :], eps_d[:, :], ALU.add).then_inc(ps.x_mean, 1)
            nc.gpsimd.wait_ge(ps.x_mean, t.n + 1)
            nc.gpsimd.tensor_tensor(rinv[:, :], msum[:, :], mhalf[:, 0:1], ALU.pow).then_inc(ps.x_rinv, 1)
            if ps is B:
                nc.gpsimd.wait_ge(ps.x_rinv, t.n + 1)
                nc.gpsimd.tensor_tensor(rscale[:, :], rinv[:, :], root_d[:, :], ALU.mult).then_inc(ps.x_scale, 1)

        def norm_scale(ps, t):
            nc.vector.wait_ge(ps.x_rinv, t.n + 1)
            nc.vector.tensor_scalar(xn[:, :], xin[t.par][:, :], rinv[:, :], D ** 0.5, ALU.mult,
                                    ALU.mult).then_inc(ps.xn_ready, 1)

        def x_bank(ps, t, g):
            early = ps is A or (t.fixed and t.n == 0)
            return T[1 - g if early else g]

        def norm_scale_act(ps, t):
            nc.scalar.wait_ge(ps.x_scale, t.n + 1)
            nc.scalar.activation(xn[:, :], xin[t.par][:, :], ACT.Copy, scale=rscale[:, :]).then_inc(ps.xn_ready, 1)

        def transpose_x(ps, t, g):
            if g == 0:
                nc.tensor.wait_ge(ps.xn_ready, t.n + 1)
            for j in range(4):
                last = nc.tensor.transpose(x_bank(ps, t, g)[:, j * P:(j + 1) * P], 
                                           xn[:, (4 * g + j) * P:(4 * g + j + 1) * P], ident[:, :])
            last.then_inc(ps.xT_psum, 1)

        def split_x_hi(ps, t, g):
            nc.scalar.wait_ge(ps.xT_psum, 2 * t.n + g + 1)
            nc.scalar.activation(xhi[:, 4 * g:4 * g + 4, :], x_bank(ps, t, g)[:, :].rearrange("p (j n) -> p j n", n=P),
                                 ACT.Copy).then_inc(ps.xT_hi, 1)

        def split_x_lo(ps, t, g):
            nc.vector.wait_ge(ps.xT_hi, 2 * t.n + g + 1)
            nc.vector.tensor_tensor(xlo[:, 4 * g:4 * g + 4, :],
                                    x_bank(ps, t, g)[:, :].rearrange("p (j n) -> p j n", n=P), f(xhi[:, 4 * g:4 * g + 4, :]), ALU.subtract).then_inc(ps.xT_lo, 1)

        def project(ps, t, c, bank, half=None):
            width = ps.widths[c]
            base = KT * sum(ps.widths[:c])
            if c == ps.order[0]:
                nc.tensor.wait_ge(ps.xT_lo, 2 * t.n + (1 if half == 0 else 2))
            if t.fixed and t.n == 0:
                nc.tensor.wait_ge(ps.wlo, KT * (ps.order.index(c) + 1))
            ks = range(KT) if half is None else range(half * KT // 2, (half + 1) * KT // 2)
            for k in ks:
                hi, lo = weights((k * width,) if c == 3 else base + k * width, width)
                for n, (x, w) in enumerate(((xhi, hi), (xhi, lo), (xlo, hi))):
                    last = nc.tensor.matmul(bank[:, 0:width], x[:, k, :], w, start=(k == 0 and n == 0),
                                            stop=(k == KT - 1 and n == 2))
            if half != 0:
                last.then_inc(ps.projected[c], 1)

        def output(ps, t, h, bank):
            if h == 0:
                nc.tensor.wait_ge(ps.y_lo, (t.n + 1) * (2 if ps is A else 1))
            if t.fixed and t.n == 0:
                nc.tensor.wait_ge(ps.wlo, len(ps.pieces))
            for k in range(4):
                col = W_OUT + k * D + h * 512
                hi, lo = weights(col, 512)
                for n, (y, w) in enumerate(((yhi, hi), (yhi, lo), (ylo, hi))):
                    last = nc.tensor.matmul(bank[:, :], y[:, k, :], w, start=(k == 0 and n == 0),
                                            stop=(k == 3 and n == 2))
            last.then_inc(ps.out_psum, 1)

        def add_out(ps, t, h, bank):
            if h == 0:
                nc.vector.wait_ge(ps.res_loaded[t.par], 16 * (t.half + 1))
            nc.vector.wait_ge(ps.out_psum, 2 * t.n + h + 1)
            dst = res[t.par][:, h * 512:(h + 1) * 512]
            nc.vector.tensor_tensor(dst, bank[:, :], dst, ALU.add).then_inc(ps.out_added, 1)

        def over_tiles(eng, body, first=3, last=14):
            for c in range(-2, first):
                body(Tile(0, c))
            with eng.Fori(0, (last - first + 1) // 2) as i:
                body(Tile(i, first))
                body(Tile(i, first + 1))
            for c in range(last + 1, TILES + 1):
                body(Tile(0, c))

        def out_bank(t, h):
            return J[h + 1] if t.fixed and t.n == TILES else J[h]

        B0 = Tile(0, 0)

        def when(t, *steps):
            for s in steps if t.real() else ():
                s(t)

        es.enter_context(nc.allow_non_contiguous_dma(reason="small vectors of parameters, once"))
        block = es.enter_context(nc.Block())

        @block.sync
        def _(sp):
            for dst, src in ((gain[:, :], io["norm_gain"][0].rearrange("(k p) -> p k", p=P)),
                             (ident[:, :], ident_d)):
                sp.dma_start(dst, src).then_inc(first_consts, 16)
            load_x(A, Tile(0, 0))
            load_weights(sp, A, 0, KT)
            load_x(A, Tile(0, 1))
            for dst, src in ((bias[:, :, :], bias_d.bitcast(BF16)),
                             (qkgain[:, 0, :], io["q_norm_gain"].partition_broadcast(P)),
                             (qkgain[:, 1, :], io["k_norm_gain"].partition_broadcast(P)),
                             (sinks[:, :], io["attn_sinks"].partition_broadcast(P)),
                             (ckv[:, 0, :], io["cache_k"][0, 0].rearrange("w h d -> w (h d)")),
                             (ckv[:, 1, :], io["cache_v"][0, 0].rearrange("w h d -> w (h d)"))):
                sp.dma_start(dst, src).then_inc(consts_a, 16)
            load_weights(sp, A, KT, 3 * KT)
            for src, dst in ((io["cache_k"], sk_o), (io["cache_v"], sv_o)):
                sp.dma_start(dst[0, 0, 0:DEC], src[0, 0, DEC:P]).then_inc(windows_stored, 16)

            def body_a(t):
                if t.fixed and t.n == -2:
                    return
                if (t + 3).real():
                    load_x(A, t + 3)
                if t.real():
                    load_res(A, t)
                if t.fixed and t.n == 0:
                    load_weights(sp, A, 3 * KT, len(A.pieces))
                if t.fixed and t.n == LAST - 1:
                    sp.wait_ge(A.xn_ready, TILES)
                    for i in range(2):
                        load_x(B, Tile(0, i))
                if t.fixed and t.n == 1:
                    for dst, src in ((tri[:, :, :], tri_d), (mask[:, :], mask_d.bitcast(U32)),
                                     (wup[0:LR, :], io["gla_w_gate_up"][0]), (wup[LR:LR + 1, :], io["gla_b_gate"]),
                                     (glagain[:, :], io["gla_norm_gain"].partition_broadcast(P)),
                                     (bpw[:, :], io["conv_b_pw"].partition_broadcast(P)),
                                     (wpw[:, :, :], io["conv_w_pw"][0].rearrange("(j p) n -> p j n", p=P)),
                                     (convp[:, 0, :], io["conv_b"][0].rearrange("(j p) -> p j", p=P)),
                                     (convp[:, 1, :], io["conv_ln_gain"][0].rearrange("(j p) -> p j", p=P)),
                                     (convp[:, 2, :], io["conv_ln_bias"][0].rearrange("(j p) -> p j", p=P)),
                                     (convw[:, 0, :], io["conv_w"][0, :, 0:P].rearrange("w p -> p w")),
                                     (convw[:, 1, :], io["conv_w"][0, :, P:CD].rearrange("w p -> p w")),
                                     (uh[:, 0, :], io["state_conv"][0, 0, :, 0:P].rearrange("w p -> p w")),
                                     (uh[:, 1, :], io["state_conv"][0, 0, :, P:CD].rearrange("w p -> p w"))):
                        sp.dma_start(dst, src).then_inc(consts_b, 16)
                    sp.wait_ge(zeros_b1, 1)
                    for h in range(GH):
                        sp.dma_start(sts[h * GK:(h + 1) * GK, h * GV:(h + 1) * GV], io["state_gla"][0, 0, h]).then_inc(
                            consts_b, 16)
                for at, first, last in ((LAST - 2, 0, STAGES), (LAST, STAGES, B_16 + STAGES),
                                        (TILES, B_16 + STAGES, B_17 + STAGES)):
                    if t.fixed and t.n == at:
                        load_weights(sp, B, first, last)
                if t.fixed and t.n + 1 in (LAST - 1, LAST):
                    rows = P if t.n + 1 == LAST - 1 else DEC
                    k_dst, v_dst = (pk_o, pv_o) if rows == P else (sk_o, sv_o)
                    sp.wait_ge(n_step, 5 * (t.n + 2))
                    sp.dma_start(k_dst[0, 0, P - rows:P].rearrange("w h d -> w (h d)"),
                                 qkn[0:rows, 512:640]).then_inc(windows_stored, 16)
                    sp.dma_start(v_dst[0, 0, P - rows:P].rearrange("w h d -> w (h d)"),
                                 raw[0:rows, 640:768]).then_inc(windows_stored, 16)
                if (t + -1).real():
                    store_out(A, t + -1)

            over_tiles(sp, body_a, 3, 12)
            load_weights(sp, B, B_17 + STAGES, 4 * KT)
            sp.wait_ge(pass_a_done, 4)
            sp.wait_ge(windows_stored, 16 * 6)
            load_weights(sp, B, 4 * KT, len(B.pieces))
            for i in range(2):
                sp.wait_ge(A.out_stored[i], 32 * ((TILES + 1 - i) // 2))

            def body_b(t):
                if t.fixed and t.n == -2:
                    return
                if (t + 3).real():
                    load_x(B, t + 3)
                if t.real():
                    load_res(B, t)
                if t.fixed and t.n in (LAST - 1, LAST):
                    end, dst = (P, pc_o) if t.n == LAST - 1 else (DEC, sc_o)
                    sp.wait_ge(u_ready, t.n + 1)
                    sp.dma_start(dst[0, 0], u[end - HIST:end, :]).then_inc(u_stored, 16)
                    st, dst = (stp, ps_o) if t.n == LAST - 1 else (sts, ss_o)
                    sp.wait_ge(g_state, t.n + 1)
                    for h in range(GH):
                        sp.dma_start(dst[0, 0, h], st[h * GK:(h + 1) * GK, h * GV:(h + 1) * GV]).then_inc(
                            states_stored, 16)
                if (t + -1).real():
                    store_out(B, t + -1)

            over_tiles(sp, body_b, 3, 12)
            for i in range(2):
                sp.wait_ge(B.out_stored[i], 32 * ((TILES + 1 - i) // 2))
            sp.wait_ge(states_stored, 16 * 8)
            sp.wait_ge(u_stored, 16 * 2)

        @block.gpsimd
        def _(pool):
            for buf, value in ((mhalf, -0.5), (eps_d, D * EPS), (eps_h, HD * EPS), (eps_1, EPS),
                               (root_d, D ** 0.5)):
                nc.gpsimd.memset(buf[:, :], value).then_inc(pool_consts, 1)
            nc.gpsimd.memset(sts[:, :], 0.0).then_inc(zeros_b1, 1)
            pool.wait_ge(pool_consts, 5)
            norm_rinv(A, Tile(0, 0))

            def body_a(t):
                if not (t.fixed and t.n == -2):
                    when(t + 2, lambda n: norm_rinv(A, n))
                if t.fixed and t.n == LAST:
                    norm_rinv(B, B0)
                n = t + 1
                if n.real():
                    pool.wait_ge(n_step, 5 * n.n + 2)
                    nc.gpsimd.tensor_tensor(qms[:, :], qss[:, :], eps_h[:, 0:10], ALU.add).then_inc(
                        n_mean, 1)
                    pool.wait_ge(n_mean, n.n + 1)
                    nc.gpsimd.tensor_tensor(qr[:, :], qms[:, :], mhalf[:, 0:10], ALU.pow).then_inc(n_rinv, 1)

            over_tiles(pool, body_a)
            pool.sem_inc(pass_a_done, 1)
            pool.wait_ge(pass_a_done, 4)
            for buf in (stp, asb):
                nc.gpsimd.memset(buf[:, :], 0.0).then_inc(zeros_b, 1)
            nc.gpsimd.memset(qbd[:, :, :], 0.0).then_inc(zeros_b, 1)
            nc.gpsimd.memset(glr1[:, LR:LR + 1], 1.0).then_inc(zeros_b, 1)

            def body_b(t):
                p = t + -1
                r = braw[t.par]

                def ln_rinv(p):
                    pool.wait_ge(bn_step, 2 * p.n + 2)
                    nc.gpsimd.tensor_tensor(mve[:, :], mv[:, 1:2], eps_1[:, :], ALU.add).then_inc(ln_mean, 1)
                    pool.wait_ge(ln_mean, p.n + 1)
                    nc.gpsimd.tensor_tensor(rs[:, :], mve[:, :], mhalf[:, 0:1], ALU.pow).then_inc(ln_r, 1)

                if p.real() and t.real():
                    ln_rinv(p)
                if not (t.fixed and t.n == -2):
                    when(t + 2, lambda n: norm_rinv(B, n))
                if t.real():
                    gg, cg = r[:, B_GG:B_GG + 256], r[:, B_CG:B_CG + 256]
                    pool.wait_ge(th_ready, 2 * t.n + 2)
                    nc.gpsimd.tensor_tensor(thg[:, :], thg[:, :], gg, ALU.mult).then_inc(gate_step, 1)
                    need(pool, yc_ready, t.n)
                    nc.gpsimd.tensor_tensor(gc[:, :], thc[:, 256:512], cg, ALU.mult).then_inc(gate_step, 1)
                    pool.wait_ge(gate_step, 2 * t.n + 2)
                    nc.gpsimd.tensor_tensor(thg[:, :], thg[:, :], gg, ALU.add).then_inc(gates_ready, 1)
                    nc.gpsimd.tensor_tensor(gc[:, :], gc[:, :], cg, ALU.add).then_inc(gates_ready, 1)
                    if t.fixed and t.n == LAST:
                        ln_rinv(t)
                    pool.wait_ge(go_ss, t.n + 1)
                    nc.gpsimd.tensor_tensor(oms[:, :], oss[:, :], eps_h[:, 0:GH], ALU.add).then_inc(
                        go_ms, 1)
                    pool.wait_ge(go_ms, t.n + 1)
                    nc.gpsimd.tensor_tensor(orr[:, :], oms[:, :], mhalf[:, 0:GH], ALU.pow).then_inc(go_r, 1)
                    pool.wait_ge(go_n, 2 * t.n + 2)
                    nc.gpsimd.tensor_tensor(yb[:, 0:256], yb[:, 0:256], thg[:, :], ALU.mult).then_inc(go_g, 1)

            over_tiles(pool, body_b)

        @block.scalar
        def _(act):
            act.wait_ge(first_consts, 32)
            norm_square(A, Tile(0, 0))
            split_hi(A, 0, KT)

            def body_a(t):
                t1 = t + 1
                if t.fixed and t.n == LAST:
                    cache_hi(act)
                if t1.real():
                    split_x_hi(A, t1, 1)
                if t.fixed and t.n == TILES:
                    split_x_hi(B, B0, 1)
                if t.fixed and t.n == -1:
                    split_hi(A, KT, 3 * KT)
                if t.real():
                    def qk_taken(n):
                        act.wait_ge(qkT_psum, 3 * t.n + n + 1)
                        src = (T[2], T[1], T[0])[n][:, :].rearrange("p (a b) -> p a b", b=P)
                        if n < 2:
                            dst = qT[:, 4 * n:4 * n + 4, :]
                        else:
                            dst = kT[:, :, :, t.par * P:(t.par + 1) * P].rearrange("p h o n -> p (h o) n")
                        nc.scalar.activation(dst, src, ACT.Copy).then_inc(qkT_taken, 1)

                    qk_taken(0)
                    qk_taken(1)
                    act.wait_ge(gate_psum, t.n + 1)
                    need(act, y_gated, 2 * t.n)
                    nc.scalar.activation(gth[:, :], T[2][:, :], ACT.Tanh, scale=0.5).then_inc(gate_tanh, 1)
                    qk_taken(2)
                    act.wait_ge(A.taken[1], t.n + 1)
                    nc.scalar.activation(vcat[t.par][:, :, 0:HD], raw[:, 640:768].rearrange("p (h d) -> p h d", d=HD),
                                         ACT.Copy).then_inc(v_hi, 1)
                if (t + -1).real():
                    y_hi_half(t + -1, 1)
                if t.fixed and t.n == 0:
                    split_hi(A, 3 * KT, 3 * KT + STAGES)
                if t.fixed and t.n == LAST:
                    split_hi(B, 0, STAGES)
                if not (t.fixed and t.n == -2):
                    when(t + 2, lambda n: norm_square(A, n))
                if t.fixed and t.n == LAST:
                    nc.scalar.wait_ge(A.xT_psum, 2 * TILES)
                    norm_square(B, B0)
                if t1.real():
                    act.wait_ge(A.projected[0], t1.n + 1)
                    need(act, n_step, 5 * t1.n)
                    nc.scalar.activation(raw[:, 0:512], J[0][:, :], ACT.Copy).then_inc(A.taken[0], 1)
                def exp_scores(n):
                    act.wait_ge(s_neg, 4 * t.n + n + 1)
                    for h in (2 * n, 2 * n + 1):
                        last = nc.scalar.activation(sc[:, h, :], sc[:, h, :], ACT.Exp, bias=nmx[:, h:h + 1],
                                                    accum_out=esum[:, h:h + 1])
                    last.then_inc(s_exp, 1)

                def pT_hi(k):
                    act.wait_ge(pt_psum, 4 * t.n + k + 1)
                    nc.scalar.activation(pthi[:, k % 2, :], T[k % 3][:, :], ACT.Copy).then_inc(pt_hi, 1)

                def o_low_half(g):
                    act.wait_ge(o_psum, 2 * t.n + g + 1)
                    need(act, o_sum, 4 * t.n + 2 * g)
                    nc.scalar.activation(olo[:, :], S[g][HD:P, :], ACT.Copy).then_inc(o_low, 1)

                if t.real():
                    exp_scores(0)
                    exp_scores(1)
                if t1.real():
                    act.wait_ge(A.projected[1], t1.n + 1)
                    need(act, v_lo, t1.n)
                    if t1.fixed and t1.n == LAST:
                        act.wait_ge(windows_stored, 16 * 4)
                    nc.scalar.activation(raw[:, 512:768], J[1][:, 0:256], ACT.Copy).then_inc(A.taken[1], 1)
                if t.real():
                    exp_scores(2)
                    exp_scores(3)
                    act.wait_ge(s_diff, t.n + 1)
                    nc.scalar.activation(esink[:, :], sdif[:, :], ACT.Exp).then_inc(s_esink, 1)
                    act.wait_ge(s_rden, t.n + 1)
                    for h in P_ACT:
                        nc.scalar.activation(sc[:, h, :], sc[:, h, :], ACT.Copy,
                                             scale=rden[:, h:h + 1]).then_inc(p_ready[1], 1)
                    pT_hi(0)
                    pT_hi(1)
                if t1.real():
                    act.wait_ge(n_step, 5 * t1.n + 5)
                    nc.scalar.activation(qcat[:, :, 0:HD], qkn[:, 0:512].rearrange("p (h d) -> p h d", d=HD),
                                         ACT.Copy).then_inc(n_hi, 1)
                    kn = qkn[:, 512:640].rearrange("p (h d) -> p h d", d=HD)
                    for o in range(2):
                        nc.scalar.activation(kcat[:, :, o, o * HD:(o + 1) * HD], kn, ACT.Copy).then_inc(n_hi, 1)
                if t.fixed and t.n == LAST:
                    split_hi(B, STAGES, B_16)
                if t1.real():
                    act.wait_ge(A.projected[2], t1.n + 1)
                    nc.scalar.activation(agraw[:, :], J[2][:, :], ACT.Copy).then_inc(A.taken[2], 1)
                if t.real():
                    o_low_half(0)
                    pT_hi(2)
                    pT_hi(3)
                when(t + 2, lambda n: split_x_hi(A, n, 0))
                if t.fixed and t.n == LAST:
                    split_x_hi(B, B0, 0)
                if t.real():
                    y_hi_half(t, 0)
                    o_low_half(1)
                if t.fixed and t.n == 0:
                    split_hi(A, 3 * KT + STAGES, len(A.pieces))
                if t.fixed and t.n == TILES:
                    split_hi(B, B_16, B_17)

            def y_hi_half(t, g):
                act.wait_ge(y_gated, 2 * t.n + g + 1)
                need(act, A.out_psum, 2 * t.n)
                nc.scalar.activation(yhi[:, 2 * g:2 * g + 2, :], osum[:, 2 * g:2 * g + 2, :],
                                     ACT.Copy).then_inc(A.y_hi, 1)

            def cache_hi(act):
                for o in range(2):
                    nc.scalar.activation(ckcat[:, :, o, o * HD:(o + 1) * HD],
                                         ckv[:, 0, :].rearrange("p (h d) -> p h d", d=HD), ACT.Copy).then_inc(c_hi, 1)
                nc.scalar.activation(vcat[1][:, :, 0:HD], ckv[:, 1, :].rearrange("p (h d) -> p h d", d=HD),
                                     ACT.Copy).then_inc(c_hi, 1)
                act.wait_ge(c_psum, 1)
                nc.scalar.activation(kT[:, :, :, P:2 * P].rearrange("p h o n -> p (h o) n"),
                                     T[0][:, :].rearrange("p (a b) -> p a b", b=P), ACT.Copy).then_inc(c_taken, 1)

            over_tiles(act, body_a)
            act.sem_inc(pass_a_done, 1)

            act.wait_ge(pass_a_done, 4)

            def body_b(t):
                t1, p = t + 1, t + -1
                r = braw[t.par]
                if t.fixed and t.n == 0:
                    act.wait_ge(consts_b, N_CONSTS_B)
                    act.wait_ge(zeros_b, 4)
                if t.fixed and t.n == -1:
                    split_hi(B, B_17, 4 * KT)
                if t.real():
                    act.wait_ge(uT_psum, t.n + 1)
                    nc.scalar.activation(ub[t.par][:, :, HIST:], T[2][:, 0:CD].rearrange("p (j n) -> p j n", n=P),
                                         ACT.Copy).then_inc(uT_taken, 1)
                    act.wait_ge(z_parts, 2 * t.n + 2)
                    nc.scalar.activation(ez[:, :], az[:, :], ACT.Exp).then_inc(z_exp, 1)
                    act.wait_ge(z_exp, t.n + 1)
                    nc.scalar.activation(ez[:, :], ez[:, :], ACT.Ln, bias=1.0).then_inc(z_ln, 1)
                if not (t.fixed and t.n == -2):
                    when(t + 2, lambda n: norm_square(B, n))
                if t.real():
                    need(act, go_g, t.n)
                    act.wait_ge(B.taken[3], t.n + 1)
                    act.wait_ge(B.taken[1], t.n + 1)
                    nc.scalar.activation(thg[:, :], r[:, B_GG:B_GG + 256], ACT.Tanh, scale=0.5).then_inc(th_ready, 1)
                if t1.real():
                    act.wait_ge(B.projected[1], t1.n + 1)
                    nc.scalar.activation(braw[t1.par][:, 272:784], J[0][:, :], ACT.Copy).then_inc(B.taken[1], 1)
                if t.real():
                    if t.fixed and t.n == 0:
                        split_hi(B, 4 * KT + STAGES, len(B.pieces))
                    act.wait_ge(cum_psum, t.n + 1)
                    nc.scalar.activation(ex[:, :, :], S[1][:, :].rearrange("p (a n) -> p a n", n=P),
                                         ACT.Exp).then_inc(cum_exp, 1)
                    nc.scalar.activation(enb[:, :], S[1][:, 0:P], ACT.Exp, scale=-1.0).then_inc(cum_exp, 1)
                if not (t.fixed and t.n == -2):
                    when(t + 2, lambda n: norm_scale_act(B, n))
                if p.real():
                    act.wait_ge(cnT_psum, p.n + 1)
                    for j in range(CJ):
                        nc.scalar.activation(cl[:, j, :], T[1][:, (2 + j) * P:(3 + j) * P], ACT.Identity,
                                             scale=convp[:, 1, j:j + 1], bias=convp[:, 2, j:j + 1]).then_inc(
                                                 cl_ready, 1)
                    act.wait_ge(cl_ready, 2 * p.n + 2)
                    nc.scalar.activation(cth[:, :, :], cl[:, :, :], ACT.Tanh, scale=0.5).then_inc(cth_ready, 1)
                if t.real():
                    act.wait_ge(g_psum, t.n + 1)
                    for h in range(GH):
                        rows = slice(h * GK, (h + 1) * GK)
                        nc.scalar.activation(qbd[rows, h, :], T[0][rows, 0:P], ACT.Copy)
                    nc.scalar.activation(gT[:, :], T[0][:, P:448], ACT.Copy).then_inc(g_T, 1)
                if t1.real():
                    act.wait_ge(B.projected[2], t1.n + 1)
                    nc.scalar.activation(braw[t1.par][:, 784:1296], J[1][:, :], ACT.Copy).then_inc(B.taken[2], 1)
                    act.wait_ge(B.projected[0], t1.n + 1)
                    nc.scalar.activation(glr1[:, 0:LR], J[2][:, 0:LR], ACT.Copy).then_inc(lr_taken, 1)
                    nc.scalar.activation(braw[t1.par][:, LR:272], J[2][:, LR:272], ACT.Copy).then_inc(B.taken[0], 1)
                if p.real():
                    act.wait_ge(yT_psum, p.n + 1)
                    nc.scalar.activation(yhi[:, :, :], T[1][:, :].rearrange("p (j n) -> p j n", n=P),
                                         ACT.Copy).then_inc(B.y_hi, 1)
                if t1.real():
                    if t1.fixed and t1.n == 0:
                        split_hi(B, 4 * KT, 4 * KT + STAGES)
                    act.wait_ge(B.projected[3], t1.n + 1)
                    nc.scalar.activation(braw[t1.par][:, 1296:1552], J[0][:, 0:256], ACT.Copy).then_inc(B.taken[3], 1)
                if t.real():
                    act.wait_ge(go_psum, t.n + 1)
                    nc.scalar.activation(osq[:, :], T[2][:, 0:256], ACT.Square).then_inc(go_sq, 1)
                if t1.real():
                    need(act, gates_ready, 2 * t1.n)
                    act.wait_ge(B.taken[3], t1.n + 1)
                    nc.scalar.activation(thc[:, :], braw[t1.par][:, B_CGL:B_CGL + 512], ACT.Tanh,
                                         scale=0.5).then_inc(th_ready, 1)
                if not (t.fixed and t.n == -2):
                    when(t + 2, lambda n: split_x_hi(B, n, 0), lambda n: split_x_hi(B, n, 1))
                if t1.real():
                    act.wait_ge(lr_psum, t1.n + 1)
                    nc.scalar.activation(glrT[:, :], S[0][0:LR + 1, 0:P], ACT.Copy).then_inc(lr_T, 1)

            over_tiles(act, body_b)

        @block.vector
        def _(dve):
            nc.vector.memset(f(vcat[1][:, :, :]), 0.0).then_inc(zeros_a, 1)
            nc.vector.memset(f(kT[:, :, :, P:2 * P]), 0.0).then_inc(zeros_a, 1)
            nc.vector.memset(sc[:, :, P:2 * P], NEG).then_inc(zeros_a, 1)
            dve.wait_ge(first_consts, 32)
            norm_scale(A, Tile(0, 0))
            split_lo(A, 0, KT)
            heads = lambda b: b.rearrange("p (h d) -> p h d", d=HD)

            def y_lo_half(t, g):
                dve.wait_ge(A.y_hi, 2 * t.n + g + 1)
                nc.vector.tensor_tensor(ylo[:, 2 * g:2 * g + 2, :], osum[:, 2 * g:2 * g + 2, :],
                                        f(yhi[:, 2 * g:2 * g + 2, :]), ALU.subtract).then_inc(A.y_lo, 1)

            def body_a(t):
                t1, t2 = t + 1, t + 2

                def scores_max(n):
                    for e in range(2):
                        h = 2 * n + e
                        cols = slice(0, P) if t.fixed and t.n == 0 else slice(0, 2 * P)
                        b0 = 0 if t.par else P
                        nc.vector.tensor_tensor_reduce(
                            out=sc[:, h, cols], in0=S[n % 2][:, e * 256:(e + 1) * 256][:, cols],
                            in1=bias[:, h, b0:b0 + 256][:, cols], scale=1.0, scalar=sinks[:, h:h + 1],
                            op0=ALU.add, op1=ALU.max, accum_out=mx[:, h:h + 1]).then_inc(s_max, 1)

                def scores_neg(n):
                    nc.vector.tensor_scalar(nmx[:, 2 * n:2 * n + 2], mx[:, 2 * n:2 * n + 2], -1.0, None,
                                            ALU.mult).then_inc(s_neg, 1)

                if t.fixed and t.n == LAST:
                    dve.wait_ge(c_hi, 3)
                    for o in range(2):
                        nc.vector.tensor_tensor(ckcat[:, :, o, (1 - o) * HD:(2 - o) * HD],
                                                ckv[:, 0, :].rearrange("p (h d) -> p h d", d=HD),
                                                f(ckcat[:, :, o, o * HD:(o + 1) * HD]), ALU.subtract).then_inc(c_lo, 1)
                    nc.vector.tensor_tensor(vcat[1][:, :, HD:P], ckv[:, 1, :].rearrange("p (h d) -> p h d", d=HD),
                                            f(vcat[1][:, :, 0:HD]), ALU.subtract).then_inc(c_lo, 1)
                if t1.real():
                    split_x_lo(A, t1, 1)
                if t.fixed and t.n == TILES:
                    split_x_lo(B, B0, 1)
                if t.fixed and t.n == -1:
                    split_lo(A, KT, 3 * KT)
                    dve.wait_ge(consts_a, N_CONSTS_A)
                if t.real():
                    dve.wait_ge(v_hi, t.n + 1)
                    nc.vector.tensor_tensor(vcat[t.par][:, :, HD:P], heads(raw[:, 640:768]),
                                            f(vcat[t.par][:, :, 0:HD]), ALU.subtract).then_inc(v_lo, 1)
                if (t + -1).real():
                    y_lo_half(t + -1, 1)
                if t.fixed and t.n == 0:
                    split_lo(A, 3 * KT, 3 * KT + STAGES)
                if t.fixed and t.n == TILES:
                    split_lo(B, B_16, B_16 + 2 * STAGES)
                if t.real():
                    need(dve, pt_psum, 4 * t.n)
                    dve.wait_ge(s_psum, 4 * t.n + 1)
                    dve.wait_ge(gate_tanh, t.n + 1)
                    nc.vector.scalar_tensor_tensor(gth[:, :], gth[:, :], 1.0, T[2][:, :], ALU.add,
                                                   ALU.mult).then_inc(gate_ready, 1)
                    scores_max(0)
                    dve.wait_ge(s_max, 8 * t.n + 2)
                    dve.wait_ge(s_psum, 4 * t.n + 2)
                    scores_neg(0)
                    scores_max(1)
                    dve.wait_ge(s_max, 8 * t.n + 4)
                    scores_neg(1)
                if not (t.fixed and t.n == -2) and t2.real():
                    dve.wait_ge(A.x_rinv, t2.n + 1)
                    need(dve, s_psum, 4 * t.n + 3)
                    norm_scale(A, t2)
                if t.fixed and t.n == LAST:
                    norm_scale(B, B0)
                if t.real():
                    if not t2.real():
                        dve.wait_ge(s_psum, 4 * t.n + 3)
                    scores_max(2)
                    dve.wait_ge(s_max, 8 * t.n + 6)
                    dve.wait_ge(s_psum, 4 * t.n + 4)
                    scores_neg(2)
                    scores_max(3)
                    dve.wait_ge(s_max, 8 * t.n + 8)
                    scores_neg(3)
                    dve.wait_ge(s_neg, 4 * t.n + 4)
                    nc.vector.tensor_tensor(sdif[:, :], sinks[:, :], nmx[:, :], ALU.add).then_inc(s_diff, 1)
                if t.fixed and t.n == LAST:
                    split_lo(B, 0, STAGES)
                if t1.real():
                    dve.wait_ge(A.taken[1], t1.n + 1)
                    if t1.fixed and t1.n == LAST:
                        dve.wait_ge(windows_stored, 16 * 4)
                    nc.vector.tensor_tensor(qkn[:, :], raw[:, 0:640], raw[:, 0:640], ALU.mult).then_inc(n_step, 1)
                    dve.wait_ge(n_step, 5 * t1.n + 1)
                    nc.vector.tensor_reduce(qss[:, :], qkn[:, :].rearrange("p (h d) -> p h d", d=HD), AX.X,
                                            ALU.add).then_inc(n_step, 1)
                if t.real():
                    dve.wait_ge(s_exp, 4 * t.n + 4)
                    dve.wait_ge(s_esink, t.n + 1)
                    nc.vector.tensor_tensor(den[:, :], esum[:, :], esink[:, :], ALU.add).then_inc(s_den, 1)
                    dve.wait_ge(s_den, t.n + 1)
                    nc.vector.reciprocal(rden[:, :], den[:, :]).then_inc(s_rden, 1)
                    dve.wait_ge(s_rden, t.n + 1)
                    for h in P_DVE:
                        nc.vector.tensor_scalar(sc[:, h, :], sc[:, h, :], rden[:, h:h + 1], None,
                                                ALU.mult).then_inc(p_ready[0], 1)
                if t.fixed and t.n == LAST:
                    split_lo(B, STAGES, B_16)

                def pT_lo(k):
                    dve.wait_ge(pt_hi, 4 * t.n + k + 1)
                    nc.vector.tensor_tensor(ptlo[:, k % 2, :], T[k % 3][:, :], f(pthi[:, k % 2, :]),
                                            ALU.subtract).then_inc(pt_lo, 1)

                def y_half(g):
                    dve.wait_ge(o_low, 2 * t.n + g + 1)
                    for e in range(2):
                        pick = lambda b: b.rearrange("p (j e n) -> p j e n", e=2, n=P)[:, :, e, :]
                        nc.vector.tensor_tensor(osum[e * HD:(e + 1) * HD, 2 * g:2 * g + 2, :],
                                                pick(S[g][0:HD, :]), pick(olo[:, :]), ALU.add).then_inc(o_sum, 1)
                    dve.wait_ge(o_sum, 4 * t.n + 2 * g + 2)
                    nc.vector.scalar_tensor_tensor(osum[:, 2 * g:2 * g + 2, :], osum[:, 2 * g:2 * g + 2, :], 0.5,
                                                   gth[:, 256 * g:256 * g + 256].rearrange("p (j n) -> p j n", n=P),
                                                   ALU.mult, ALU.mult).then_inc(y_gated, 1)

                if t.real():
                    pT_lo(0)
                    pT_lo(1)
                if t1.real():
                    dve.wait_ge(n_rinv, t1.n + 1)
                    nc.vector.tensor_tensor(heads(qkn[:, :]), heads(raw[:, 0:640]),
                                            qr[:, :].unsqueeze(2).to_broadcast([P, 10, HD]),
                                            ALU.mult).then_inc(n_step, 1)
                    dve.wait_ge(n_step, 5 * t1.n + 3)
                    nc.vector.scalar_tensor_tensor(heads(qkn[:, 0:512]), heads(qkn[:, 0:512]), 1.0,
                                                   qkgain[:, 0, :].unsqueeze(1).to_broadcast([P, HEADS, HD]),
                                                   ALU.mult, ALU.mult).then_inc(n_step, 1)
                    nc.vector.scalar_tensor_tensor(heads(qkn[:, 512:640]), heads(qkn[:, 512:640]), HD ** 0.5,
                                                   qkgain[:, 1, :].unsqueeze(1).to_broadcast([P, KVH, HD]),
                                                   ALU.mult, ALU.mult).then_inc(n_step, 1)
                if (t + -1).real():
                    add_out(A, t + -1, 0, out_bank(t, 0))
                if t1.real():
                    dve.wait_ge(n_hi, 3 * t1.n + 3)
                    nc.vector.tensor_tensor(qcat[:, :, HD:P], heads(qkn[:, 0:512]), f(qcat[:, :, 0:HD]),
                                            ALU.subtract).then_inc(n_lo, 1)
                    for o in range(2):
                        nc.vector.tensor_tensor(kcat[:, :, o, (1 - o) * HD:(2 - o) * HD], heads(qkn[:, 512:640]),
                                                f(kcat[:, :, o, o * HD:(o + 1) * HD]), ALU.subtract).then_inc(n_lo, 1)
                if t.real():
                    pT_lo(2)
                    pT_lo(3)
                    y_half(0)
                when(t + 2, lambda n: split_x_lo(A, n, 0))
                if t.fixed and t.n == LAST:
                    split_x_lo(B, B0, 0)
                if t.fixed and t.n == TILES:
                    split_lo(B, B_16 + 2 * STAGES, B_17)
                if (t + -1).real():
                    add_out(A, t + -1, 1, out_bank(t, 1))
                if t.real():
                    y_lo_half(t, 0)
                    y_half(1)
                if t.fixed and t.n == 0:
                    split_lo(A, 3 * KT + STAGES, len(A.pieces))

            over_tiles(dve, body_a)
            dve.sem_inc(pass_a_done, 1)

            dve.wait_ge(pass_a_done, 4)

            def body_b(t):
                t1, p = t + 1, t + -1
                r = braw[t.par]
                st = sts if t.fixed and t.n == LAST else stp
                if t.fixed and t.n == -1:
                    split_lo(B, B_17, 4 * KT)
                if t.fixed and t.n == 0:
                    dve.wait_ge(consts_b, N_CONSTS_B)
                    dve.wait_ge(zeros_b, 4)
                if t.real():
                    dve.wait_ge(z_psum, t.n + 1)
                    nc.vector.tensor_scalar(zm[:, :], S[0][:, 0:P], 0.0, None, ALU.min).then_inc(z_parts, 1)
                    dve.wait_ge(z_parts, 2 * t.n + 1)
                    nc.vector.scalar_tensor_tensor(az[:, :], zm[:, :], 2.0, S[0][:, 0:P], ALU.mult,
                                                   ALU.subtract).then_inc(z_parts, 1)
                def ln_stats(p):
                    dve.wait_ge(cT_psum, p.n + 1)
                    nc.vector.bn_stats(bst[:, :], S[0][:, 256:512]).then_inc(bn_step, 1)
                    dve.wait_ge(bn_step, 2 * p.n + 1)

                def ln_scale(p):
                    dve.wait_ge(ln_r, p.n + 1)
                    nc.vector.tensor_scalar(cn[:, :], S[0][:, 256:512], mv[:, 0:1], rs[:, :], ALU.subtract,
                                            ALU.mult).then_inc(cn_ready, 1)

                if p.real() and t.real():
                    ln_stats(p)
                if t.real():
                    if t.fixed and t.n == LAST:
                        nc.vector.tensor_copy(ub[t.par][:, :, 0:HIST], uh[:, :, :]).then_inc(hist_ready, 1)
                    elif t.fixed and t.n == 0:
                        nc.vector.memset(ub[t.par][:, :, 0:HIST], 0.0).then_inc(hist_ready, 1)
                    else:
                        nc.vector.tensor_copy(ub[t.par][:, :, 0:HIST], ub[1 - t.par][:, :, P:P + HIST]).then_inc(
                            hist_ready, 1)
                if p.real() and t.real():
                    nc.vector.bn_aggr(mv[:, :], bst[:, :]).then_inc(bn_step, 1)
                if t.real():
                    dve.wait_ge(uT_taken, t.n + 1)
                    dve.wait_ge(hist_ready, t.n + 1)
                    conv(t, 0, 6)
                    dve.wait_ge(z_ln, t.n + 1)
                    nc.vector.tensor_tensor(zm[:, :], zm[:, :], ez[:, :], ALU.subtract).then_inc(la_ready, 1)
                if p.real() and t.real():
                    ln_scale(p)
                if t.real():
                    conv(t, 6, 20)
                    dve.wait_ge(cum_exp, 2 * t.n + 2)
                    scale = GK ** -0.5
                    q, k = r[:, B_Q:B_Q + P], r[:, B_K:B_K + P]
                    nc.vector.scalar_tensor_tensor(qt[:, :], q, scale, ex[:, 0, :], ALU.mult, ALU.mult).then_inc(
                        qk_scaled, 1)
                    nc.vector.scalar_tensor_tensor(qf[:, :], q, scale, ex[:, 1, :], ALU.mult, ALU.mult).then_inc(
                        qk_scaled, 1)
                    nc.vector.tensor_tensor(kend[:, :], k, ex[:, 2, :], ALU.mult).then_inc(qk_scaled, 1)
                    nc.vector.tensor_tensor(kk[0:64, :], k[0:64], ex[0:64, 3, :], ALU.mult).then_inc(qk_scaled, 1)
                    nc.vector.tensor_tensor(kk[64:P, :], k[64:P], enb[64:P, :], ALU.mult).then_inc(qk_scaled, 1)
                    nc.vector.tensor_tensor(kt0[:, :], k[0:64], enb[0:64, :], ALU.mult).then_inc(qk_scaled, 1)
                if t.fixed and t.n == -1:
                    split_lo(B, 4 * KT, 4 * KT + STAGES)
                if t.fixed and t.n == 0:
                    split_lo(B, 4 * KT + STAGES, len(B.pieces))
                if p.real():
                    dve.wait_ge(cth_ready, p.n + 1)
                    nc.vector.scalar_tensor_tensor(cth[:, :, :], cth[:, :, :], 1.0, cl[:, :, :], ALU.add,
                                                   ALU.mult).then_inc(cs_ready, 1)
                if t.real():
                    conv(t, 20, 44)
                    dve.wait_ge(g_dec, t.n + 1)
                    col = DEC - 1 if t.fixed and t.n == LAST else P - 1
                    nc.vector.tensor_copy(dec[:, :], T[1][:, col:col + 1]).then_inc(dec_ready, 1)
                if p.real():
                    dve.wait_ge(pw_psum, p.n + 1)
                    nc.vector.scalar_tensor_tensor(yb[:, 256:512], T[0][:, 0:CD], 0.5, bpw[:, :], ALU.mult,
                                                   ALU.add).then_inc(c2_ready, 1)
                    dve.wait_ge(c2_ready, p.n + 1)
                    dve.wait_ge(gates_ready, 2 * (p.n + 1))
                    nc.vector.scalar_tensor_tensor(yb[:, 256:512], yb[:, 256:512], 0.5, gc[:, :], ALU.mult,
                                                   ALU.mult).then_inc(yc_ready, 1)
                if t.real():
                    dve.wait_ge(a_psum, t.n + 1)
                    conv(t, 44, 46)
                    nc.vector.copy_predicated(asb[0:64, 0:256], mask[0:64, 0:256], S[0][0:64, 0:256]).then_inc(
                        a_masked, 1)
                    nc.vector.copy_predicated(asb[:, 256:512], mask[:, 256:512], S[0][:, 256:512]).then_inc(a_masked, 1)
                if p.real():
                    dve.wait_ge(B.y_hi, p.n + 1)
                    nc.vector.tensor_tensor(ylo[:, :, :], T[1][:, :].rearrange("p (j n) -> p j n", n=P),
                                            f(yhi[:, :, :]), ALU.subtract).then_inc(B.y_lo, 1)
                if t.real():
                    conv(t, 46, 2 * CW)
                    if t.fixed and t.n == LAST:
                        ln_stats(t)
                        nc.vector.bn_aggr(mv[:, :], bst[:, :]).then_inc(bn_step, 1)
                    dve.wait_ge(go_psum, t.n + 1)
                    dve.wait_ge(dec_ready, t.n + 1)
                    for h in range(GH):
                        rows, cols = slice(h * GK, (h + 1) * GK), slice(h * GV, (h + 1) * GV)
                        last = nc.vector.scalar_tensor_tensor(st[rows, cols], st[rows, cols], dec[rows, :],
                                                              S[1][rows, cols], ALU.mult, ALU.add)
                    last.then_inc(g_state, 1)
                    dve.wait_ge(go_sq, t.n + 1)
                    nc.vector.tensor_reduce(oss[:, :], osq[:, :].rearrange("p (h d) -> p h d", d=GV), AX.X,
                                            ALU.add).then_inc(go_ss, 1)
                if t.fixed and t.n == LAST:
                    ln_scale(t)
                if t1.real():
                    dve.wait_ge(th_ready, 2 * t1.n + 1)
                    nc.vector.tensor_scalar(thc[:, 0:256], thc[:, 0:256], 0.5, 0.5, ALU.mult, ALU.add).then_inc(sg_ready, 1)
                    dve.wait_ge(sg_ready, t1.n + 1)
                    if t1.fixed and t1.n == LAST:
                        dve.wait_ge(u_stored, 16)
                    nc.vector.tensor_tensor(u[:, :], braw[t1.par][:, B_CV:B_CV + 256], thc[:, 0:256], ALU.mult).then_inc(
                        u_ready, 1)
                if p.real():
                    add_out(B, p, 0, J[1])
                if t.real():
                    dve.wait_ge(go_r, t.n + 1)
                    need(dve, yT_psum, t.n)
                    gv = lambda b: b.rearrange("p (h d) -> p h d", d=GV)
                    nc.vector.tensor_tensor(gv(yb[:, 0:256]), gv(T[2][:, 0:256]),
                                            orr[:, :].unsqueeze(2).to_broadcast([P, GH, GV]),
                                            ALU.mult).then_inc(go_n, 1)
                    dve.wait_ge(go_n, 2 * t.n + 1)
                    nc.vector.scalar_tensor_tensor(gv(yb[:, 0:256]), gv(yb[:, 0:256]), 0.5 * GV ** 0.5,
                                                   glagain[:, :].unsqueeze(1).to_broadcast([P, GH, GV]),
                                                   ALU.mult, ALU.mult).then_inc(go_n, 1)
                if not (t.fixed and t.n == -2):
                    when(t + 2, lambda n: split_x_lo(B, n, 0), lambda n: split_x_lo(B, n, 1))
                if p.real():
                    add_out(B, p, 1, J[2])

            def conv(t, a, b):
                frames = DEC if t.fixed and t.n == LAST else P
                for n in range(a, b):
                    tap, j = n // CJ, n % CJ
                    src = ub[t.par][:, j, tap:tap + frames]
                    w = convw[:, j, tap:tap + 1]
                    if tap == 0:
                        nc.vector.tensor_scalar(acc[:, j, 0:frames], src, w, convp[:, 0, j:j + 1], ALU.mult,
                                                ALU.add).then_inc(conv_step, 1)
                    else:
                        dve.wait_ge(conv_step, 2 * CW * t.n + n - 1)
                        nc.vector.scalar_tensor_tensor(acc[:, j, 0:frames], src, w, acc[:, j, 0:frames], ALU.mult,
                                                       ALU.add).then_inc(conv_step, 1)

            over_tiles(dve, body_b)

        @block.tensor
        def _(pe):
            pe.wait_ge(first_consts, 32)

            def body_a(t):
                t1 = t + 1
                if t.fixed and t.n == 0:
                    pe.wait_ge(zeros_a, 3)
                if t1.real():
                    need(pe, pt_lo, 4 * t.n)
                    transpose_x(A, t1, 1)
                if t.fixed and t.n == TILES:
                    pe.wait_ge(pt_lo, 4 * TILES)
                    transpose_x(B, B0, 1)
                    pe.wait_ge(A.out_added, 2 * LAST - 1)
                    project(B, B0, 1, J[0])
                if t.real():
                    if t.fixed and t.n == LAST:
                        pe.wait_ge(c_lo, 3)
                        pe.wait_ge(pt_lo, 4 * t.n)
                        for j in range(4):
                            last = nc.tensor.transpose(T[0][:, j * P:(j + 1) * P], f(ckcat[:, j // 2, j % 2, :]),
                                                       ident[:, :])
                        last.then_inc(c_psum, 1)
                        pe.wait_ge(c_taken, 1)
                    pe.wait_ge(n_lo, 3 * t.n + 3)
                    need(pe, pt_lo, 4 * t.n)
                    for n, (bank, h0) in enumerate(((T[2], 0), (T[1], 4))):
                        if n == 1 and t1.real():
                            pe.wait_ge(A.xT_lo, 2 * t1.n + 1)
                        for j in range(4):
                            last = nc.tensor.transpose(bank[:, j * P:(j + 1) * P], f(qcat[:, h0 + j, :]), ident[:, :])
                        last.then_inc(qkT_psum, 1)
                if t1.real():
                    need(pe, A.out_added, 2 * t.n - 2)
                    project(A, t1, 0, J[0], 0)
                if t.real():
                    pe.wait_ge(qkT_taken, 3 * t.n + 1)
                    for j in range(4):
                        last = nc.tensor.transpose(T[2][:, j * P:(j + 1) * P], agraw[:, j * P:(j + 1) * P],
                                                   ident[:, :])
                    last.then_inc(gate_psum, 1)
                    if t1.real():
                        pe.wait_ge(A.xT_lo, 2 * t1.n + 2)
                    for j in range(4):
                        last = nc.tensor.transpose(T[0][:, j * P:(j + 1) * P], f(kcat[:, j // 2, j % 2, :]),
                                                   ident[:, :])
                    last.then_inc(qkT_psum, 1)
                if t1.real():
                    project(A, t1, 0, J[0], 1)

                def scores(n):
                    if n < 2:
                        need(pe, o_sum, 4 * t.n)
                    else:
                        pe.wait_ge(s_max, 8 * t.n + 2 * (n - 1))
                    for e in range(2):
                        h = 2 * n + e
                        for o in range(2):
                            last = nc.tensor.matmul(S[n % 2][:, e * 256:(e + 1) * 256], qT[:, h, :],
                                                    kT[:, h // GROUP, o, :], start=(o == 0), stop=(o == 1))
                    last.then_inc(s_psum, 1)

                if t.real():
                    pe.wait_ge(qkT_taken, 3 * t.n + 3)
                    scores(0)
                    scores(1)
                if t1.real():
                    need(pe, A.out_added, 2 * t.n - 2)
                    project(A, t1, 1, J[1])
                if t.real():
                    scores(2)
                    scores(3)
                if t1.real():
                    need(pe, A.taken[2], t1.n)
                    project(A, t1, 2, J[2])

                def pT(g, n):
                    bank = T[(2 * g + n) % 3]
                    k = 2 * g + n
                    if k == 2:
                        pe.wait_ge(gate_ready, t.n + 1)
                    if k == 3:
                        pe.wait_ge(pt_lo, 4 * t.n + 1)
                    for j in range(GROUP):
                        h = GROUP * g + j
                        e = 1 if h in P_ACT else 0
                        mine = (P_DVE, P_ACT)[e]
                        pe.wait_ge(p_ready[e], len(mine) * t.n + mine.index(h) + 1)
                        last = nc.tensor.transpose(bank[:, j * P:(j + 1) * P],
                                                   sc[:, GROUP * g + j, n * P:(n + 1) * P], ident[:, :])
                    last.then_inc(pt_psum, 1)

                def pv(g):
                    pe.wait_ge(pt_lo, 4 * t.n + 2 * g + 2)
                    if g == 0:
                        pe.wait_ge(v_lo, t.n + 1)
                    for n in range(2):
                        for m, pt in enumerate((pthi, ptlo)):
                            last = nc.tensor.matmul(S[g][:, :], vcat[n][:, g, :], pt[:, n, :],
                                                    start=(n == 0 and m == 0), stop=(n == 1 and m == 1))
                    last.then_inc(o_psum, 1)

                def out(h):
                    if (t + -1).real():
                        if t1.real():
                            pe.wait_ge(A.taken[h], t1.n + 1)
                        elif h == 0 and not t1.real():
                            need(pe, A.out_added, 2 * t.n - 2)
                        output(A, t + -1, h, out_bank(t, h))

                if t.real():
                    pT(0, 0)
                    pT(0, 1)
                out(0)
                if t.real():
                    pv(0)
                    pT(1, 0)
                    pT(1, 1)
                when(t + 2, lambda n: transpose_x(A, n, 0))
                if t.fixed and t.n == LAST:
                    transpose_x(B, B0, 0)
                out(1)
                if t.real():
                    pv(1)

            over_tiles(pe, body_a)
            pe.sem_inc(pass_a_done, 1)

            pe.wait_ge(pass_a_done, 4)
            pe.wait_ge(A.out_added, 2 * TILES)

            def body_b(t):
                t1, p = t + 1, t + -1
                r = braw[t.par]
                st = sts if t.fixed and t.n == LAST else stp
                if t.fixed and t.n == 0:
                    pe.wait_ge(consts_b, N_CONSTS_B)
                    pe.wait_ge(zeros_b, 4)
                def conv_T(p):
                    pe.wait_ge(conv_step, 2 * CW * (p.n + 1))
                    pe.wait_ge(a_masked, 2 * (p.n + 1))
                    for j in range(CJ):
                        last = nc.tensor.transpose(S[0][:, (2 + j) * P:(3 + j) * P], acc[:, j, :], ident[:, :])
                    last.then_inc(cT_psum, 1)

                if p.real() and t.real():
                    pe.wait_ge(lr_T, t.n + 1)
                    conv_T(p)
                if t.real():
                    pe.wait_ge(lr_T, t.n + 1)
                    nc.tensor.matmul(S[0][:, 0:P], glrT[:, :], wup[:, :], start=True, stop=True).then_inc(z_psum, 1)
                    pe.wait_ge(u_ready, t.n + 1)
                    need(pe, go_n, 2 * t.n)
                    for j in range(CJ):
                        last = nc.tensor.transpose(T[2][:, j * P:(j + 1) * P], u[:, j * P:(j + 1) * P], ident[:, :])
                    last.then_inc(uT_psum, 1)
                if t1.real():
                    need(pe, B.taken[3], t1.n)
                    if not (t1.fixed and t1.n == 0):
                        project(B, t1, 1, J[0])
                if t.real():
                    pe.wait_ge(la_ready, t.n + 1)
                    need(pe, g_state, t.n)
                    for n in range(4):
                        rows = slice(0, DEC) if n == 2 and t.fixed and t.n == LAST else slice(0, P)
                        last = nc.tensor.matmul(S[1][:, n * P:(n + 1) * P], tri[rows, n, :], zm[rows, :], start=True,
                                                stop=True)
                    last.then_inc(cum_psum, 1)
                if p.real():
                    pe.wait_ge(cn_ready, p.n + 1)
                    for j in range(CJ):
                        last = nc.tensor.transpose(T[1][:, (2 + j) * P:(3 + j) * P], cn[:, j * P:(j + 1) * P],
                                                   ident[:, :])
                    last.then_inc(cnT_psum, 1)
                if t1.real():
                    need(pe, B.out_added, 2 * p.n - 1)
                    project(B, t1, 2, J[1])
                if t.real():
                    pe.wait_ge(qk_scaled, 6 * t.n + 6)
                    pe.wait_ge(uT_taken, t.n + 1)
                    if t1.real():
                        pe.wait_ge(B.xT_lo, 2 * t1.n + 2)
                    nc.tensor.transpose(T[0][:, 0:P], qt[:, :], ident[:, :])
                    nc.tensor.transpose(T[0][:, P:2 * P], qf[:, :], ident[:, :])
                    nc.tensor.transpose(T[0][:, 2 * P:3 * P], kk[:, :], ident[:, :])
                    nc.tensor.transpose(T[0][:, 3 * P:3 * P + 64], kt0[:, :], ident[0:64, 0:64]).then_inc(g_psum, 1)
                    if p.real():
                        pe.wait_ge(cl_ready, 2 * p.n + 2)
                    nc.tensor.transpose(T[1][:, 0:P], ex[:, 1, :], ident[:, :]).then_inc(g_dec, 1)
                if t1.real():
                    need(pe, B.out_added, 2 * p.n)
                    project(B, t1, 0, J[2])
                if p.real():
                    if t.real():
                        pe.wait_ge(g_T, t.n + 1)
                    pe.wait_ge(cs_ready, p.n + 1)
                    for j in range(CJ):
                        last = nc.tensor.matmul(T[0][:, 0:CD], cth[:, j, :], wpw[:, j, :], start=(j == 0),
                                                stop=(j == CJ - 1))
                    last.then_inc(pw_psum, 1)
                if t.real():
                    qfT, kkT, ktT = gT[:, 0:P], gT[:, P:2 * P], gT[:, 2 * P:2 * P + 64]
                    pe.wait_ge(g_T, t.n + 1)
                    nc.tensor.matmul(S[0][0:64, 0:256].rearrange("p (h n) -> p h n", n=64), ktT, qbd[:, :, 0:64],
                                     start=True, stop=True)
                    nc.tensor.matmul(S[0][:, 256:512].rearrange("p (h n) -> p h n", n=64), kkT, qbd[:, :, 64:P],
                                     start=True, stop=True).then_inc(a_psum, 1)
                    rows = slice(0, DEC) if t.fixed and t.n == LAST else slice(0, P)
                    pe.wait_ge(cum_exp, 2 * t.n + 2)
                    pe.wait_ge(B.taken[1], t.n + 1)
                    nc.tensor.matmul(S[1][:, 0:256], kend[rows, :], r[rows, B_V:B_V + 256], start=True,
                                     stop=True).then_inc(su_psum, 1)
                if p.real():
                    if t.real():
                        pe.wait_ge(dec_ready, t.n + 1)
                    pe.wait_ge(go_g, p.n + 1)
                    pe.wait_ge(yc_ready, p.n + 1)
                    for j in range(4):
                        last = nc.tensor.transpose(T[1][:, j * P:(j + 1) * P], yb[:, j * P:(j + 1) * P], ident[:, :])
                    last.then_inc(yT_psum, 1)
                if t1.real():
                    pe.wait_ge(B.taken[1], t1.n + 1)
                    project(B, t1, 3, J[0])
                if t.real():
                    pe.wait_ge(a_masked, 2 * t.n + 2)
                    nc.tensor.matmul(T[2][:, 0:256], qfT, st[:, :], start=True, stop=False, skip_group_check=True)
                    for c in range(2):
                        for h in range(GH):
                            rows = slice(0, 64) if c == 0 else slice(0, P)
                            last = nc.tensor.matmul(T[2][64 * c:64 * c + 64, h * GV:(h + 1) * GV],
                                                    asb[rows, 256 * c + 64 * h:256 * c + 64 * h + 64],
                                                    r[rows, B_V + h * GV:B_V + (h + 1) * GV], start=False,
                                                    stop=(c == 1 and h == GH - 1), skip_group_check=True)
                    last.then_inc(go_psum, 1)
                def out(h):
                    if p.real():
                        if t1.real():
                            pe.wait_ge(B.taken[2 - 2 * h], t1.n + 1)
                        else:
                            need(pe, B.out_added, 2 * p.n - 1 + h)
                        output(B, p, h, J[1 + h])

                out(0)
                if t.fixed and t.n == LAST:
                    conv_T(t)
                if (t + 2).real() and not (t.fixed and t.n == -2):
                    if t.real():
                        need(pe, B.y_lo, t.n)
                        pe.wait_ge(dec_ready, t.n + 1)
                    transpose_x(B, t + 2, 0)
                    transpose_x(B, t + 2, 1)
                if t1.real():
                    if t1.fixed and t1.n == 0:
                        pe.wait_ge(zeros_b, 4)
                    pe.wait_ge(lr_taken, t1.n + 1)
                    nc.tensor.transpose(S[0][0:LR + 1, 0:P], glr1[:, :], ident[:, :]).then_inc(lr_psum, 1)
                out(1)

            over_tiles(pe, body_b)


def shape_constants():
    q = np.arange(P)[:, None]
    key = np.concatenate([np.arange(-P, P), np.arange(-P, 0)])[None, :]
    seen = np.where(q < CHUNK, (key >= -P) & (key < CHUNK), (key >= -CHUNK) & (key < P))
    slopes = 2.0 ** (-8.0 * np.arange(1, HEADS + 1) / HEADS)
    bias = np.where(seen[:, None, :], -slopes[None, :, None] * np.abs(q - key)[:, None, :], NEG).astype(np.float32)
    bias = (bias.view(np.uint32) >> 16).astype(np.uint16)
    ident = np.eye(P, dtype=np.float32)
    s, t = np.arange(P)[:, None], np.arange(P)[None, :]
    same = (s // CHUNK) == (t // CHUNK)
    tri = np.stack([(s <= t) & same, s <= t, s > t, (s > t) & same], 1).astype(np.float32) / 16.0
    tt = np.arange(64)[None, None, :]
    m0 = (s[:, :, None] < 64) & (s[:, :, None] <= tt)
    m1 = s[:, :, None] <= 64 + tt
    mask = np.concatenate([np.broadcast_to(m, (P, GH, 64)).reshape(P, 256) for m in (m0, m1)], 1).astype(np.float32)
    return bias, ident, tri, mask


def kernel(**inputs):
    import concourse.bacc as bacc
    from concourse.bass_utils import run_bass_kernel_spmd

    nc = bacc.Bacc("TRN2", target_bir_lowering=False, num_devices=1, dynamic_dma_scratch_size=1024)
    arrays, ins, consts = {}, [], []
    for name in INS:
        a = np.ascontiguousarray(inputs[name])
        arrays[f"in_{name}"] = a
        ins.append(nc.dram_tensor(f"in_{name}", a.shape, mybir.dt.from_np(a.dtype), kind="ExternalInput").ap())
    for n, a in enumerate(shape_constants()):
        a = np.ascontiguousarray(a)
        arrays[f"const_{n}"] = a
        consts.append(nc.dram_tensor(f"const_{n}", a.shape, mybir.dt.from_np(a.dtype), kind="ExternalInput").ap())
    outs = [nc.dram_tensor(f"out_{n}", shape, F32, kind="ExternalOutput").ap() for n, shape in enumerate(OUTS)]
    build(nc, ins, consts, outs)
    r = run_bass_kernel_spmd(nc, [arrays], core_ids=[0])
    return tuple(r.results[0][f"out_{n}"] for n in range(len(OUTS)))
```
